# Optimizing a Trainium2 kernel written in Bass

```python
import math
import jax, jax.numpy as jnp
from jax import lax
import numpy as np

D_MODEL = 1024
BATCH = 1
SEQ = 512
DEPTH = 1

N_META = 16
BLOCK = 128
PAD = BLOCK - N_META
HEAD_DIM = 64
N_HEADS_A = 8
N_KV_A = 2
GROUP_A = N_HEADS_A // N_KV_A
WINDOW = 128
N_HEADS_B = 8
T5_BUCKETS = 32
T5_MAX_DIST = 128
PEER_HEADS = 8
PEER_NKEYS = 128
PEER_EXPERTS = PEER_NKEYS * PEER_NKEYS
PEER_DQ = 256
PEER_TOPK = 16
PEER_CHUNK = 128
LN_EPS = 1e-5
NEG = -1e30
DEEPNORM_ALPHA = (2 * DEPTH) ** 0.25
DEEPNORM_BETA = (8 * DEPTH) ** -0.25
FORGET_BIAS = 3.0

W_QA = N_HEADS_A * HEAD_DIM
W_KA = N_KV_A * HEAD_DIM
W_B = N_HEADS_B * HEAD_DIM
IN_SIZES = (W_QA, W_KA, W_KA, W_B, W_B, W_B, N_HEADS_B, D_MODEL, D_MODEL)
IN_VALUE_COLS = (False, False, True, False, False, True, False, False, False)
IN_COLS = W_QA + 2 * W_KA + 3 * W_B + N_HEADS_B + 2 * D_MODEL

kernel_name = 'hybrid_swa_fox_peer_block'

def layer_norm(x, g, b):
    xf = x.astype(jnp.float32)
    mu = jnp.mean(xf, axis=-1, keepdims=True)
    xc = xf - mu
    var = jnp.mean(xc * xc, axis=-1, keepdims=True)
    y = xc * lax.rsqrt(var + LN_EPS) * g.astype(jnp.float32) + b.astype(jnp.float32)
    return y.astype(x.dtype)

def t5_bucket(n):
    max_exact = T5_BUCKETS // 2
    nf = jnp.maximum(n, 1).astype(jnp.float32)
    large = max_exact + (jnp.log(nf / max_exact) / math.log(T5_MAX_DIST / max_exact)
                         * (T5_BUCKETS - max_exact)).astype(jnp.int32)
    large = jnp.minimum(large, T5_BUCKETS - 1)
    return jnp.where(n < max_exact, n, large)

def sliding_window_attention(q, k, v, sinks, rel_table):
    B, P = q.shape[0], q.shape[1]
    nb = P // BLOCK
    qb = q.reshape(B, nb, BLOCK, N_KV_A, GROUP_A, HEAD_DIM)
    kb = k.reshape(B, nb, BLOCK, N_KV_A, HEAD_DIM)
    vb = v.reshape(B, nb, BLOCK, N_KV_A, HEAD_DIM)

    def with_prev(t):
        prev = jnp.pad(t, ((0, 0), (1, 0), (0, 0), (0, 0), (0, 0)))[:, :-1]
        return jnp.concatenate([prev, t], axis=2)

    kk, vv = with_prev(kb), with_prev(vb)
    s = jnp.einsum('bnqhgd,bnkhd->bnhgqk', qb, kk).astype(jnp.float32) * (HEAD_DIM ** -0.5)
    qi = jnp.arange(BLOCK)[:, None] + BLOCK
    kj = jnp.arange(2 * BLOCK)[None, :]
    dist = qi - kj
    bias = rel_table[t5_bucket(jnp.maximum(dist, 0))]
    bias = bias.reshape(BLOCK, 2 * BLOCK, N_KV_A, GROUP_A).transpose(2, 3, 0, 1).astype(jnp.float32)
    kabs = jnp.arange(nb)[:, None] * BLOCK - BLOCK + kj
    valid = (dist >= 0) & (dist < WINDOW) & (kabs[:, None, :] >= PAD)
    s = jnp.where(valid[None, :, None, None], s + bias, NEG)
    sink = jnp.broadcast_to(
        sinks.reshape(N_KV_A, GROUP_A)[None, None, :, :, None, None].astype(jnp.float32),
        s.shape[:-1] + (1,))
    p = jax.nn.softmax(jnp.concatenate([s, sink], axis=-1), axis=-1)[..., :-1]
    o = jnp.einsum('bnhgqk,bnkhd->bnqhgd', p.astype(v.dtype), vv)
    return o.reshape(B, P, N_HEADS_A * HEAD_DIM)

def forgetting_attention(q, k, v, log_f):
    B, P = q.shape[0], q.shape[1]
    nb = P // BLOCK
    c = jnp.cumsum(log_f, axis=1).transpose(0, 2, 1)
    outs = []
    for n in range(nb):
        q0, q1 = n * BLOCK, (n + 1) * BLOCK
        s = jnp.einsum('bqhd,bkhd->bhqk', q[:, q0:q1], k[:, :q1]).astype(jnp.float32) * (HEAD_DIM ** -0.5)
        s = s + (c[:, :, q0:q1, None] - c[:, :, None, :q1])
        qidx = jnp.arange(q0, q1)[:, None]
        kidx = jnp.arange(q1)[None, :]
        valid = (kidx <= qidx) & (kidx >= PAD)
        p = jax.nn.softmax(jnp.where(valid, s, NEG), axis=-1)
        outs.append(jnp.einsum('bhqk,bkhd->bqhd', p.astype(v.dtype), v[:, :q1]))
    return jnp.concatenate(outs, axis=1).reshape(B, P, N_HEADS_B * HEAD_DIM)

def mixer_sublayer(h, w_in, b_in, sinks, rel_table, w_pa, w_pb, w_o):
    B, L, _ = h.shape
    z = h @ w_in + b_in
    offs = np.cumsum(IN_SIZES)[:-1].tolist()
    qa, ka, va, qb, kb, vb, fb, ga, gb = jnp.split(z, offs, axis=-1)

    def heads(t, n_heads):
        t = jnp.pad(t, ((0, 0), (PAD, 0), (0, 0)))
        return t.reshape(B, PAD + L, n_heads, HEAD_DIM)

    log_f = jnp.pad(jax.nn.log_sigmoid(fb.astype(jnp.float32)), ((0, 0), (PAD, 0), (0, 0)))
    oa = sliding_window_attention(heads(qa, N_HEADS_A), heads(ka, N_KV_A), heads(va, N_KV_A),
                                  sinks, rel_table)[:, PAD:]
    ob = forgetting_attention(heads(qb, N_HEADS_B), heads(kb, N_HEADS_B), heads(vb, N_HEADS_B),
                              log_f)[:, PAD:]
    merged = jax.nn.sigmoid(ga) * (oa @ w_pa) + jax.nn.sigmoid(gb) * (ob @ w_pb)
    return merged @ w_o

def peer_ffn(h, w_q, sub_keys, u, v):
    B, L, D = h.shape
    T = B * L
    n_chunks = -(-T // PEER_CHUNK)
    xt = jnp.pad(h.reshape(T, D), ((0, n_chunks * PEER_CHUNK - T), (0, 0))).reshape(n_chunks, PEER_CHUNK, D)
    K = PEER_TOPK

    def chunk(xc):
        q = (xc @ w_q).reshape(PEER_CHUNK, PEER_HEADS, 2, PEER_DQ // 2)
        sc = jnp.einsum('chpd,hpkd->chpk', q, sub_keys).astype(jnp.float32)
        top_s, top_i = lax.top_k(sc, K)
        cand = top_s[:, :, 0, :, None] + top_s[:, :, 1, None, :]
        best_s, best_flat = lax.top_k(cand.reshape(PEER_CHUNK, PEER_HEADS, K * K), K)
        ia = jnp.take_along_axis(top_i[:, :, 0], best_flat // K, axis=-1)
        ib = jnp.take_along_axis(top_i[:, :, 1], best_flat % K, axis=-1)
        expert = ia * PEER_NKEYS + ib
        g = jax.nn.softmax(best_s, axis=-1).astype(xc.dtype)
        u_sel = u[expert]
        v_sel = v[expert]
        a = jax.nn.gelu(jnp.einsum('cd,chkd->chk', xc, u_sel), approximate=False) * g
        return jnp.einsum('chk,chkd->cd', a, v_sel)

    out = lax.map(chunk, xt)
    return out.reshape(n_chunks * PEER_CHUNK, D)[:T].reshape(B, L, D)

def setup_inputs(seed: int = 0) -> dict:
    key = jax.random.key(seed)
    ks = jax.random.split(key, 24)
    f32 = jnp.float32
    D = D_MODEL
    beta = DEEPNORM_BETA
    nrm = lambda k, shape, s: jax.random.normal(k, shape, f32) * s
    x = nrm(ks[0], (BATCH, SEQ, D), 1.0)
    meta_tokens = nrm(ks[1], (N_META, D), 1.0)
    emb_ln_g = 1.0 + nrm(ks[2], (D,), 0.02)
    emb_ln_b = nrm(ks[3], (D,), 0.02)
    rel_bias = nrm(ks[4], (T5_BUCKETS, N_HEADS_A), 0.5)
    in_keys = jax.random.split(ks[5], len(IN_SIZES))
    w_in = jnp.concatenate(
        [nrm(kk, (DEPTH, D, n), D ** -0.5 * (beta if isv else 1.0))
         for kk, n, isv in zip(in_keys, IN_SIZES, IN_VALUE_COLS)], axis=-1)
    b_in = nrm(ks[6], (DEPTH, IN_COLS), 0.02)
    f0 = W_QA + 2 * W_KA + 3 * W_B
    b_in = b_in.at[:, f0:f0 + N_HEADS_B].add(FORGET_BIAS)
    attn_sinks = nrm(ks[7], (DEPTH, N_HEADS_A), 0.5)
    w_pa = nrm(ks[8], (DEPTH, W_QA, D), W_QA ** -0.5 * beta)
    w_pb = nrm(ks[9], (DEPTH, W_B, D), W_B ** -0.5 * beta)
    w_o = nrm(ks[10], (DEPTH, D, D), D ** -0.5 * beta)
    ln1_g = 1.0 + nrm(ks[11], (DEPTH, D), 0.02)
    ln1_b = nrm(ks[12], (DEPTH, D), 0.02)
    peer_wq = nrm(ks[13], (DEPTH, D, PEER_HEADS * PEER_DQ), D ** -0.5)
    peer_subkeys = nrm(ks[14], (DEPTH, PEER_HEADS, 2, PEER_NKEYS, PEER_DQ // 2), (PEER_DQ // 2) ** -0.5)
    peer_u = nrm(ks[15], (DEPTH, PEER_EXPERTS, D), D ** -0.5 * beta)
    peer_v = nrm(ks[16], (DEPTH, PEER_EXPERTS, D), beta)
    ln2_g = 1.0 + nrm(ks[17], (DEPTH, D), 0.02)
    ln2_b = nrm(ks[18], (DEPTH, D), 0.02)
    return {'x': x, 'meta_tokens': meta_tokens, 'emb_ln_g': emb_ln_g, 'emb_ln_b': emb_ln_b,
            'rel_bias': rel_bias, 'w_in': w_in, 'b_in': b_in, 'attn_sinks': attn_sinks,
            'w_pa': w_pa, 'w_pb': w_pb, 'w_o': w_o, 'ln1_g': ln1_g, 'ln1_b': ln1_b,
            'peer_wq': peer_wq, 'peer_subkeys': peer_subkeys, 'peer_u': peer_u, 'peer_v': peer_v,
            'ln2_g': ln2_g, 'ln2_b': ln2_b}

def reference(x, meta_tokens, emb_ln_g, emb_ln_b, rel_bias, w_in, b_in, attn_sinks, w_pa, w_pb, w_o,
              ln1_g, ln1_b, peer_wq, peer_subkeys, peer_u, peer_v, ln2_g, ln2_b):
    B = x.shape[0]
    meta = jnp.broadcast_to(meta_tokens[None].astype(x.dtype), (B, N_META, D_MODEL))
    h = layer_norm(jnp.concatenate([meta, x], axis=1), emb_ln_g, emb_ln_b)
    for l in range(DEPTH):
        y = mixer_sublayer(h, w_in[l], b_in[l], attn_sinks[l], rel_bias, w_pa[l], w_pb[l], w_o[l])
        h = layer_norm(DEEPNORM_ALPHA * h + y, ln1_g[l], ln1_b[l])
        y = peer_ffn(h, peer_wq[l], peer_subkeys[l], peer_u[l], peer_v[l])
        h = layer_norm(DEEPNORM_ALPHA * h + y, ln2_g[l], ln2_b[l])
    return h[:, N_META:]


_drawn_inputs = setup_inputs


def setup_inputs(seed=0):
    import zlib

    import numpy as np

    out = dict(_drawn_inputs(seed))
    spreads = {}
    factors = {'meta_tokens': 21.143,
     'rel_bias': 3.852,
     'attn_sinks': 64.0,
     'ln2_g': 8.243,
     'ln2_b': 8.334}
    for name, (base, spread) in spreads.items():
        noise = np.random.default_rng([zlib.crc32(name.encode()), seed]).standard_normal(out[name].shape)
        drawn = base * np.exp(spread * noise) if base else spread * noise
        out[name] = __import__('jax').numpy.asarray(drawn.astype(out[name].dtype))
    for name, factor in factors.items():
        out[name] = (out[name] * factor).astype(out[name].dtype)
    return out
```

```python
from contextlib import ExitStack

import numpy as np

import concourse.bass as bass
from concourse import mybir

P = 128
D = 1024
SEQ = 512
META = 16
COLS = SEQ + META
KT = D // P
NBLK = SEQ // P
HEADS = 8
HD = 64
NKEYS = 128
TOPK = 16
BUCKETS = 32
EPS = 1e-5
ALPHA = 2.0 ** 0.25
NEG = -1e30
LOWEST = -3.0e38
GATE_SCALE = 2.0 ** 15

RING = 4
N_PROJ = 19
N_MERGE = 24
N_OUT = 8
N_PQ = 16
FIRST_MERGE = N_PROJ
FIRST_OUT = FIRST_MERGE + N_MERGE
FIRST_PQ = FIRST_OUT + N_OUT
FIRST_U = FIRST_PQ + N_PQ
FIRST_V = FIRST_U + NKEYS
UNITS = 2 * NBLK * HEADS
GROUP = 4
NGROUP = NKEYS // GROUP
CHUNK = 16
TOP_STEPS = 26

F32 = mybir.dt.float32
F32R = mybir.dt.float32r
F16 = mybir.dt.float16
U32 = mybir.dt.uint32
ALU = mybir.AluOpType
ACT = mybir.ActivationFunctionType
AX = mybir.AxisListType

C_ID, C_MASK, C_MEAN, C_IOTA, C_IOTA16, C_EPS, C_ONE = 0, 128, 256, 384, 512, 528, 529
C_COLS = 530


class Chain:

    def __init__(self, eng, sem):
        self.eng, self.sem, self.n, self.past = eng, sem, 0, 0

    def mark(self, ins):
        ins.then_inc(self.sem, 1)
        self.n += 1

    def settle(self):
        self.eng.wait_ge(self.sem, self.n + self.past)

    def settle_apart(self, memset, spare):
        self.settle()
        memset(spare, 0.0)

    def link(self, ins):
        self.mark(ins)
        self.settle()

    def loop(self, i, each):
        self.start, self.each, self.past = self.n, each, i * each

    def end(self, times):
        assert self.n - self.start == self.each, (self.n - self.start, self.each)
        self.n = self.start + self.each * times
        self.past = 0


def unit_of(u):
    window = u < UNITS // 2
    n, h = (u % (UNITS // 2)) // HEADS, u % HEADS
    tile, half = (h % 4, h // 4) if window else (h // 2, h % 2)
    return window, n, h, tile, half


def pieces_of(u):
    window, n, _, _, _ = unit_of(u)
    if window:
        return [(0, META, None), (META, P, 0)] if n == 0 else [(0, P, n - 1), (P, P, n)]
    return [(P * b, P, b) for b in range(n + 1)] + [(P * (n + 1), META, None)]


def width_of(u):
    c, k, _ = pieces_of(u)[-1]
    return c + k


def build(nc, x, meta, consts, buckets, outside, norm_cols, b_cols, rel_bias, sinks, w_proj, w_merge, w_out,
          w_pq, subkeys, u_exp, v_exp, out):
    ctx = ExitStack()
    with ctx:
        def sem(name):
            return ctx.enter_context(nc.semaphore(name))

        def place(stack, **specs):
            return [stack.enter_context(nc.sbuf_tensor(n, s, t)) for n, (s, t) in specs.items()]

        cst, ncol, bcol = place(ctx, cst=([P, C_COLS], F32), ncol=([P, 6 * KT], F32), bcol=([P, N_PROJ + 16], F32))
        raw, hi, lo = place(ctx, raw=([P, RING, D], F32), hi=([P, RING, D], F32R), lo=([P, RING, D], F32R))
        hT_hi, hT_lo = place(ctx, hT_hi=([P, KT, COLS], F32R), hT_lo=([P, KT, COLS], F32R))
        ident = cst[:, C_ID:C_ID + P]
        mask = cst[:, C_MASK:C_MASK + P]
        mean_of = cst[:, C_MEAN:C_MEAN + P]
        iota16 = cst[:, C_IOTA16:C_IOTA16 + TOPK]
        eps = cst[:, C_EPS:C_EPS + 1]
        one = cst[:, C_ONE:C_ONE + 1]
        spare, = place(ctx, spare=([P, 1], F32))
        with ExitStack() as s:
            biasA, qaT = place(s, biasA=([P, HEADS, 2 * P], F32), qaT=([P, 4, SEQ], F32))
        acc, = place(ctx, acc=([P, KT, SEQ], F32))
        with ExitStack() as s:
            xin, xT = place(s, xin=([P, 5, D], F32), xT=([P, 2, COLS], F32))
            stats, mv, rs = place(s, stats=([P, 5, 12], F32), mv=([P, 5, 2], F32), rs=([P, 4, 5], F32))
        with ExitStack() as s:
            vT, logf = place(s, vT=([P, 5, COLS], F32), logf=([HEADS, 6, COLS], F32))
        with ExitStack() as s:
            oT_hi, oT_lo = place(s, oT_hi=([P, 2, 4, SEQ], F32R), oT_lo=([P, 2, 4, SEQ], F32R))
            with ExitStack() as t:
                kaT, qbT, kbT = place(t, kaT=([P, COLS], F32), qbT=([P, 4, SEQ], F32), kbT=([P, 4, COLS], F32))
                vN, vM = place(t, vN=([P, NBLK, 640], F32), vM=([META, 640], F32))
                ckB, cq = place(t, ckB=([P, HEADS, COLS], F32), cq=([P, NBLK, HEADS], F32))
                pexp, pT, pM = place(t, pexp=([P, 2, COLS], F32), pT=([P, 2, SEQ], F32), pM=([META, 2, P], F32))
                nmax, rsum, sexp, snk = place(t, nmax=([P, UNITS], F32), rsum=([P, 2, UNITS], F32),
                                              sexp=([P, UNITS], F32), snk=([P, 2, HEADS], F32))
                relb, buck, wrow = place(t, relb=([BUCKETS, HEADS], F32), buck=([BUCKETS, 3 * P], F32),
                                         wrow=([HEADS, 2, 3 * P], F32))
            gate, mix = place(s, gate=([P, 2, 2, SEQ], F32), mix=([P, 2, 2, SEQ], F32))
            m_hi, m_lo = place(s, m_hi=([P, KT, SEQ], F32R), m_lo=([P, KT, SEQ], F32R))
        with ExitStack() as s:
            sq, rinv, nw = place(s, sq=([P, 2, SEQ], F32), rinv=([P, SEQ], F32), nw=([P, 2, SEQ], F32))
        ia, ib, best = place(ctx, ia=([P, SEQ], F32), ib=([P, SEQ], F32), best=([P, SEQ], F32))
        with ExitStack() as s:
            sc, gelu = place(s, sc=([P, 2 * HEADS * SEQ], F32), gelu=([P, RING, SEQ], F32))
            sk_raw, sk_hi, sk_lo = place(s, sk_raw=([P, 2 * HEADS, NKEYS], F32),
                                         sk_hi=([P, 2 * HEADS, NKEYS], F32R), sk_lo=([P, 2 * HEADS, NKEYS], F32R))
            pq, pq_hi, pq_lo = place(s, pq=([P, 2, SEQ], F32), pq_hi=([P, 2, SEQ], F32R), pq_lo=([P, 2, SEQ], F32R))
            now, rest, cand, topv, topi, topf = place(
                s, now=([P, 2, NKEYS], F32), rest=([P, 2 * NKEYS], F32), cand=([P, TOPK * TOPK], F32),
                topv=([P, 2, TOPK], F32), topi=([P, 2, TOPK], U32), topf=([P, 2, TOPK], F32))
            flat, pos, posf, eq = place(s, flat=([P, TOPK], U32), pos=([P, 2, TOPK], U32),
                                        posf=([P, 2, TOPK], F32), eq=([P, 2, TOPK * TOPK], F32))
        with ExitStack() as s:
            gsum, iaT, ibT, gT_hi, gT_lo, iota_h = place(
                s, gsum=([P, 3, NBLK * HEADS], F32), iaT=([P, SEQ], F16), ibT=([P, SEQ], F16), gT_hi=([P, SEQ], F16),
                gT_lo=([P, SEQ], F16), iota_h=([P, P], F16))
            hotA, hotB, hotG_hi, hotG_lo = place(
                s, hotA=([P, 2, NKEYS, CHUNK], F16), hotB=([P, NKEYS, CHUNK], F16),
                hotG_hi=([P, 2, NKEYS, CHUNK], F16), hotG_lo=([P, 2, NKEYS, CHUNK], F16))
            gates, = place(s, gates=([P, NKEYS, P], F32))
        with ExitStack() as s:
            hi_x, lo_x = place(s, hi_x=([P, RING, D], F32R), lo_x=([P, RING, D], F32R))
            gel_in, gate_in, act_t = place(s, gel_in=([P, RING, SEQ], F32), gate_in=([P, RING, SEQ], F32),
                                           act_t=([P, RING, SEQ], F32))
        with ExitStack() as s:
            tok, = place(s, tok=([P, 2, D], F32))

        psS = ctx.enter_context(nc.psum_tensor("psS", [P, 2, 2 * SEQ], F32))
        psT = ctx.enter_context(nc.psum_tensor("psT", [P, 2 * SEQ], F32))
        psO = ctx.enter_context(nc.psum_tensor("psO", [P, 2, SEQ], F32))
        banks = [psS[:, 0, 0:SEQ], psS[:, 0, SEQ:], psS[:, 1, 0:SEQ], psS[:, 1, SEQ:],
                 psT[:, 0:SEQ], psT[:, SEQ:], psO[:, 0, :], psO[:, 1, :]]

        w_dram = nc.dram_tensor("w_dram", [P, HEADS, 3 * P], F32).ap()
        c_dram = nc.dram_tensor("c_dram", [HEADS, COLS], F32).ap()
        gelu_dram = nc.dram_tensor("gelu_dram", [NKEYS, P, SEQ], F32).ap()
        gates_dram = nc.dram_tensor("gates_dram", [NKEYS, P, SEQ], F32).ap()

        cst_in, bias_in, x_in, keys_in = sem("cst_in"), sem("bias_in"), [sem(f"x_in{t}") for t in range(5)], sem("keys_in")
        landed = [sem(f"landed{r}") for r in range(RING)]
        hi_done, lo_done, slab_used = sem("hi_done"), sem("lo_done"), sem("slab_used")
        std_done, norm_done, turned, xT_done, hT_hi_done, hT_lo_done = (
            sem("std_done"), sem("norm_done"), sem("turned"), sem("xT_done"), sem("hT_hi_done"), sem("hT_lo_done"))
        evacuated = sem("evacuated")
        z_done, soft_done, c_done, c_out, ck_in, c_turned = (
            sem("z_done"), sem("soft_done"), sem("c_done"), sem("c_out"), sem("ck_in"), sem("c_turned"))
        w_mm, w_done, w_out_s, biasA_in = sem("w_mm"), sem("w_done"), sem("w_stored"), sem("biasA_in")
        v_turned, v_ready = sem("v_turned"), sem("v_ready")
        s_mm, nmax_done, exp_done, p_done, p_turned, pT_done, pM_done = (
            sem("s_mm"), sem("nmax_done"), sem("exp_done"), sem("p_done"), sem("p_turned"), sem("pT_done"), sem("pM_done"))
        pv_mm, o_hi_done, o_lo_done = sem("pv_mm"), sem("o_hi_done"), sem("o_lo_done")
        gate_done, mix_done, m_hi_done, m_lo_done = sem("gate_done"), sem("mix_done"), sem("m_hi_done"), sem("m_lo_done")
        r_done, mean_mm, xc_done, sq_done, var_mm, sd_done, h_done, scaled = (
            sem("r_done"), sem("mean_mm"), sem("xc_done"), sem("sq_done"), sem("var_mm"), sem("sd_done"), sem("h_done"), sem("scaled"))
        sk_hi_done, sk_done, pq_done, pq_hi_done, pq_lo_done, sc_mm, sc_done = (
            sem("sk_hi_done"), sem("sk_done"), sem("pq_done"), sem("pq_hi_done"), sem("pq_lo_done"), sem("sc_mm"), sem("sc_done"))
        gelu_done, now_done, top_done = sem("gelu_done"), sem("now_done"), sem("top_done")
        gelu_out = [sem(f"gelu_out{r}") for r in range(RING)]
        less_done, g_exp_done, g_done, idx_turned, gT_hi_done, idx_done = (
            sem("less_done"), sem("g_exp_done"), sem("g_done"), sem("idx_turned"), sem("gT_hi_done"), sem("idx_done"))
        iota_done = sem("iota_done")
        hot_done, G_mm, G_act, G_dve, gates_out = sem("hot_done"), sem("G_mm"), sem("G_act"), sem("G_dve"), sem("gates_out")
        gel_in_s, gate_in_s = [sem(f"gel_in{r}") for r in range(RING)], [sem(f"gate_in{r}") for r in range(RING)]
        vhi_done, vlo_done, act_done, ahi_done, alo_done = (
            sem("vhi_done"), sem("vlo_done"), sem("act_done"), sem("ahi_done"), sem("alo_done"))
        v_mm, y_added = sem("v_mm"), sem("y_added")
        out_turned, tok_done, out_sent = sem("out_turned"), sem("tok_done"), [sem(f"out_sent{r}") for r in range(2)]
        act_step, dve_step = sem("act_step"), sem("dve_step")

        block = ctx.enter_context(nc.Block())

        def slab_source(n):
            if n < FIRST_MERGE:
                return w_proj[n]
            if n < FIRST_OUT:
                return w_merge[n - FIRST_MERGE]
            if n < FIRST_PQ:
                return w_out[n - FIRST_OUT]
            if n < FIRST_U:
                return w_pq[n - FIRST_PQ]
            return u_exp[n - FIRST_U]

        def landed_wait(eng, n, i=0, per=0):
            eng.wait_ge(landed[n % RING], 16 * (n // RING + 1) + i * (16 * per // RING))

        def load(sp, n, source, i=0, per=0):
            if n >= RING:
                sp.wait_ge(lo_done, n - RING + 1 + i * per)
            sp.dma_start(raw[:, n % RING, :], source).then_inc(landed[n % RING], 16)

        def split_hi(act, n, i=0, per=0):
            landed_wait(act, n, i, per)
            if n >= RING:
                act.wait_ge(slab_used, n - RING + 1 + i * per)
            nc.scalar.activation(hi[:, n % RING, :], raw[:, n % RING, :], ACT.Copy).then_inc(hi_done, 1)

        def split_lo(dve, n, i=0, per=0):
            dve.wait_ge(hi_done, n + 1 + i * per)
            nc.vector.tensor_tensor(lo[:, n % RING, :], raw[:, n % RING, :], hi[:, n % RING, :].bitcast(F32),
                                    ALU.subtract).then_inc(lo_done, 1)

        def split_product(out_ap, w_h, w_l, x_h, x_l, start, stop):
            nc.tensor.matmul(out_ap, w_h, x_l, start=start, stop=False)
            nc.tensor.matmul(out_ap, w_l, x_h, start=False, stop=False)
            return nc.tensor.matmul(out_ap, w_h, x_h, start=False, stop=stop)

        def slab_parts(slot, k):
            return hi[:, slot, k * P:(k + 1) * P], lo[:, slot, k * P:(k + 1) * P]

        AHEAD = 2

        def wait_at(eng, semaphore, first, per, i):
            if not isinstance(i, int) or first + per * i > 0:
                eng.wait_ge(semaphore, first + per * i)

        def exp_count(u):
            half = UNITS // 2
            return 2 * (u + 1) if u < half else 2 * half + (u + 1 - half)

        def meta_count(u):
            return sum(any(b is None for _, _, b in pieces_of(v)) for v in range(u + 1))

        @block.sync
        def _(sp):
            for t in range(NBLK):
                sp.dma_start(xin[:, t, :], x[t * P:(t + 1) * P, :]).then_inc(x_in[t], 16)
            sp.dma_start(xin[0:META, NBLK, :], meta).then_inc(x_in[NBLK], 16)
            sp.dma_start(cst[:, :], consts).then_inc(cst_in, 16)
            sp.dma_start(ncol[:, :], norm_cols).then_inc(cst_in, 16)
            sp.dma_start(bcol[:, :], b_cols).then_inc(cst_in, 16)
            for n in range(RING):
                load(sp, n, slab_source(n))
            sp.dma_start(relb[:, :], rel_bias).then_inc(bias_in, 16)
            sp.dma_start(buck[:, :], buckets).then_inc(bias_in, 16)
            sp.dma_start(wrow[:, 1, :], outside).then_inc(bias_in, 16)
            sp.dma_start(snk[:, 0, :], sinks.partition_broadcast(P)).then_inc(bias_in, 16)
            for n in range(RING, FIRST_U + RING):
                load(sp, n, slab_source(n))
            with sp.Fori(1, NGROUP) as i:
                for j in range(GROUP):
                    n = FIRST_U + j
                    load(sp, n, u_exp[i * GROUP + j], i, GROUP)
                    sp.wait_ge(gelu_done, i * GROUP + (j - GROUP + 1))
                    sp.dma_start(gelu_dram[i * GROUP + (j - GROUP)], gelu[:, j, :]).then_inc(gelu_out[j], 16)
            for j in range(GROUP):
                n = FIRST_V + j
                load(sp, n, v_exp[j])
                sp.wait_ge(gelu_done, NKEYS - GROUP + j + 1)
                sp.dma_start(gelu_dram[NKEYS - GROUP + j], gelu[:, j, :]).then_inc(gelu_out[j], 16)
            for t in range(NBLK):
                sp.wait_ge(G_act, (t + 1) * (P // CHUNK))
                sp.dma_start(gates_dram[:, :, t * P:(t + 1) * P].rearrange("b a c -> a b c"),
                             gates[:, :, :]).then_inc(gates_out, 16)
            for j in range(RING):
                sp.wait_ge(gelu_out[j], 16 * NGROUP)
            sp.wait_ge(gates_out, 16 * NBLK)

            def load_tiles(b, j, i):
                wait_at(sp, act_done, j - RING + 1, RING, i)
                sp.dma_start(gel_in[:, j, :], gelu_dram[b]).then_inc(gel_in_s[j], 16)
                sp.dma_start(gate_in[:, j, :], gates_dram[b]).then_inc(gate_in_s[j], 16)

            for j in range(RING):
                load_tiles(j, j, 0)
            with sp.Fori(1, NGROUP) as i:
                for j in range(GROUP):
                    sp.wait_ge(vlo_done, i * GROUP + (j - RING + 1))
                    sp.dma_start(raw[:, (FIRST_V + j) % RING, :],
                                 v_exp[i * GROUP + j]).then_inc(landed[(FIRST_V + j) % RING], 16)
                    load_tiles(i * GROUP + j, j, i)
            for t in range(NBLK):
                sp.wait_ge(tok_done, t + 1)
                sp.dma_start(out[t * P:(t + 1) * P, :], tok[:, t % 2, :]).then_inc(out_sent[t % 2], 16)
            for r in range(2):
                sp.wait_ge(out_sent[r], 16 * NBLK // 2)

        @block.gpsimd
        def _(pool):
            pool.wait_ge(w_done, 1)
            pool.dma_start(w_dram.rearrange("q h m -> h q m"),
                           wrow[:, 0, :].unsqueeze(1).to_broadcast([HEADS, P, 3 * P])).then_inc(w_out_s, 16)
            pool.wait_ge(w_out_s, 16)
            skewed = bass.AP(w_dram.tensor, P - 1, [[3 * P * HEADS - 1, P], [3 * P, HEADS], [1, 2 * P]])
            pool.dma_start(biasA[:, :, :], skewed).then_inc(biasA_in, 16)
            pool.wait_ge(c_done, 1)
            pool.dma_start(c_dram, logf[:, 5, :]).then_inc(c_out, 16)
            pool.wait_ge(c_out, 16)
            pool.wait_ge(xT_done, KT)
            pool.dma_start(ckB[:, :, :].rearrange("p h c -> p (h c)"),
                           c_dram.rearrange("h c -> (h c)").partition_broadcast(P)).then_inc(ck_in, 16)
            pool.wait_ge(r_done, N_OUT)
            pool.dma_start(sk_raw[:, :, :], subkeys).then_inc(keys_in, 16)

        @block.scalar
        def _(act):
            own = Chain(act, act_step)
            act.wait_ge(norm_done, 1)
            nc.scalar.activation(rs[:, 0, :], mv[:, :, 1], ACT.Sqrt, bias=eps).then_inc(std_done, 1)
            for n in range(AHEAD):
                split_hi(act, n)
            for k in range(KT):
                act.wait_ge(xT_done, k + 1)
                nc.scalar.activation(hT_hi[:, k, :], xT[:, k % 2, :], ACT.Copy).then_inc(hT_hi_done, 1)
            for n in range(N_PROJ):
                split_hi(act, n + AHEAD)
                if n == 1:
                    act.wait_ge(z_done, 1)
                    own.link(nc.scalar.activation(logf[:, 1, :], logf[:, 0, :], ACT.Abs))
                    own.link(nc.scalar.activation(logf[:, 2, :], logf[:, 1, :], ACT.Exp, scale=-1.0))
                    nc.scalar.activation(logf[:, 3, :], logf[:, 2, :], ACT.Ln, bias=one[0:HEADS, :]).then_inc(soft_done, 1)
            for b in range(NBLK + 1):
                act.wait_ge(v_turned, b + 1)
                if b < NBLK:
                    nc.scalar.activation(vN[:, b, :], psS[:, b % 2, 0:640], ACT.Copy).then_inc(v_ready, 1)
                else:
                    nc.scalar.activation(vM[:, :], psT[0:META, 0:640], ACT.Copy).then_inc(v_ready, 1)

            for s in range(UNITS + 4):
                if s < UNITS:
                    window, n, h, tile, half = unit_of(s)
                    act.wait_ge(nmax_done, s + 1)
                    if s >= 2:
                        act.wait_ge(p_turned, s - 1)
                    if window:
                        nc.scalar.activation(sexp[:, s:s + 1], snk[:, 0, h:h + 1], ACT.Exp,
                                             bias=nmax[:, s:s + 1]).then_inc(exp_done, 1)
                    nc.scalar.activation(pexp[:, s % 2, 0:width_of(s)], psS[:, s % 2, 0:width_of(s)], ACT.Exp,
                                         bias=nmax[:, s:s + 1], accum_out=rsum[:, 0, s:s + 1]).then_inc(exp_done, 1)
                if 1 <= s <= UNITS:
                    u = s - 1
                    act.wait_ge(p_turned, u + 1)
                    if u >= 2:
                        act.wait_ge(pv_mm, u - 1)
                    cols = P * sum(b is not None for _, _, b in pieces_of(u))
                    nc.scalar.activation(pT[:, u % 2, 0:cols], psT[:, 0:cols], ACT.Copy).then_inc(pT_done, 1)
                if s >= 3 and (s - 3) % HEADS == HEADS - 1:
                    w = (s - 3) // HEADS
                    act.wait_ge(pv_mm, HEADS * (w + 1))
                    nc.scalar.activation(oT_hi[:, w // NBLK, :, (w % NBLK) * P:(w % NBLK + 1) * P],
                                         psO[:, w % 2, :].rearrange("p (t q) -> p t q", t=4),
                                         ACT.Copy).then_inc(o_hi_done, 1)

            for m in range(KT):
                for j in range(3):
                    n = FIRST_MERGE + 3 * m + j
                    split_hi(act, n + AHEAD)
                    if j < 2:
                        act.wait_ge(slab_used, n + 1)
                        if m >= 2:
                            act.wait_ge(mix_done, m - 1)
                        nc.scalar.activation(gate[:, m % 2, j, :], psS[:, m % 2, j * SEQ:(j + 1) * SEQ], ACT.Sigmoid,
                                             bias=bcol[:, N_PROJ + 8 * j + m:N_PROJ + 8 * j + m + 1]).then_inc(gate_done, 1)
                act.wait_ge(mix_done, m + 1)
                nc.scalar.activation(m_hi[:, m, :], mix[:, m % 2, 0, :], ACT.Copy).then_inc(m_hi_done, 1)
            for m in range(N_OUT):
                split_hi(act, FIRST_OUT + m + AHEAD)

            def norm_scalar(r):
                for k in range(KT):
                    act.wait_ge(xc_done, KT * r + k + 1)
                    if KT * r + k >= 2:
                        act.wait_ge(var_mm, KT * r + k - 1)
                    nc.scalar.activation(sq[:, k % 2, :], acc[:, k, :], ACT.Square).then_inc(sq_done, 1)
                act.wait_ge(var_mm, KT * (r + 1))
                nc.scalar.activation(nw[:, 0, :], banks[5], ACT.Sqrt, bias=eps).then_inc(sd_done, 1)

            norm_scalar(0)
            for k in range(KT):
                act.wait_ge(h_done, k + 1)
                nc.scalar.activation(hT_hi[:, k, 0:SEQ], acc[:, k, :], ACT.Copy).then_inc(hT_hi_done, 1)
            act.wait_ge(keys_in, 16)
            nc.scalar.activation(sk_hi[:, :, :], sk_raw[:, :, :], ACT.Copy).then_inc(sk_hi_done, 1)
            sc_view = sc[:, :].rearrange("p (t x) -> p t x", t=NBLK)
            for q in range(N_PQ + 1):
                if q < N_PQ:
                    n = FIRST_PQ + q
                    split_hi(act, n + AHEAD)
                    act.wait_ge(slab_used, n + 1)
                    if q >= 2:
                        act.wait_ge(sc_mm, q - 1)
                    nc.scalar.activation(pq_hi[:, q % 2, :], psS[:, q % 2, 0:SEQ], ACT.Copy).then_inc(pq_hi_done, 1)
                if q >= 1:
                    act.wait_ge(sc_mm, q)
                    nc.scalar.activation(sc_view[:, :, (q - 1) * P:q * P],
                                         banks[4 + (q - 1) % 4].rearrange("p (t k) -> p t k", t=NBLK),
                                         ACT.Copy).then_inc(sc_done, 1)

            def expert_inputs(i, last=False):
                for j in range(GROUP):
                    n = FIRST_U + j
                    if not (last and j >= GROUP - AHEAD):
                        split_hi(act, n + AHEAD, i, GROUP)
                    if j == 0:
                        wait_at(act, top_done, 0, 1, i)
                        nc.scalar.activation(now[:, :, :].rearrange("p s k -> p (s k)"),
                                             sc[:, bass.ds(i * 2 * NKEYS, 2 * NKEYS)], ACT.Copy).then_inc(now_done, 1)
                    act.wait_ge(slab_used, n + 1 + i * GROUP)
                    wait_at(act, gelu_out[j], 0, 16, i)
                    nc.scalar.activation(gelu[:, j, :], banks[j], ACT.Gelu).then_inc(gelu_done, 1)

            expert_inputs(0)
            with act.Fori(1, NGROUP - 1) as i:
                expert_inputs(i)
            expert_inputs(NGROUP - 1, last=True)

            act.wait_ge(less_done, 1)
            nc.scalar.activation(best[:, :], best[:, :], ACT.Exp).then_inc(g_exp_done, 1)
            act.wait_ge(idx_turned, 1)
            nc.scalar.activation(gT_hi[:, :], banks[2], ACT.Copy, scale=GATE_SCALE).then_inc(gT_hi_done, 1)
            per = P // CHUNK
            for j in range(RING):
                act.wait_ge(gelu_out[j], 16 * NGROUP)
            for t in range(NBLK):
                if t >= 1:
                    act.wait_ge(gates_out, 16 * t)
                with act.Fori(0, per // 2) as i:
                    for r in range(2):
                        act.wait_ge(G_mm, i * 2 + (per * t + r + 1))
                        for half in range(2):
                            src = psS[:, half, :] if r == 0 else (psT[:, :] if half == 0 else psO[:, :, :].rearrange("p o q -> p (o q)"))
                            ins = nc.scalar.activation(
                                gates[:, :, bass.ds(i * 2 * CHUNK + (r * CHUNK + half * 8), 8)],
                                src.rearrange("p (c b) -> p b c", c=8), ACT.Copy, scale=1.0 / GATE_SCALE)
                        ins.then_inc(G_act, 1)

            def weigh(j, g, par):
                slot = par * GROUP + j
                dst = hi[:, slot, :] if slot < RING else hi_x[:, slot - RING, :]
                act.wait_ge(landed[(FIRST_V + j) % RING], 16 * ((FIRST_V + j) // RING + 1) + g * 16)
                wait_at(act, v_mm, -KT, KT, g)
                nc.scalar.activation(dst, raw[:, (FIRST_V + j) % RING, :], ACT.Copy).then_inc(vhi_done, 1)
                act.wait_ge(act_done, g * GROUP + (j + 1))
                nc.scalar.activation(hT_hi[:, slot, 0:SEQ], act_t[:, j, :], ACT.Copy).then_inc(ahi_done, 1)

            act.wait_ge(slab_used, FIRST_V)
            for j in range(GROUP):
                weigh(j, 0, 0)
            for j in range(GROUP):
                weigh(j, 1, 1)
            with act.Fori(1, NGROUP // 2) as i:
                for par in range(2):
                    for j in range(GROUP):
                        weigh(j, i * 2 + par, par)
            norm_scalar(1)
            for t in range(NBLK):
                act.wait_ge(out_turned, t + 1)
                if t >= 2:
                    act.wait_ge(out_sent[t % 2], 16 * (t // 2))
                nc.scalar.activation(tok[:, t % 2, :], psS[:, t % 2, :], ACT.Copy).then_inc(tok_done, 1)

        @block.vector
        def _(dve):
            own = Chain(dve, dve_step)
            V = nc.vector

            def newton(y, var, t1):
                own.link(V.tensor_tensor(t1, y, y, ALU.mult))
                own.link(V.scalar_tensor_tensor(t1, var, EPS, t1, ALU.add, ALU.mult))
                own.link(V.tensor_scalar(t1, t1, -0.5, 1.5, ALU.mult, ALU.add))
                own.link(V.tensor_tensor(y, y, t1, ALU.mult))

            own.link(V.memset(mv[:, :, :], 1.0))
            for t in range(NBLK + 1):
                rows = P if t < NBLK else META
                dve.wait_ge(x_in[t], 16)
                for c in range(2):
                    own.mark(V.bn_stats(stats[0:rows, t, 6 * c:6 * c + 6], xin[0:rows, t, c * 512:(c + 1) * 512]))
                own.settle()
                own.mark(V.bn_aggr(mv[0:rows, t, :], stats[0:rows, t, :]))
            own.settle()
            own.link(V.tensor_copy(rs[:, 1, :], mv[:, :, 1]))
            dve.wait_ge(cst_in, 48)
            V.tensor_copy(rs[:, 2, :], mv[:, :, 0]).then_inc(norm_done, 1)
            dve.wait_ge(std_done, 1)
            own.link(V.reciprocal(rs[:, 3, :], rs[:, 0, :]))
            newton(rs[:, 3, :], rs[:, 1, :], rs[:, 2, :])
            for t in range(NBLK + 1):
                rows = P if t < NBLK else META
                V.tensor_scalar(xin[0:rows, t, :], xin[0:rows, t, :], mv[0:rows, t, 0:1], rs[0:rows, 3, t:t + 1],
                                ALU.subtract, ALU.mult).then_inc(norm_done, 1)
            for k in range(KT):
                dve.wait_ge(turned, k + 1)
                if k >= 2:
                    dve.wait_ge(hT_hi_done, k - 1)
                    dve.wait_ge(hT_lo_done, k - 1)
                V.tensor_scalar(xT[:, k % 2, :], psS[:, k % 2, 0:COLS], ncol[:, k:k + 1], ncol[:, KT + k:KT + k + 1],
                                ALU.mult, ALU.add).then_inc(xT_done, 1)
                dve.wait_ge(xT_done, k + 1)
                dve.wait_ge(hT_hi_done, k + 1)
                V.tensor_tensor(hT_lo[:, k, :], xT[:, k % 2, :], hT_hi[:, k, :].bitcast(F32),
                                ALU.subtract).then_inc(hT_lo_done, 1)
                if k < AHEAD:
                    split_lo(dve, k)
            dve.wait_ge(bias_in, 64)
            dve.wait_ge(w_mm, 1)
            V.tensor_tensor(wrow[:, 0, :], psO[0:HEADS, 0, 0:3 * P], wrow[:, 1, :], ALU.add).then_inc(w_done, 1)
            own.link(V.tensor_scalar(snk[:, 1, :], snk[:, 0, :], -1.0, None, ALU.mult))

            for n in range(N_PROJ):
                split_lo(dve, n + AHEAD)
                dve.wait_ge(slab_used, n + 1)
                bias = bcol[:, n:n + 1]
                ps = psS[:, n % 2, 0:COLS]
                if n == 0:
                    V.tensor_scalar(logf[:, 0, :], ps[0:HEADS, :], bias[0:HEADS, :], None, ALU.add).then_inc(z_done, 1)
                    dve.wait_ge(z_done, 1)
                    V.tensor_scalar(logf[:, 4, :], logf[:, 0, :], 0.0, None, ALU.min).then_inc(evacuated, 1)
                    continue
                if 1 <= n <= 4 or 7 <= n <= 10:
                    dst = (qaT[:, n - 1, :] if n <= 4 else qbT[:, n - 7, :])
                    V.tensor_scalar(dst, ps[:, 0:SEQ], bias, HD ** -0.5, ALU.add, ALU.mult).then_inc(evacuated, 1)
                else:
                    dst = kaT[:, :] if n == 5 else vT[:, 0, :] if n == 6 else (
                        kbT[:, n - 11, :] if n <= 14 else vT[:, n - 14, :])
                    V.tensor_scalar(dst, ps, bias, None, ALU.add).then_inc(evacuated, 1)
                if n == 3:
                    dve.wait_ge(soft_done, 1)
                    own.mark(V.memset(logf[:, 1, :], 1.0))
                    own.link(V.tensor_tensor(logf[:, 4, :], logf[:, 4, :], logf[:, 3, :], ALU.subtract))
                    own.link(V.tensor_tensor_scan(logf[:, 5, SEQ:COLS], logf[:, 1, SEQ:COLS], logf[:, 4, SEQ:COLS],
                                                  0.0, ALU.mult, ALU.add))
                    V.tensor_tensor_scan(logf[:, 5, 0:SEQ], logf[:, 1, 0:SEQ], logf[:, 4, 0:SEQ],
                                         logf[:, 5, COLS - 1:COLS], ALU.mult, ALU.add).then_inc(c_done, 1)
                if n == 8:
                    dve.wait_ge(c_turned, 1)
                    own.link(V.tensor_copy(cq[:, :, :].rearrange("p n h -> p (n h)"), psO[:, 1, 0:NBLK * HEADS]))

            dve.wait_ge(biasA_in, 16)
            dve.wait_ge(ck_in, 16)
            for s in range(UNITS + 4):
                if s < UNITS:
                    window, n, h, tile, half = unit_of(s)
                    L = width_of(s)
                    S = psS[:, s % 2, 0:L]
                    dve.wait_ge(s_mm, s + 1)
                    if window:
                        own.link(V.tensor_tensor(S, S, biasA[:, h, 2 * P - L:2 * P], ALU.add))
                        own.link(V.tensor_reduce(nmax[:, s:s + 1], S, AX.X, ALU.max, negate=True))
                        V.tensor_tensor(nmax[:, s:s + 1], nmax[:, s:s + 1], snk[:, 1, h:h + 1],
                                        ALU.min).then_inc(nmax_done, 1)
                    else:
                        T = P * (n + 1)
                        own.mark(V.scalar_tensor_tensor(S[:, 0:T], S[:, 0:T], cq[:, n, h:h + 1], ckB[:, h, 0:T],
                                                        ALU.add, ALU.subtract))
                        own.link(V.scalar_tensor_tensor(S[:, T:L], S[:, T:L], cq[:, n, h:h + 1], ckB[:, h, SEQ:COLS],
                                                        ALU.add, ALU.subtract))
                        own.link(V.tensor_tensor(S[:, T - P:T], S[:, T - P:T], mask, ALU.add))
                        V.tensor_reduce(nmax[:, s:s + 1], S, AX.X, ALU.max, negate=True).then_inc(nmax_done, 1)
                if 2 <= s <= UNITS + 1 and pieces_of(s - 2)[0 if unit_of(s - 2)[0] else -1][2] is None:
                    u = s - 2
                    dve.wait_ge(p_turned, u + 1)
                    if u >= 2:
                        dve.wait_ge(pv_mm, u - 1)
                    V.tensor_copy(pM[:, u % 2, :], psT[0:META, SEQ:SEQ + P]).then_inc(pM_done, 1)
                if 1 <= s <= UNITS:
                    u = s - 1
                    window = unit_of(u)[0]
                    dve.wait_ge(exp_done, exp_count(u))
                    r0, r1 = rsum[:, 0, u:u + 1], rsum[:, 1, u:u + 1]
                    if window:
                        own.link(V.tensor_tensor(r0, r0, sexp[:, u:u + 1], ALU.add))
                    own.link(V.reciprocal(r1, r0))
                    Pu = pexp[:, u % 2, 0:width_of(u)]
                    V.tensor_scalar(Pu, Pu, r1, None, ALU.mult).then_inc(p_done, 1)
                if s >= 3 and (s - 3) % HEADS == HEADS - 1:
                    w = (s - 3) // HEADS
                    dve.wait_ge(o_hi_done, w + 1)
                    cols = slice((w % NBLK) * P, (w % NBLK + 1) * P)
                    V.tensor_tensor(oT_lo[:, w // NBLK, :, cols], psO[:, w % 2, :].rearrange("p (t q) -> p t q", t=4),
                                    oT_hi[:, w // NBLK, :, cols].bitcast(F32), ALU.subtract).then_inc(o_lo_done, 1)

            for m in range(KT):
                for j in range(3):
                    split_lo(dve, FIRST_MERGE + 3 * m + j + AHEAD)
                dve.wait_ge(slab_used, FIRST_MERGE + 3 * m + 3)
                dve.wait_ge(gate_done, 2 * m + 2)
                if m >= 2:
                    dve.wait_ge(m_hi_done, m - 1)
                for j in range(2):
                    own.mark(V.tensor_tensor(mix[:, m % 2, j, :], banks[4 + 2 * (m % 2) + j], gate[:, m % 2, j, :], ALU.mult))
                own.settle()
                V.tensor_tensor(mix[:, m % 2, 0, :], mix[:, m % 2, 0, :], mix[:, m % 2, 1, :], ALU.add).then_inc(mix_done, 1)
                dve.wait_ge(m_hi_done, m + 1)
                V.tensor_tensor(m_lo[:, m, :], mix[:, m % 2, 0, :], m_hi[:, m, :].bitcast(F32),
                                ALU.subtract).then_inc(m_lo_done, 1)
            for m in range(KT):
                split_lo(dve, FIRST_OUT + m + AHEAD)
                own.link(V.tensor_tensor(acc[:, m, :], hT_hi[:, m, 0:SEQ].bitcast(F32), hT_lo[:, m, 0:SEQ].bitcast(F32),
                                         ALU.add))
                dve.wait_ge(slab_used, FIRST_OUT + m + 1)
                V.scalar_tensor_tensor(acc[:, m, :], acc[:, m, :], ALPHA, psS[:, m % 2, 0:SEQ],
                                       ALU.mult, ALU.add).then_inc(r_done, 1)

            def norm_vector(r):
                dve.wait_ge(mean_mm, r + 1)
                for k in range(KT):
                    V.tensor_tensor(acc[:, k, :], acc[:, k, :], banks[4], ALU.subtract).then_inc(xc_done, 1)
                dve.wait_ge(sd_done, r + 1)
                own.link(V.reciprocal(rinv[:, :], nw[:, 0, :]))
                newton(rinv[:, :], banks[5], nw[:, 1, :])
                for k in range(KT):
                    own.mark(V.tensor_tensor(acc[:, k, :], acc[:, k, :], rinv[:, :], ALU.mult))
                own.settle()
                g = 2 * KT * (r + 1)
                for k in range(KT):
                    V.tensor_scalar(acc[:, k, :], acc[:, k, :], ncol[:, g + k:g + k + 1],
                                    ncol[:, g + KT + k:g + KT + k + 1], ALU.mult, ALU.add).then_inc(h_done, 1)

            norm_vector(0)
            for k in range(KT):
                dve.wait_ge(hT_hi_done, KT + k + 1)
                V.tensor_tensor(hT_lo[:, k, 0:SEQ], acc[:, k, :], hT_hi[:, k, 0:SEQ].bitcast(F32),
                                ALU.subtract).then_inc(hT_lo_done, 1)
                dve.wait_ge(hT_lo_done, KT + k + 1)
                V.tensor_scalar(acc[:, k, :], acc[:, k, :], ALPHA, None, ALU.mult).then_inc(scaled, 1)
            dve.wait_ge(sk_hi_done, 1)
            V.tensor_tensor(sk_lo[:, :, :], sk_raw[:, :, :], sk_hi[:, :, :].bitcast(F32), ALU.subtract).then_inc(sk_done, 1)
            for q in range(N_PQ):
                split_lo(dve, FIRST_PQ + q + AHEAD)
                dve.wait_ge(pq_hi_done, q + 1)
                if q >= 2:
                    dve.wait_ge(sc_mm, q - 1)
                V.tensor_tensor(pq_lo[:, q % 2, :], psS[:, q % 2, 0:SEQ], pq_hi[:, q % 2, :].bitcast(F32),
                                ALU.subtract).then_inc(pq_lo_done, 1)

            def top_part(part, i):
                if part == 0:
                    dve.wait_ge(now_done, i + 1)
                    V.memset(spare[:, :], 0.0)
                    for p in range(2):
                        own.mark(V.max(topv[:, p, 0:8], now[:, p, :]))
                    own.settle_apart(V.memset, spare[:, :])
                    for p in range(2):
                        own.mark(V.max_index(topi[:, p, 0:8], topv[:, p, 0:8], now[:, p, :]))
                        own.mark(V.match_replace(rest[:, p * NKEYS:(p + 1) * NKEYS], topv[:, p, 0:8], now[:, p, :], LOWEST))
                    own.settle_apart(V.memset, spare[:, :])
                    for p in range(2):
                        own.mark(V.max(topv[:, p, 8:16], rest[:, p * NKEYS:(p + 1) * NKEYS]))
                    own.settle()
                if part == 1:
                    for p in range(2):
                        own.mark(V.max_index(topi[:, p, 8:16], topv[:, p, 8:16], rest[:, p * NKEYS:(p + 1) * NKEYS]))
                    own.link(V.tensor_tensor(cand[:, :].rearrange("p (a b) -> p a b", a=TOPK),
                                             topv[:, 0, :].unsqueeze(2).to_broadcast([P, TOPK, TOPK]),
                                             topv[:, 1, :].unsqueeze(1).to_broadcast([P, TOPK, TOPK]), ALU.add))
                    own.mark(V.tensor_copy(topf[:, :, :], topi[:, :, :]))
                    own.mark(V.max(topv[:, 0, 0:8], cand[:, :]))
                if part == 2:
                    own.settle_apart(V.memset, spare[:, :])
                    own.mark(V.max_index(flat[:, 0:8], topv[:, 0, 0:8], cand[:, :]))
                    own.mark(V.match_replace(rest[:, :], topv[:, 0, 0:8], cand[:, :], LOWEST))
                    own.settle_apart(V.memset, spare[:, :])
                    own.mark(V.max(topv[:, 0, 8:16], rest[:, :]))
                    own.settle_apart(V.memset, spare[:, :])
                    own.mark(V.max_index(flat[:, 8:16], topv[:, 0, 8:16], rest[:, :]))
                    own.link(V.tensor_copy(best[:, bass.ds(i * TOPK, TOPK)], topv[:, 0, :]))
                    own.mark(V.tensor_single_scalar(pos[:, 0, :], flat[:, :], 4, ALU.logical_shift_right))
                    own.link(V.tensor_single_scalar(pos[:, 1, :], flat[:, :], TOPK - 1, ALU.bitwise_and))
                    own.link(V.tensor_copy(posf[:, :, :], pos[:, :, :]))
                if part == 3:
                    view = eq[:, :, :].rearrange("p s (k j) -> p s k j", k=TOPK)
                    for p in range(2):
                        own.mark(V.tensor_tensor(view[:, p], posf[:, p, :].unsqueeze(2).to_broadcast([P, TOPK, TOPK]),
                                                 iota16.unsqueeze(1).to_broadcast([P, TOPK, TOPK]), ALU.is_equal))
                    own.settle()
                    for p in range(2):
                        own.mark(V.tensor_tensor(view[:, p], view[:, p],
                                                 topf[:, p, :].unsqueeze(1).to_broadcast([P, TOPK, TOPK]), ALU.mult))
                    own.settle()
                    own.mark(V.tensor_reduce(ia[:, bass.ds(i * TOPK, TOPK)], view[:, 0], AX.X, ALU.add))
                    V.tensor_reduce(ib[:, bass.ds(i * TOPK, TOPK)], view[:, 1], AX.X, ALU.add).then_inc(top_done, 1)

            def expert_inputs(i, last=False):
                for j in range(GROUP):
                    if not (last and j >= GROUP - AHEAD):
                        split_lo(dve, FIRST_U + j + AHEAD, i, GROUP)
                    top_part(j, i)
                own.settle()

            expert_inputs(0)
            each = own.n
            with dve.Fori(1, NGROUP - 1) as i:
                own.loop(i - 1, TOP_STEPS)
                expert_inputs(i)
                own.end(NGROUP - 2)
            expert_inputs(NGROUP - 1, last=True)

            dve.wait_ge(top_done, NGROUP)
            b3 = best[:, :].rearrange("p (u k) -> p u k", k=TOPK)
            own.link(V.tensor_reduce(gsum[:, 2, :], b3, AX.X, ALU.max))
            V.tensor_tensor(b3, b3, gsum[:, 2, :].unsqueeze(2).to_broadcast([P, NBLK * HEADS, TOPK]),
                            ALU.subtract).then_inc(less_done, 1)
            own.link(V.tensor_copy(iota_h[:, :], cst[:, C_IOTA:C_IOTA + P]))
            dve.wait_ge(g_exp_done, 1)
            own.link(V.tensor_reduce(gsum[:, 0, :], b3, AX.X, ALU.add))
            own.link(V.reciprocal(gsum[:, 1, :], gsum[:, 0, :]))
            V.tensor_tensor(b3, b3, gsum[:, 1, :].unsqueeze(2).to_broadcast([P, NBLK * HEADS, TOPK]),
                            ALU.mult).then_inc(g_done, 1)
            dve.wait_ge(idx_turned, 1)
            own.mark(V.tensor_copy(iaT[:, :], banks[0]))
            own.mark(V.tensor_copy(ibT[:, :], banks[1]))
            dve.wait_ge(gT_hi_done, 1)
            own.mark(V.scalar_tensor_tensor(gT_lo[:, :], banks[2], GATE_SCALE, gT_hi[:, :], ALU.mult, ALU.subtract))
            own.settle()
            V.tensor_copy(gsum[:, 0, 0:1], gsum[:, 1, 0:1]).then_inc(idx_done, 1)
            for j in range(RING):
                dve.wait_ge(gelu_out[j], 16 * NGROUP)

            def hot(q, r):
                wait_at(dve, G_mm, -1, 1, q)
                toks = bass.ds(q * CHUNK, CHUNK)

                def spread(v):
                    return v[:, toks].unsqueeze(1).to_broadcast([P, NKEYS, CHUNK])

                keys = iota_h[:, :].unsqueeze(2).to_broadcast([P, NKEYS, CHUNK])
                own.mark(V.tensor_tensor(hotA[:, r], spread(iaT), keys, ALU.is_equal))
                own.link(V.tensor_tensor(hotB[:, :, :], spread(ibT), keys, ALU.is_equal))
                own.mark(V.tensor_tensor(hotG_hi[:, r], hotB[:, :, :], spread(gT_hi), ALU.mult))
                V.tensor_tensor(hotG_lo[:, r], hotB[:, :, :], spread(gT_lo), ALU.mult).then_inc(hot_done, 1)

            for r in range(2):
                hot(r, r)
                dve.wait_ge(hot_done, r + 1)
            with dve.Fori(1, SEQ // CHUNK // 2) as i:
                own.loop(i - 1, 6)
                for r in range(2):
                    hot(i * 2 + r, r)
                    dve.wait_ge(hot_done, i * 2 + (r + 1))
                own.end(SEQ // CHUNK // 2 - 1)

            def weigh(j, g, par, part):
                slot = par * GROUP + j
                src = hi[:, slot, :] if slot < RING else hi_x[:, slot - RING, :]
                dst = lo[:, slot, :] if slot < RING else lo_x[:, slot - RING, :]
                if part == 0:
                    dve.wait_ge(gel_in_s[j], 16 + g * 16)
                    dve.wait_ge(gate_in_s[j], 16 + g * 16)
                    wait_at(dve, ahi_done, j - RING + 1, RING, g)
                    wait_at(dve, alo_done, j - RING + 1, RING, g)
                    V.tensor_tensor(act_t[:, j, :], gel_in[:, j, :], gate_in[:, j, :], ALU.mult).then_inc(act_done, 1)
                    dve.wait_ge(vhi_done, g * GROUP + (j + 1))
                    V.tensor_tensor(dst, raw[:, (FIRST_V + j) % RING, :], src.bitcast(F32), ALU.subtract).then_inc(vlo_done, 1)
                else:
                    dve.wait_ge(ahi_done, g * GROUP + (j + 1))
                    V.tensor_tensor(hT_lo[:, slot, 0:SEQ], act_t[:, j, :], hT_hi[:, slot, 0:SEQ].bitcast(F32),
                                    ALU.subtract).then_inc(alo_done, 1)

            def group(g, par, last=False):
                for m in range(KT):
                    if not last:
                        weigh(m // 2, g + 1, 1 - par, m % 2)
                    dve.wait_ge(v_mm, g * KT + (m + 1))
                    V.tensor_tensor(acc[:, m, :], acc[:, m, :], banks[4 + m % 4], ALU.add).then_inc(y_added, 1)

            for j in range(GROUP):
                weigh(j, 0, 0, 0)
                weigh(j, 0, 0, 1)
            with dve.Fori(0, NGROUP // 2 - 1) as i:
                for par in range(2):
                    group(i * 2 + par, par)
            group(NGROUP - 2, 0)
            group(NGROUP - 1, 1, last=True)
            dve.wait_ge(y_added, NGROUP * KT)
            norm_vector(1)

        @block.tensor
        def _(pe):
            mm, turn = nc.tensor.matmul, nc.tensor.transpose

            def slab(n, slot, out_ap, x_h, x_l, ks, i=0, per=0):
                for a, (k, kx) in enumerate(ks):
                    wh, wl = slab_parts(slot, k)
                    last = split_product(out_ap, wh, wl, x_h(kx), x_l(kx), a == 0, a == len(ks) - 1)
                return last

            def tokens(k):
                return hT_hi[:, k, 0:SEQ]

            def tokens_lo(k):
                return hT_lo[:, k, 0:SEQ]

            all_k = [(k, k) for k in range(KT)]
            pe.wait_ge(cst_in, 48)
            pe.wait_ge(norm_done, NBLK + 2)
            for k in range(KT):
                if k >= 2:
                    pe.wait_ge(xT_done, k - 1)
                for t in range(NBLK):
                    turn(psS[:, k % 2, t * P:(t + 1) * P], xin[:, t, k * P:(k + 1) * P], ident)
                turn(psS[:, k % 2, SEQ:COLS], xin[0:META, NBLK, k * P:(k + 1) * P],
                     ident[0:META, 0:META]).then_inc(turned, 1)
            pe.wait_ge(bias_in, 64)
            mm(psO[0:HEADS, 0, 0:3 * P], relb[:, :], buck[:, :], start=True, stop=True).then_inc(w_mm, 1)
            pe.wait_ge(hT_lo_done, KT)
            for n in range(N_PROJ):
                pe.wait_ge(lo_done, n + 1)
                if n >= 2:
                    pe.wait_ge(evacuated, n - 1)
                last = slab(n, n % RING, psS[:, n % 2, 0:SEQ], tokens, tokens_lo, all_k)
                if not (1 <= n <= 4 or 7 <= n <= 10):
                    last = slab(n, n % RING, psS[:, n % 2, SEQ:COLS], lambda k: hT_hi[:, k, SEQ:COLS],
                                lambda k: hT_lo[:, k, SEQ:COLS], all_k)
                last.then_inc(slab_used, 1)
                if n == 6:
                    pe.wait_ge(c_done, 1)
                    for b in range(NBLK):
                        last = turn(psO[:, 1, b * HEADS:(b + 1) * HEADS], logf[:, 5, b * P:(b + 1) * P],
                                    ident[0:HEADS, 0:HEADS])
                    last.then_inc(c_turned, 1)
            pe.wait_ge(evacuated, N_PROJ)
            for b in range(NBLK + 1):
                if 2 <= b < NBLK:
                    pe.wait_ge(v_ready, b - 1)
                for f in range(5):
                    if b < NBLK:
                        last = turn(psS[:, b % 2, f * P:(f + 1) * P], vT[:, f, b * P:(b + 1) * P], ident)
                    else:
                        last = turn(psT[0:META, f * P:(f + 1) * P], vT[:, f, SEQ:COLS], ident)
                last.then_inc(v_turned, 1)
            pe.wait_ge(v_ready, NBLK + 1)

            def key_cols(block_no):
                return slice(SEQ, COLS) if block_no is None else slice(block_no * P, (block_no + 1) * P)

            for s in range(UNITS + 2):
                if s < UNITS:
                    window, n, h, tile, half = unit_of(s)
                    rows = slice(HD * half, HD * half + HD)
                    if s >= 2:
                        pe.wait_ge(exp_done, exp_count(s - 2))
                    q = (qaT if window else qbT)[rows, tile, n * P:(n + 1) * P]
                    for c, width, b in pieces_of(s):
                        k = kaT[rows, key_cols(b)] if window else kbT[rows, tile, key_cols(b)]
                        last = mm(psS[:, s % 2, c:c + width], q, k, start=True, stop=True)
                    last.then_inc(s_mm, 1)
                if 1 <= s <= UNITS:
                    u = s - 1
                    pe.wait_ge(p_done, u + 1)
                    if u >= 1:
                        pe.wait_ge(pT_done, u)
                        pe.wait_ge(pM_done, max(1, meta_count(u - 1)))
                    at = 0
                    for c, width, b in pieces_of(u):
                        src = pexp[:, u % 2, c:c + width]
                        if b is None:
                            last = turn(psT[0:META, SEQ:SEQ + P], src, ident)
                        else:
                            last = turn(psT[:, at:at + P], src, ident)
                            at += P
                    last.then_inc(p_turned, 1)
                if s >= 2:
                    u = s - 2
                    window, n, h, tile, half = unit_of(u)
                    w = u // HEADS
                    pe.wait_ge(pT_done, u + 1)
                    pe.wait_ge(pM_done, max(1, meta_count(u)))
                    if w >= 2 and h == 0:
                        pe.wait_ge(o_hi_done, w - 1)
                        pe.wait_ge(o_lo_done, w - 1)
                    f = half * HD if window else P + h * HD
                    dst = psO[HD * half:HD * half + HD, w % 2, tile * P:(tile + 1) * P]
                    pieces = pieces_of(u)
                    at = 0
                    for a, (_, _, b) in enumerate(pieces):
                        ends = dict(start=a == 0, stop=a == len(pieces) - 1)
                        if b is None:
                            last = mm(dst, vM[:, f:f + HD], pM[:, u % 2, :], **ends)
                        else:
                            last = mm(dst, vN[:, b, f:f + HD], pT[:, u % 2, at:at + P], **ends)
                            at += P
                    last.then_inc(pv_mm, 1)

            pe.wait_ge(o_lo_done, 2 * NBLK)
            for m in range(KT):
                for j in range(3):
                    n = FIRST_MERGE + 3 * m + j
                    pe.wait_ge(lo_done, n + 1)
                    if j < 2:
                        if m >= 2:
                            pe.wait_ge(gate_done, 2 * (m - 2) + j + 1)
                        last = slab(n, n % RING, psS[:, m % 2, j * SEQ:(j + 1) * SEQ], tokens, tokens_lo, all_k)
                    else:
                        if m >= 2:
                            pe.wait_ge(mix_done, m - 1)
                        for e in range(2):
                            last = slab(n, n % RING, banks[4 + 2 * (m % 2) + e], lambda k: oT_hi[:, e, k, :],
                                        lambda k: oT_lo[:, e, k, :], [(4 * e + k, k) for k in range(4)])
                    last.then_inc(slab_used, 1)
            pe.wait_ge(gate_done, 2 * KT)
            for m in range(N_OUT):
                n = FIRST_OUT + m
                pe.wait_ge(lo_done, n + 1)
                pe.wait_ge(m_lo_done, KT)
                if m >= 2:
                    pe.wait_ge(r_done, m - 1)
                slab(n, n % RING, psS[:, m % 2, 0:SEQ], lambda k: m_hi[:, k, :], lambda k: m_lo[:, k, :],
                     all_k).then_inc(slab_used, 1)

            def norm_tensor(r):
                for k in range(KT):
                    last = mm(banks[4], mean_of, acc[:, k, :], start=k == 0, stop=k == KT - 1)
                last.then_inc(mean_mm, 1)
                for k in range(KT):
                    pe.wait_ge(sq_done, KT * r + k + 1)
                    mm(banks[5], mean_of, sq[:, k % 2, :], start=k == 0, stop=k == KT - 1).then_inc(var_mm, 1)

            pe.wait_ge(r_done, N_OUT)
            norm_tensor(0)
            pe.wait_ge(hT_lo_done, 2 * KT)
            pe.wait_ge(sk_done, 1)
            for q in range(N_PQ + 1):
                if q < N_PQ:
                    n = FIRST_PQ + q
                    pe.wait_ge(lo_done, n + 1)
                    if q >= 2:
                        pe.wait_ge(pq_lo_done, q - 1)
                    slab(n, n % RING, psS[:, q % 2, 0:SEQ], tokens, tokens_lo, all_k).then_inc(slab_used, 1)
                if q >= 1:
                    c = q - 1
                    pe.wait_ge(pq_lo_done, c + 1)
                    if c >= 4:
                        pe.wait_ge(sc_done, c - 3)
                    for t in range(NBLK):
                        toks = slice(t * P, (t + 1) * P)
                        last = split_product(banks[4 + c % 4][:, toks], pq_hi[:, c % 2, toks], pq_lo[:, c % 2, toks],
                                             sk_hi[:, c, :], sk_lo[:, c, :], True, True)
                    last.then_inc(sc_mm, 1)

            def expert_inputs(i):
                for j in range(GROUP):
                    n = FIRST_U + j
                    pe.wait_ge(lo_done, n + 1 + i * GROUP)
                    wait_at(pe, gelu_done, j - GROUP + 1, GROUP, i)
                    slab(n, n % RING, banks[j], tokens, tokens_lo, all_k).then_inc(slab_used, 1)

            pe.wait_ge(pq_lo_done, N_PQ)
            expert_inputs(0)
            with pe.Fori(1, NGROUP) as i:
                expert_inputs(i)

            pe.wait_ge(gelu_done, NKEYS)
            pe.wait_ge(sc_done, N_PQ)
            pe.wait_ge(g_done, 1)
            for a, v in enumerate((ia, ib, best)):
                for t in range(NBLK):
                    last = turn(banks[a][:, t * P:(t + 1) * P], v[:, t * P:(t + 1) * P], ident)
            last.then_inc(idx_turned, 1)
            pe.wait_ge(idx_done, 1)

            def gate_matrices(q, r):
                pe.wait_ge(hot_done, q + 1)
                wait_at(pe, G_act, -1, 1, q)
                for c in range(CHUNK):
                    dst = banks[4 * r + c // 4][:, (c % 4) * P:(c % 4 + 1) * P]
                    mm(dst, hotA[:, r, :, c], hotG_hi[:, r, :, c], start=True, stop=False)
                    last = mm(dst, hotA[:, r, :, c], hotG_lo[:, r, :, c], start=False, stop=True)
                last.then_inc(G_mm, 1)

            for r in range(2):
                gate_matrices(r, r)
            with pe.Fori(1, SEQ // CHUNK // 2) as i:
                for r in range(2):
                    gate_matrices(i * 2 + r, r)

            def group(g, par):
                pe.wait_ge(vlo_done, (g + 1) * GROUP)
                pe.wait_ge(alo_done, (g + 1) * GROUP)
                for m in range(KT):
                    wait_at(pe, y_added, m - 3, KT, g)
                    for j in range(GROUP):
                        slot = par * GROUP + j
                        wh, wl = (hi, lo) if slot < RING else (hi_x, lo_x)
                        cols = slice(m * P, (m + 1) * P)
                        last = split_product(banks[4 + m % 4], wh[:, slot % RING, cols], wl[:, slot % RING, cols],
                                             hT_hi[:, slot, 0:SEQ], hT_lo[:, slot, 0:SEQ], j == 0, j == GROUP - 1)
                    last.then_inc(v_mm, 1)

            pe.wait_ge(G_act, SEQ // CHUNK)
            for g in range(2):
                group(g, g)
            with pe.Fori(1, NGROUP // 2) as i:
                for par in range(2):
                    group(i * 2 + par, par)
            pe.wait_ge(y_added, NGROUP * KT)
            norm_tensor(1)
            pe.wait_ge(h_done, 2 * KT)
            for t in range(NBLK):
                if t >= 2:
                    pe.wait_ge(tok_done, t - 1)
                for k in range(KT):
                    last = turn(psS[:, t % 2, k * P:(k + 1) * P], acc[:, k, t * P:(t + 1) * P], ident)
                last.then_inc(out_turned, 1)


def constants():
    c = np.zeros((P, C_COLS), np.float32)
    c[:, C_ID:C_ID + P] = np.eye(P)
    c[:, C_MASK:C_MASK + P] = np.where(np.arange(P)[None, :] > np.arange(P)[:, None], NEG, 0.0)
    c[:, C_MEAN:C_MEAN + P] = 1.0 / D
    c[:, C_IOTA:C_IOTA + P] = np.arange(P)
    c[:, C_IOTA16:C_IOTA16 + TOPK] = np.arange(TOPK)
    c[:, C_EPS] = EPS
    c[:, C_ONE] = 1.0
    dist = 2 * P - 1 - np.arange(3 * P)
    inside = (dist >= 0) & (dist < P)
    d = np.clip(dist, 1, P - 1).astype(np.float32)
    exact = BUCKETS // 2
    large = exact + (np.log(d / exact) / np.log(P / exact) * (BUCKETS - exact)).astype(np.int32)
    bucket = np.where(dist < exact, np.clip(dist, 0, P), np.minimum(large, BUCKETS - 1))
    hot = ((np.arange(BUCKETS)[:, None] == bucket[None, :]) & inside[None, :]).astype(np.float32)
    outside = np.repeat(np.where(inside, 0.0, NEG)[None, :], HEADS, axis=0).astype(np.float32)
    return c, hot, outside


def tiles(w):
    k, f = w.shape
    return w.reshape(k // P, P, f // P, P).transpose(2, 1, 0, 3)


def kernel(x, meta_tokens, emb_ln_g, emb_ln_b, rel_bias, w_in, b_in, attn_sinks, w_pa, w_pb, w_o,
           ln1_g, ln1_b, peer_wq, peer_subkeys, peer_u, peer_v, ln2_g, ln2_b):
    import concourse.bacc as bacc
    from concourse.bass_utils import run_bass_kernel_spmd

    a = {k: np.asarray(v) for k, v in dict(
        x=x, meta=meta_tokens, eg=emb_ln_g, eb=emb_ln_b, rel=rel_bias, w_in=w_in, b_in=b_in, sinks=attn_sinks, w_pa=w_pa,
        w_pb=w_pb, w_o=w_o, g1=ln1_g, b1=ln1_b, wq=peer_wq, sk=peer_subkeys, u=peer_u, v=peer_v, g2=ln2_g,
        b2=ln2_b).items()}
    order = [h + 4 * s for h in range(4) for s in range(2)]
    qa, ka, va, qb, kb, vb = 0, 512, 640, 768, 1280, 1792
    fb = vb + 512
    ga = fb + HEADS
    gb = ga + D
    win = a["w_in"][0]
    pick = np.concatenate([np.arange(fb, fb + P)] + [np.arange(qa + h * HD, qa + (h + 1) * HD) for h in order] +
                          [np.arange(ka, ka + 2 * P), np.arange(qb, fb)])
    w_proj = tiles(win[:, pick])
    both = np.stack([tiles(win[:, ga:ga + D]), tiles(win[:, gb:gb + D]),
                     np.concatenate([tiles(a["w_pa"][0].reshape(HEADS, HD, D)[order].reshape(512, D)),
                                     tiles(a["w_pb"][0])], axis=2)], axis=1)
    bias = a["b_in"][0]
    b_cols = np.concatenate([bias[pick], bias[ga:ga + 2 * D]]).reshape(-1, P).T
    norm_cols = np.stack([a[n].reshape(KT, P) for n in ("eg", "eb", "g1", "b1", "g2", "b2")]).reshape(-1, P).T
    cst, hot, outside = constants()
    ins = {
        "x": a["x"][0], "meta": a["meta"], "consts": cst, "buckets": hot, "outside": outside, "norm_cols": norm_cols,
        "b_cols": b_cols, "rel_bias": a["rel"], "sinks": a["sinks"][0],
        "w_proj": w_proj.reshape(N_PROJ, P, D), "w_merge": both.reshape(N_MERGE, P, D),
        "w_out": tiles(a["w_o"][0]).reshape(N_OUT, P, D), "w_pq": tiles(a["wq"][0]).reshape(N_PQ, P, D),
        "subkeys": a["sk"][0].reshape(2 * HEADS, NKEYS, P).transpose(2, 0, 1),
        "u_exp": a["u"][0].reshape(NKEYS, NKEYS, KT, P).transpose(1, 3, 2, 0).reshape(NKEYS, P, D),
        "v_exp": a["v"][0].reshape(NKEYS, NKEYS, D).transpose(1, 0, 2),
    }
    nc = bacc.Bacc("TRN2", target_bir_lowering=False, num_devices=1)
    arrays, args = {}, []
    for name, v in ins.items():
        v = np.ascontiguousarray(v)
        arrays[f"in_{name}"] = v
        args.append(nc.dram_tensor(f"in_{name}", v.shape, mybir.dt.from_np(v.dtype), kind="ExternalInput").ap())
    out = nc.dram_tensor("out_0", (SEQ, D), F32, kind="ExternalOutput").ap()
    build(nc, *args, out)
    r = run_bass_kernel_spmd(nc, [arrays], core_ids=[0])
    return r.results[0]["out_0"].reshape(1, SEQ, D)
```

```python
from contextlib import ExitStack

import numpy as np

import concourse.bass as bass
from concourse import mybir

P = 128
D = 1024
SEQ = 512
META = 16
COLS = SEQ + META
KT = D // P
NBLK = SEQ // P
HEADS = 8
HD = 64
NKEYS = 128
TOPK = 16
BUCKETS = 32
EPS = 1e-5
ALPHA = 2.0 ** 0.25
NEG = -1e30
LOWEST = -3.0e38
GATE_SCALE = 2.0 ** 15

RING = 4
N_PROJ = 19
N_MERGE = 24
N_OUT = 8
N_PQ = 16
FIRST_MERGE = N_PROJ
FIRST_OUT = FIRST_MERGE + N_MERGE
FIRST_PQ = FIRST_OUT + N_OUT
FIRST_U = FIRST_PQ + N_PQ
FIRST_V = FIRST_U + NKEYS
UNITS = 2 * NBLK * HEADS
GROUP = 4
NGROUP = NKEYS // GROUP
BGROUP = NGROUP // NBLK
CHUNK = P // (BGROUP // 2 * GROUP)
RANGES = 4
TOP_MARKS = 52
HOT_MARKS = 12
BATCHES = SEQ // CHUNK

F32 = mybir.dt.float32
F32R = mybir.dt.float32r
F16 = mybir.dt.float16
U32 = mybir.dt.uint32
ALU = mybir.AluOpType
ACT = mybir.ActivationFunctionType
AX = mybir.AxisListType

C_ID, C_MASK, C_MEAN, C_IOTA, C_IOTA16, C_EPS, C_ONE = 0, 128, 256, 384, 512, 528, 529
C_COLS = 530


class Chain:

    def __init__(self, eng, sem):
        self.eng, self.sem, self.n, self.past = eng, sem, 0, 0

    def mark(self, ins):
        ins.then_inc(self.sem, 1)
        self.n += 1

    def settle(self):
        self.eng.wait_ge(self.sem, self.n + self.past)

    def settle_apart(self, memset, spare):
        self.settle()
        memset(spare, 0.0)

    def link(self, ins):
        self.mark(ins)
        self.settle()

    def loop(self, i, each):
        self.start, self.each, self.past = self.n, each, i * each

    def end(self, times):
        assert self.n - self.start == self.each, (self.n - self.start, self.each)
        self.n = self.start + self.each * times
        self.past = 0


def unit_of(u):
    window = u < UNITS // 2
    n, h = (u % (UNITS // 2)) // HEADS, u % HEADS
    tile, half = (h % 4, h // 4) if window else (h // 2, h % 2)
    return window, n, h, tile, half


def pieces_of(u):
    window, n, _, _, _ = unit_of(u)
    if window:
        return [(0, META, None), (META, P, 0)] if n == 0 else [(0, P, n - 1), (P, P, n)]
    return [(P * b, P, b) for b in range(n + 1)] + [(P * (n + 1), META, None)]


def width_of(u):
    c, k, _ = pieces_of(u)[-1]
    return c + k


def build(nc, x, meta, consts, buckets, outside, norm_cols, b_cols, rel_bias, sinks, w_proj, w_merge, w_out,
          w_pq, subkeys, u_exp, v_exp, out):
    ctx = ExitStack()
    with ctx:
        def sem(name):
            return ctx.enter_context(nc.semaphore(name))

        def place(stack, **specs):
            return [stack.enter_context(nc.sbuf_tensor(n, s, t)) for n, (s, t) in specs.items()]

        cst, ncol, bcol = place(ctx, cst=([P, C_COLS], F32), ncol=([P, 6 * KT], F32), bcol=([P, N_PROJ + 16], F32))
        raw, hi, lo = place(ctx, raw=([P, RING, D], F32), hi=([P, RING, D], F32R), lo=([P, RING, D], F32R))
        hT_hi, hT_lo = place(ctx, hT_hi=([P, KT, COLS], F32R), hT_lo=([P, KT, COLS], F32R))
        ident = cst[:, C_ID:C_ID + P]
        mask = cst[:, C_MASK:C_MASK + P]
        mean_of = cst[:, C_MEAN:C_MEAN + P]
        iota16 = cst[:, C_IOTA16:C_IOTA16 + TOPK]
        eps = cst[:, C_EPS:C_EPS + 1]
        one = cst[:, C_ONE:C_ONE + 1]
        spare, = place(ctx, spare=([P, 1], F32))
        with ExitStack() as s:
            biasA, qaT = place(s, biasA=([P, HEADS, 2 * P], F32), qaT=([P, 4, SEQ], F32))
        acc, = place(ctx, acc=([P, KT, SEQ], F32))
        with ExitStack() as s:
            xin, xT = place(s, xin=([P, 5, D], F32), xT=([P, 2, COLS], F32))
            stats, mv, rs = place(s, stats=([P, 5, 12], F32), mv=([P, 5, 2], F32), rs=([P, 4, 5], F32))
        with ExitStack() as s:
            vT, logf = place(s, vT=([P, 5, COLS], F32), logf=([HEADS, 6, COLS], F32))
        with ExitStack() as s:
            oT_hi, oT_lo = place(s, oT_hi=([P, 2, 4, SEQ], F32R), oT_lo=([P, 2, 4, SEQ], F32R))
            with ExitStack() as t:
                kaT, qbT, kbT = place(t, kaT=([P, COLS], F32), qbT=([P, 4, SEQ], F32), kbT=([P, 4, COLS], F32))
                vN, vM = place(t, vN=([P, NBLK, 640], F32), vM=([META, 640], F32))
                ckB, cq = place(t, ckB=([P, HEADS, COLS], F32), cq=([P, NBLK, HEADS], F32))
                pexp, pT, pM = place(t, pexp=([P, 2, COLS], F32), pT=([P, 2, SEQ], F32), pM=([META, 2, P], F32))
                nmax, rsum, sexp, snk = place(t, nmax=([P, UNITS], F32), rsum=([P, 2, UNITS], F32),
                                              sexp=([P, UNITS], F32), snk=([P, 2, HEADS], F32))
                relb, buck, wrow = place(t, relb=([BUCKETS, HEADS], F32), buck=([BUCKETS, 3 * P], F32),
                                         wrow=([HEADS, 2, 3 * P], F32))
            gate, mix = place(s, gate=([P, 2, 2, SEQ], F32), mix=([P, 2, 2, SEQ], F32))
            m_hi, m_lo = place(s, m_hi=([P, KT, SEQ], F32R), m_lo=([P, KT, SEQ], F32R))
        with ExitStack() as s:
            sq, rinv, nw = place(s, sq=([P, 2, SEQ], F32), rinv=([P, SEQ], F32), nw=([P, 2, SEQ], F32))
        with ExitStack() as s:
            gelu, now = place(s, gelu=([P, RING, SEQ], F32), now=([P, 2, 2, NKEYS], F32))
            ia, ib, best = place(s, ia=([P, P], F32), ib=([P, P], F32), best=([P, P], F32))
            rest, cand, topv, topi, topf = place(
                s, rest=([P, 2 * NKEYS], F32), cand=([P, TOPK * TOPK], F32),
                topv=([P, 2, TOPK], F32), topi=([P, 2, TOPK], U32), topf=([P, 2, TOPK], F32))
            flat, pos, posf, eq = place(s, flat=([P, TOPK], U32), pos=([P, 2, TOPK], U32),
                                        posf=([P, 2, TOPK], F32), eq=([P, 2, TOPK * TOPK], F32))
            gsum, iaT, ibT, gT_hi, gT_lo, iota_h = place(
                s, gsum=([P, 3, HEADS], F32), iaT=([P, P], F16), ibT=([P, P], F16), gT_hi=([P, P], F16),
                gT_lo=([P, P], F16), iota_h=([P, NKEYS, CHUNK], F16))
            hotA, hotB, hotG_hi, hotG_lo = place(
                s, hotA=([P, 2, NKEYS, CHUNK], F16), hotB=([P, NKEYS, CHUNK], F16),
                hotG_hi=([P, 2, NKEYS, CHUNK], F16), hotG_lo=([P, 2, NKEYS, CHUNK], F16))
            with ExitStack() as t:
                sk_raw, sk_hi, sk_lo = place(t, sk_raw=([P, 2 * HEADS, NKEYS], F32),
                                             sk_hi=([P, 2 * HEADS, NKEYS], F32R), sk_lo=([P, 2 * HEADS, NKEYS], F32R))
                pq_hi, pq_lo, sc = place(t, pq_hi=([P, 2, SEQ], F32R), pq_lo=([P, 2, SEQ], F32R), sc=([P, 2, SEQ], F32))
            gates, = place(s, gates=([P, NKEYS, P], F32))
        with ExitStack() as s:
            gel_in, gate_in, act_t = place(s, gel_in=([P, RING, SEQ], F32), gate_in=([P, RING, SEQ], F32),
                                           act_t=([P, RING, SEQ], F32))
            hi_x, lo_x = place(s, hi_x=([P, RING, D], F32R), lo_x=([P, RING, D], F32R))
        with ExitStack() as s:
            tok, = place(s, tok=([P, 2, D], F32))

        psS = ctx.enter_context(nc.psum_tensor("psS", [P, 2, 2 * SEQ], F32))
        psT = ctx.enter_context(nc.psum_tensor("psT", [P, 2 * SEQ], F32))
        psO = ctx.enter_context(nc.psum_tensor("psO", [P, 2, SEQ], F32))
        banks = [psS[:, 0, 0:SEQ], psS[:, 0, SEQ:], psS[:, 1, 0:SEQ], psS[:, 1, SEQ:],
                 psT[:, 0:SEQ], psT[:, SEQ:], psO[:, 0, :], psO[:, 1, :]]

        w_dram = nc.dram_tensor("w_dram", [P, HEADS, 3 * P], F32).ap()
        c_dram = nc.dram_tensor("c_dram", [HEADS, COLS], F32).ap()
        sc_dram = nc.dram_tensor("sc_dram", [NBLK, P, 2 * HEADS * NKEYS], F32).ap()
        gelu_dram = nc.dram_tensor("gelu_dram", [NKEYS, P, SEQ], F32).ap()
        gates_dram = nc.dram_tensor("gates_dram", [NKEYS, P, SEQ], F32).ap()

        cst_in, bias_in, x_in, keys_in = sem("cst_in"), sem("bias_in"), [sem(f"x_in{t}") for t in range(5)], sem("keys_in")
        landed = [sem(f"landed{r}") for r in range(RING)]
        hi_done, lo_done, slab_used = sem("hi_done"), sem("lo_done"), sem("slab_used")
        std_done, norm_done, turned, xT_done, hT_hi_done, hT_lo_done = (
            sem("std_done"), sem("norm_done"), sem("turned"), sem("xT_done"), sem("hT_hi_done"), sem("hT_lo_done"))
        evacuated = sem("evacuated")
        z_done, soft_done, c_done, c_out, ck_in, c_turned = (
            sem("z_done"), sem("soft_done"), sem("c_done"), sem("c_out"), sem("ck_in"), sem("c_turned"))
        w_mm, w_done, w_out_s, biasA_in = sem("w_mm"), sem("w_done"), sem("w_stored"), sem("biasA_in")
        v_turned, v_ready = sem("v_turned"), sem("v_ready")
        s_mm, nmax_done, exp_done, p_done, p_turned, pT_done, pM_done = (
            sem("s_mm"), sem("nmax_done"), sem("exp_done"), sem("p_done"), sem("p_turned"), sem("pT_done"), sem("pM_done"))
        pv_mm, o_hi_done, o_lo_done = sem("pv_mm"), sem("o_hi_done"), sem("o_lo_done")
        gate_done, mix_done, m_hi_done, m_lo_done = sem("gate_done"), sem("mix_done"), sem("m_hi_done"), sem("m_lo_done")
        r_done, mean_mm, xc_done, sq_done, var_mm, sd_done, h_done, scaled = (
            sem("r_done"), sem("mean_mm"), sem("xc_done"), sem("sq_done"), sem("var_mm"), sem("sd_done"), sem("h_done"), sem("scaled"))
        sk_hi_done, sk_done, pq_done, pq_hi_done, pq_lo_done, sc_mm, sc_done = (
            sem("sk_hi_done"), sem("sk_done"), sem("pq_done"), sem("pq_hi_done"), sem("pq_lo_done"), sem("sc_mm"), sem("sc_done"))
        gelu_done, top_done = sem("gelu_done"), sem("top_done")
        sc_out, now_in = [sem(f"sc_out{r}") for r in range(2)], [sem(f"now_in{r}") for r in range(2)]
        gelu_out = [sem(f"gelu_out{r}") for r in range(RING)]
        less_done, g_exp_done, g_done, idx_turned, gT_hi_done, idx_done = (
            sem("less_done"), sem("g_exp_done"), sem("g_done"), sem("idx_turned"), sem("gT_hi_done"), sem("idx_done"))
        iota_done = sem("iota_done")
        hot_done, G_mm, G_act, gates_out = sem("hot_done"), sem("G_mm"), sem("G_act"), [sem(f"gates_out{r}") for r in range(RANGES)]
        gel_in_s, gate_in_s = [sem(f"gel_in{r}") for r in range(RING)], [sem(f"gate_in{r}") for r in range(RING)]
        vhi_done, vlo_done, act_done, ahi_done, alo_done = (
            sem("vhi_done"), sem("vlo_done"), sem("act_done"), sem("ahi_done"), sem("alo_done"))
        v_mm, y_added = sem("v_mm"), sem("y_added")
        out_turned, tok_done, out_sent = sem("out_turned"), sem("tok_done"), [sem(f"out_sent{r}") for r in range(2)]
        act_step, dve_step = sem("act_step"), sem("dve_step")

        block = ctx.enter_context(nc.Block())

        def slab_source(n):
            if n < FIRST_MERGE:
                return w_proj[n]
            if n < FIRST_OUT:
                return w_merge[n - FIRST_MERGE]
            if n < FIRST_PQ:
                return w_out[n - FIRST_OUT]
            if n < FIRST_U:
                return w_pq[n - FIRST_PQ]
            return u_exp[n - FIRST_U]

        def landed_wait(eng, n, i=0, per=0):
            eng.wait_ge(landed[n % RING], 16 * (n // RING + 1) + i * (16 * per // RING))

        def load(sp, n, source, i=0, per=0):
            if n >= RING:
                sp.wait_ge(lo_done, n - RING + 1 + i * per)
            sp.dma_start(raw[:, n % RING, :], source).then_inc(landed[n % RING], 16)

        def split_hi(act, n, i=0, per=0):
            landed_wait(act, n, i, per)
            if n >= RING:
                act.wait_ge(slab_used, n - RING + 1 + i * per)
            nc.scalar.activation(hi[:, n % RING, :], raw[:, n % RING, :], ACT.Copy).then_inc(hi_done, 1)

        def split_lo(dve, n, i=0, per=0):
            dve.wait_ge(hi_done, n + 1 + i * per)
            nc.vector.tensor_tensor(lo[:, n % RING, :], raw[:, n % RING, :], hi[:, n % RING, :].bitcast(F32),
                                    ALU.subtract).then_inc(lo_done, 1)

        def split_product(out_ap, w_h, w_l, x_h, x_l, start, stop):
            nc.tensor.matmul(out_ap, w_h, x_l, start=start, stop=False)
            nc.tensor.matmul(out_ap, w_l, x_h, start=False, stop=False)
            return nc.tensor.matmul(out_ap, w_h, x_h, start=False, stop=stop)

        def slab_parts(slot, k):
            return hi[:, slot, k * P:(k + 1) * P], lo[:, slot, k * P:(k + 1) * P]

        AHEAD = 2

        def wait_at(eng, semaphore, first, per, i):
            if not isinstance(i, int) or first + per * i > 0:
                eng.wait_ge(semaphore, first + per * i)

        def exp_count(u):
            half = UNITS // 2
            return 2 * (u + 1) if u < half else 2 * half + (u + 1 - half)

        def meta_count(u):
            return sum(any(b is None for _, _, b in pieces_of(v)) for v in range(u + 1))

        @block.sync
        def _(sp):
            for t in range(NBLK):
                sp.dma_start(xin[:, t, :], x[t * P:(t + 1) * P, :]).then_inc(x_in[t], 16)
            sp.dma_start(xin[0:META, NBLK, :], meta).then_inc(x_in[NBLK], 16)
            sp.dma_start(cst[:, :], consts).then_inc(cst_in, 16)
            sp.dma_start(ncol[:, :], norm_cols).then_inc(cst_in, 16)
            sp.dma_start(bcol[:, :], b_cols).then_inc(cst_in, 16)
            for n in range(RING):
                load(sp, n, slab_source(n))
            sp.dma_start(relb[:, :], rel_bias).then_inc(bias_in, 16)
            sp.dma_start(buck[:, :], buckets).then_inc(bias_in, 16)
            sp.dma_start(wrow[:, 1, :], outside).then_inc(bias_in, 16)
            sp.dma_start(snk[:, 0, :], sinks.partition_broadcast(P)).then_inc(bias_in, 16)
            for n in range(RING, FIRST_U + RING):
                load(sp, n, slab_source(n))
            with sp.Fori(1, NGROUP) as i:
                for j in range(GROUP):
                    n = FIRST_U + j
                    load(sp, n, u_exp[i * GROUP + j], i, GROUP)
                    sp.wait_ge(gelu_done, i * GROUP + (j - GROUP + 1))
                    sp.dma_start(gelu_dram[i * GROUP + (j - GROUP)], gelu[:, j, :]).then_inc(gelu_out[j], 16)
            for j in range(GROUP):
                n = FIRST_V + j
                load(sp, n, v_exp[j])
                sp.wait_ge(gelu_done, NKEYS - GROUP + j + 1)
                sp.dma_start(gelu_dram[NKEYS - GROUP + j], gelu[:, j, :]).then_inc(gelu_out[j], 16)
            for j in range(RING):
                sp.wait_ge(gelu_out[j], 16 * NGROUP)
            sp.wait_ge(G_mm, BATCHES)
            sp.wait_ge(gates_out[0], 16 * NBLK)

            def load_tiles(b, j, i):
                wait_at(sp, act_done, j - RING + 1, RING, i)
                sp.dma_start(gel_in[:, j, :], gelu_dram[b]).then_inc(gel_in_s[j], 16)
                sp.dma_start(gate_in[:, j, :], gates_dram[b]).then_inc(gate_in_s[j], 16)

            def load_group(i):
                for j in range(GROUP):
                    sp.wait_ge(vlo_done, i * GROUP + (j - RING + 1))
                    sp.dma_start(raw[:, (FIRST_V + j) % RING, :],
                                 v_exp[i * GROUP + j]).then_inc(landed[(FIRST_V + j) % RING], 16)
                    load_tiles(i * GROUP + j, j, i)

            for j in range(RING):
                load_tiles(j, j, 0)
            load_group(1)
            for r in range(1, RANGES):
                sp.wait_ge(gates_out[r], 16 * NBLK)
            with sp.Fori(2, NGROUP) as i:
                load_group(i)
            for t in range(NBLK):
                sp.wait_ge(tok_done, t + 1)
                sp.dma_start(out[t * P:(t + 1) * P, :], tok[:, t % 2, :]).then_inc(out_sent[t % 2], 16)
            for r in range(2):
                sp.wait_ge(out_sent[r], 16 * NBLK // 2)

        @block.gpsimd
        def _(pool):
            pool.wait_ge(w_done, 1)
            pool.dma_start(w_dram.rearrange("q h m -> h q m"),
                           wrow[:, 0, :].unsqueeze(1).to_broadcast([HEADS, P, 3 * P])).then_inc(w_out_s, 16)
            pool.wait_ge(w_out_s, 16)
            skewed = bass.AP(w_dram.tensor, P - 1, [[3 * P * HEADS - 1, P], [3 * P, HEADS], [1, 2 * P]])
            pool.dma_start(biasA[:, :, :], skewed).then_inc(biasA_in, 16)
            pool.wait_ge(c_done, 1)
            pool.dma_start(c_dram, logf[:, 5, :]).then_inc(c_out, 16)
            pool.wait_ge(c_out, 16)
            pool.wait_ge(xT_done, KT)
            pool.dma_start(ckB[:, :, :].rearrange("p h c -> p (h c)"),
                           c_dram.rearrange("h c -> (h c)").partition_broadcast(P)).then_inc(ck_in, 16)
            pool.wait_ge(r_done, N_OUT)
            pool.dma_start(sk_raw[:, :, :], subkeys).then_inc(keys_in, 16)
            for q in range(N_PQ):
                pool.wait_ge(sc_done, q + 1)
                pool.dma_start(sc_dram[:, :, q * NKEYS:(q + 1) * NKEYS].rearrange("t p k -> p t k"),
                               sc[:, q % 2, :].rearrange("p (t k) -> p t k", t=NBLK)).then_inc(sc_out[q % 2], 16)
            for r in range(2):
                pool.wait_ge(sc_out[r], 16 * N_PQ // 2)

            def load_now(t, h, r):
                pool.dma_start(now[:, r, :, :].rearrange("p s k -> p (s k)"),
                               sc_dram[t][:, bass.ds(h * 2 * NKEYS, 2 * NKEYS)]).then_inc(now_in[r], 16)

            for t in range(NBLK):
                for r in range(2):
                    if t > 0:
                        pool.wait_ge(top_done, HEADS * t + r - 1)
                    load_now(t, r, r)
                with pool.Fori(1, HEADS // 2) as i:
                    for r in range(2):
                        pool.wait_ge(top_done, i * 2 + (HEADS * t + r - 1))
                        load_now(t, i * 2 + r, r)

        @block.scalar
        def _(act):
            own = Chain(act, act_step)
            act.wait_ge(norm_done, 1)
            nc.scalar.activation(rs[:, 0, :], mv[:, :, 1], ACT.Sqrt, bias=eps).then_inc(std_done, 1)
            for n in range(AHEAD):
                split_hi(act, n)
            for k in range(KT):
                act.wait_ge(xT_done, k + 1)
                nc.scalar.activation(hT_hi[:, k, :], xT[:, k % 2, :], ACT.Copy).then_inc(hT_hi_done, 1)
            for n in range(N_PROJ):
                split_hi(act, n + AHEAD)
                if n == 1:
                    act.wait_ge(z_done, 1)
                    own.link(nc.scalar.activation(logf[:, 1, :], logf[:, 0, :], ACT.Abs))
                    own.link(nc.scalar.activation(logf[:, 2, :], logf[:, 1, :], ACT.Exp, scale=-1.0))
                    nc.scalar.activation(logf[:, 3, :], logf[:, 2, :], ACT.Ln, bias=one[0:HEADS, :]).then_inc(soft_done, 1)
            for b in range(NBLK + 1):
                act.wait_ge(v_turned, b + 1)
                if b < NBLK:
                    nc.scalar.activation(vN[:, b, :], psS[:, b % 2, 0:640], ACT.Copy).then_inc(v_ready, 1)
                else:
                    nc.scalar.activation(vM[:, :], psT[0:META, 0:640], ACT.Copy).then_inc(v_ready, 1)

            for s in range(UNITS + 4):
                if s < UNITS:
                    window, n, h, tile, half = unit_of(s)
                    act.wait_ge(nmax_done, s + 1)
                    if s >= 2:
                        act.wait_ge(p_turned, s - 1)
                    if window:
                        nc.scalar.activation(sexp[:, s:s + 1], snk[:, 0, h:h + 1], ACT.Exp,
                                             bias=nmax[:, s:s + 1]).then_inc(exp_done, 1)
                    nc.scalar.activation(pexp[:, s % 2, 0:width_of(s)], psS[:, s % 2, 0:width_of(s)], ACT.Exp,
                                         bias=nmax[:, s:s + 1], accum_out=rsum[:, 0, s:s + 1]).then_inc(exp_done, 1)
                if 1 <= s <= UNITS:
                    u = s - 1
                    act.wait_ge(p_turned, u + 1)
                    if u >= 2:
                        act.wait_ge(pv_mm, u - 1)
                    cols = P * sum(b is not None for _, _, b in pieces_of(u))
                    nc.scalar.activation(pT[:, u % 2, 0:cols], psT[:, 0:cols], ACT.Copy).then_inc(pT_done, 1)
                if s >= 3 and (s - 3) % HEADS == HEADS - 1:
                    w = (s - 3) // HEADS
                    act.wait_ge(pv_mm, HEADS * (w + 1))
                    nc.scalar.activation(oT_hi[:, w // NBLK, :, (w % NBLK) * P:(w % NBLK + 1) * P],
                                         psO[:, w % 2, :].rearrange("p (t q) -> p t q", t=4),
                                         ACT.Copy).then_inc(o_hi_done, 1)

            for m in range(KT):
                for j in range(3):
                    n = FIRST_MERGE + 3 * m + j
                    split_hi(act, n + AHEAD)
                    if j < 2:
                        act.wait_ge(slab_used, n + 1)
                        if m >= 2:
                            act.wait_ge(mix_done, m - 1)
                        nc.scalar.activation(gate[:, m % 2, j, :], psS[:, m % 2, j * SEQ:(j + 1) * SEQ], ACT.Sigmoid,
                                             bias=bcol[:, N_PROJ + 8 * j + m:N_PROJ + 8 * j + m + 1]).then_inc(gate_done, 1)
                act.wait_ge(mix_done, m + 1)
                nc.scalar.activation(m_hi[:, m, :], mix[:, m % 2, 0, :], ACT.Copy).then_inc(m_hi_done, 1)
            for m in range(N_OUT):
                split_hi(act, FIRST_OUT + m + AHEAD)

            def norm_scalar(r):
                for k in range(KT):
                    act.wait_ge(xc_done, KT * r + k + 1)
                    if KT * r + k >= 2:
                        act.wait_ge(var_mm, KT * r + k - 1)
                    nc.scalar.activation(sq[:, k % 2, :], acc[:, k, :], ACT.Square).then_inc(sq_done, 1)
                act.wait_ge(var_mm, KT * (r + 1))
                nc.scalar.activation(nw[:, 0, :], banks[5], ACT.Sqrt, bias=eps).then_inc(sd_done, 1)

            norm_scalar(0)
            for k in range(KT):
                act.wait_ge(h_done, k + 1)
                nc.scalar.activation(hT_hi[:, k, 0:SEQ], acc[:, k, :], ACT.Copy).then_inc(hT_hi_done, 1)
            act.wait_ge(keys_in, 16)
            nc.scalar.activation(sk_hi[:, :, :], sk_raw[:, :, :], ACT.Copy).then_inc(sk_hi_done, 1)
            for q in range(N_PQ + 1):
                if q < N_PQ:
                    n = FIRST_PQ + q
                    split_hi(act, n + AHEAD)
                    act.wait_ge(slab_used, n + 1)
                    if q >= 2:
                        act.wait_ge(sc_mm, q - 1)
                    nc.scalar.activation(pq_hi[:, q % 2, :], psS[:, q % 2, 0:SEQ], ACT.Copy).then_inc(pq_hi_done, 1)
                if q >= 1:
                    act.wait_ge(sc_mm, q)
                    if q >= 3:
                        act.wait_ge(sc_out[(q - 1) % 2], 16 * ((q - 1) // 2))
                    nc.scalar.activation(sc[:, (q - 1) % 2, :], banks[4 + (q - 1) % 4], ACT.Copy).then_inc(sc_done, 1)

            def expert_step(j, i, block=None, before_gelu=None):
                n = FIRST_U + j + 1
                if not (isinstance(i, int) and GROUP * i + j + 1 + AHEAD >= NKEYS):
                    split_hi(act, n + AHEAD, i, GROUP)
                if before_gelu:
                    before_gelu()
                if not (isinstance(i, int) and GROUP * i + j + 1 >= NKEYS):
                    act.wait_ge(slab_used, n + 1 + i * GROUP)
                    wait_at(act, gelu_out[(j + 1) % RING], 16 * ((j + 1) // RING), 16, i)
                    nc.scalar.activation(gelu[:, (j + 1) % RING, :], banks[(j + 1) % RING], ACT.Gelu).then_inc(gelu_done, 1)
                if block is not None:
                    first = block * BGROUP + BGROUP // 2
                    act.wait_ge(G_mm, (i - first) * GROUP + (block * (P // CHUNK) + j + 1))
                    src = (psT[:, :], psO[:, :, :].rearrange("p o q -> p (o q)"))[j % 2]
                    nc.scalar.activation(gates[:, :, bass.ds((i - first) * (GROUP * CHUNK) + j * CHUNK, CHUNK)],
                                         src.rearrange("p (c b) -> p b c", c=CHUNK), ACT.Copy,
                                         scale=1.0 / GATE_SCALE).then_inc(G_act, 1)

            def gate_exp(t):
                act.wait_ge(less_done, t + 1)
                nc.scalar.activation(best[:, :], best[:, :], ACT.Exp).then_inc(g_exp_done, 1)

            split_hi(act, FIRST_U + AHEAD)
            act.wait_ge(slab_used, FIRST_U + 1)
            nc.scalar.activation(gelu[:, 0, :], banks[0], ACT.Gelu).then_inc(gelu_done, 1)
            for t in range(NBLK):
                start, mid, end = BGROUP * t, BGROUP * t + BGROUP // 2, BGROUP * (t + 1)
                if t == 0:
                    for j in range(GROUP):
                        expert_step(j, 0)
                with act.Fori(max(start, 1), mid - 1) as i:
                    for j in range(GROUP):
                        expert_step(j, i)
                for j in range(GROUP):
                    expert_step(j, mid - 1, before_gelu=(lambda: gate_exp(t)) if j == GROUP - 1 else None)
                act.wait_ge(idx_turned, t + 1)
                nc.scalar.activation(gT_hi[:, :], banks[5][:, 0:P], ACT.Copy, scale=GATE_SCALE).then_inc(gT_hi_done, 1)
                for r in range(RANGES):
                    if t == 0 and r < 2:
                        act.wait_ge(sc_out[r], 16 * N_PQ // 2)
                    if t > 0:
                        act.wait_ge(gates_out[r], 16 * t)
                with act.Fori(mid, end if t < NBLK - 1 else end - 1) as i:
                    for j in range(GROUP):
                        expert_step(j, i, t)
                if t == NBLK - 1:
                    for j in range(GROUP):
                        expert_step(j, end - 1, t)
                act.wait_ge(G_act, (t + 1) * (P // CHUNK))
                for r in range(RANGES):
                    bs = slice(r * NKEYS // RANGES, (r + 1) * NKEYS // RANGES)
                    act.dma_start(gates_dram[bs, :, t * P:(t + 1) * P].rearrange("b a c -> a b c"),
                                  gates[:, bs, :]).then_inc(gates_out[r], 16)

            def weigh(j, g, par):
                slot = par * GROUP + j
                dst = hi[:, slot, :] if slot < RING else hi_x[:, slot - RING, :]
                act.wait_ge(landed[(FIRST_V + j) % RING], 16 * ((FIRST_V + j) // RING + 1) + g * 16)
                wait_at(act, v_mm, -KT, KT, g)
                nc.scalar.activation(dst, raw[:, (FIRST_V + j) % RING, :], ACT.Copy).then_inc(vhi_done, 1)
                act.wait_ge(act_done, g * GROUP + (j + 1))
                nc.scalar.activation(hT_hi[:, slot, 0:SEQ], act_t[:, j, :], ACT.Copy).then_inc(ahi_done, 1)

            act.wait_ge(slab_used, FIRST_V)
            for j in range(GROUP):
                weigh(j, 0, 0)
            for r in range(2):
                act.wait_ge(gates_out[r], 16 * NBLK)
            for j in range(GROUP):
                weigh(j, 1, 1)
            with act.Fori(1, NGROUP // 2) as i:
                for par in range(2):
                    for j in range(GROUP):
                        weigh(j, i * 2 + par, par)
            norm_scalar(1)
            for t in range(NBLK):
                act.wait_ge(out_turned, t + 1)
                if t >= 2:
                    act.wait_ge(out_sent[t % 2], 16 * (t // 2))
                nc.scalar.activation(tok[:, t % 2, :], psS[:, t % 2, :], ACT.Copy).then_inc(tok_done, 1)

        @block.vector
        def _(dve):
            own = Chain(dve, dve_step)
            V = nc.vector

            def newton(y, var, t1):
                own.link(V.tensor_tensor(t1, y, y, ALU.mult))
                own.link(V.scalar_tensor_tensor(t1, var, EPS, t1, ALU.add, ALU.mult))
                own.link(V.tensor_scalar(t1, t1, -0.5, 1.5, ALU.mult, ALU.add))
                own.link(V.tensor_tensor(y, y, t1, ALU.mult))

            own.link(V.memset(mv[:, :, :], 1.0))
            for t in range(NBLK + 1):
                rows = P if t < NBLK else META
                dve.wait_ge(x_in[t], 16)
                for c in range(2):
                    own.mark(V.bn_stats(stats[0:rows, t, 6 * c:6 * c + 6], xin[0:rows, t, c * 512:(c + 1) * 512]))
                own.settle()
                own.mark(V.bn_aggr(mv[0:rows, t, :], stats[0:rows, t, :]))
            own.settle()
            own.link(V.tensor_copy(rs[:, 1, :], mv[:, :, 1]))
            dve.wait_ge(cst_in, 48)
            V.tensor_copy(rs[:, 2, :], mv[:, :, 0]).then_inc(norm_done, 1)
            dve.wait_ge(std_done, 1)
            own.link(V.reciprocal(rs[:, 3, :], rs[:, 0, :]))
            newton(rs[:, 3, :], rs[:, 1, :], rs[:, 2, :])
            for t in range(NBLK + 1):
                rows = P if t < NBLK else META
                V.tensor_scalar(xin[0:rows, t, :], xin[0:rows, t, :], mv[0:rows, t, 0:1], rs[0:rows, 3, t:t + 1],
                                ALU.subtract, ALU.mult).then_inc(norm_done, 1)
            for k in range(KT):
                dve.wait_ge(turned, k + 1)
                if k >= 2:
                    dve.wait_ge(hT_hi_done, k - 1)
                    dve.wait_ge(hT_lo_done, k - 1)
                V.tensor_scalar(xT[:, k % 2, :], psS[:, k % 2, 0:COLS], ncol[:, k:k + 1], ncol[:, KT + k:KT + k + 1],
                                ALU.mult, ALU.add).then_inc(xT_done, 1)
                dve.wait_ge(xT_done, k + 1)
                dve.wait_ge(hT_hi_done, k + 1)
                V.tensor_tensor(hT_lo[:, k, :], xT[:, k % 2, :], hT_hi[:, k, :].bitcast(F32),
                                ALU.subtract).then_inc(hT_lo_done, 1)
                if k < AHEAD:
                    split_lo(dve, k)
            dve.wait_ge(bias_in, 64)
            dve.wait_ge(w_mm, 1)
            V.tensor_tensor(wrow[:, 0, :], psO[0:HEADS, 0, 0:3 * P], wrow[:, 1, :], ALU.add).then_inc(w_done, 1)
            own.link(V.tensor_scalar(snk[:, 1, :], snk[:, 0, :], -1.0, None, ALU.mult))

            for n in range(N_PROJ):
                split_lo(dve, n + AHEAD)
                dve.wait_ge(slab_used, n + 1)
                bias = bcol[:, n:n + 1]
                ps = psS[:, n % 2, 0:COLS]
                if n == 0:
                    V.tensor_scalar(logf[:, 0, :], ps[0:HEADS, :], bias[0:HEADS, :], None, ALU.add).then_inc(z_done, 1)
                    dve.wait_ge(z_done, 1)
                    V.tensor_scalar(logf[:, 4, :], logf[:, 0, :], 0.0, None, ALU.min).then_inc(evacuated, 1)
                    continue
                if 1 <= n <= 4 or 7 <= n <= 10:
                    dst = (qaT[:, n - 1, :] if n <= 4 else qbT[:, n - 7, :])
                    V.tensor_scalar(dst, ps[:, 0:SEQ], bias, HD ** -0.5, ALU.add, ALU.mult).then_inc(evacuated, 1)
                else:
                    dst = kaT[:, :] if n == 5 else vT[:, 0, :] if n == 6 else (
                        kbT[:, n - 11, :] if n <= 14 else vT[:, n - 14, :])
                    V.tensor_scalar(dst, ps, bias, None, ALU.add).then_inc(evacuated, 1)
                if n == 3:
                    dve.wait_ge(soft_done, 1)
                    own.mark(V.memset(logf[:, 1, :], 1.0))
                    own.link(V.tensor_tensor(logf[:, 4, :], logf[:, 4, :], logf[:, 3, :], ALU.subtract))
                    own.link(V.tensor_tensor_scan(logf[:, 5, SEQ:COLS], logf[:, 1, SEQ:COLS], logf[:, 4, SEQ:COLS],
                                                  0.0, ALU.mult, ALU.add))
                    V.tensor_tensor_scan(logf[:, 5, 0:SEQ], logf[:, 1, 0:SEQ], logf[:, 4, 0:SEQ],
                                         logf[:, 5, COLS - 1:COLS], ALU.mult, ALU.add).then_inc(c_done, 1)
                if n == 8:
                    dve.wait_ge(c_turned, 1)
                    own.link(V.tensor_copy(cq[:, :, :].rearrange("p n h -> p (n h)"), psO[:, 1, 0:NBLK * HEADS]))

            dve.wait_ge(biasA_in, 16)
            dve.wait_ge(ck_in, 16)
            for s in range(UNITS + 4):
                if s < UNITS:
                    window, n, h, tile, half = unit_of(s)
                    L = width_of(s)
                    S = psS[:, s % 2, 0:L]
                    dve.wait_ge(s_mm, s + 1)
                    if window:
                        own.link(V.tensor_tensor(S, S, biasA[:, h, 2 * P - L:2 * P], ALU.add))
                        own.link(V.tensor_reduce(nmax[:, s:s + 1], S, AX.X, ALU.max, negate=True))
                        V.tensor_tensor(nmax[:, s:s + 1], nmax[:, s:s + 1], snk[:, 1, h:h + 1],
                                        ALU.min).then_inc(nmax_done, 1)
                    else:
                        T = P * (n + 1)
                        own.mark(V.scalar_tensor_tensor(S[:, 0:T], S[:, 0:T], cq[:, n, h:h + 1], ckB[:, h, 0:T],
                                                        ALU.add, ALU.subtract))
                        own.link(V.scalar_tensor_tensor(S[:, T:L], S[:, T:L], cq[:, n, h:h + 1], ckB[:, h, SEQ:COLS],
                                                        ALU.add, ALU.subtract))
                        own.link(V.tensor_tensor(S[:, T - P:T], S[:, T - P:T], mask, ALU.add))
                        V.tensor_reduce(nmax[:, s:s + 1], S, AX.X, ALU.max, negate=True).then_inc(nmax_done, 1)
                if 2 <= s <= UNITS + 1 and pieces_of(s - 2)[0 if unit_of(s - 2)[0] else -1][2] is None:
                    u = s - 2
                    dve.wait_ge(p_turned, u + 1)
                    if u >= 2:
                        dve.wait_ge(pv_mm, u - 1)
                    V.tensor_copy(pM[:, u % 2, :], psT[0:META, SEQ:SEQ + P]).then_inc(pM_done, 1)
                if 1 <= s <= UNITS:
                    u = s - 1
                    window = unit_of(u)[0]
                    dve.wait_ge(exp_done, exp_count(u))
                    r0, r1 = rsum[:, 0, u:u + 1], rsum[:, 1, u:u + 1]
                    if window:
                        own.link(V.tensor_tensor(r0, r0, sexp[:, u:u + 1], ALU.add))
                    own.link(V.reciprocal(r1, r0))
                    Pu = pexp[:, u % 2, 0:width_of(u)]
                    V.tensor_scalar(Pu, Pu, r1, None, ALU.mult).then_inc(p_done, 1)
                if s >= 3 and (s - 3) % HEADS == HEADS - 1:
                    w = (s - 3) // HEADS
                    dve.wait_ge(o_hi_done, w + 1)
                    cols = slice((w % NBLK) * P, (w % NBLK + 1) * P)
                    V.tensor_tensor(oT_lo[:, w // NBLK, :, cols], psO[:, w % 2, :].rearrange("p (t q) -> p t q", t=4),
                                    oT_hi[:, w // NBLK, :, cols].bitcast(F32), ALU.subtract).then_inc(o_lo_done, 1)

            for m in range(KT):
                for j in range(3):
                    split_lo(dve, FIRST_MERGE + 3 * m + j + AHEAD)
                dve.wait_ge(slab_used, FIRST_MERGE + 3 * m + 3)
                dve.wait_ge(gate_done, 2 * m + 2)
                if m >= 2:
                    dve.wait_ge(m_hi_done, m - 1)
                for j in range(2):
                    own.mark(V.tensor_tensor(mix[:, m % 2, j, :], banks[4 + 2 * (m % 2) + j], gate[:, m % 2, j, :], ALU.mult))
                own.settle()
                V.tensor_tensor(mix[:, m % 2, 0, :], mix[:, m % 2, 0, :], mix[:, m % 2, 1, :], ALU.add).then_inc(mix_done, 1)
                dve.wait_ge(m_hi_done, m + 1)
                V.tensor_tensor(m_lo[:, m, :], mix[:, m % 2, 0, :], m_hi[:, m, :].bitcast(F32),
                                ALU.subtract).then_inc(m_lo_done, 1)
            for m in range(KT):
                split_lo(dve, FIRST_OUT + m + AHEAD)
                own.link(V.tensor_tensor(acc[:, m, :], hT_hi[:, m, 0:SEQ].bitcast(F32), hT_lo[:, m, 0:SEQ].bitcast(F32),
                                         ALU.add))
                dve.wait_ge(slab_used, FIRST_OUT + m + 1)
                V.scalar_tensor_tensor(acc[:, m, :], acc[:, m, :], ALPHA, psS[:, m % 2, 0:SEQ],
                                       ALU.mult, ALU.add).then_inc(r_done, 1)

            def norm_vector(r):
                dve.wait_ge(mean_mm, r + 1)
                for k in range(KT):
                    V.tensor_tensor(acc[:, k, :], acc[:, k, :], banks[4], ALU.subtract).then_inc(xc_done, 1)
                dve.wait_ge(sd_done, r + 1)
                own.link(V.reciprocal(rinv[:, :], nw[:, 0, :]))
                newton(rinv[:, :], banks[5], nw[:, 1, :])
                for k in range(KT):
                    own.mark(V.tensor_tensor(acc[:, k, :], acc[:, k, :], rinv[:, :], ALU.mult))
                own.settle()
                g = 2 * KT * (r + 1)
                for k in range(KT):
                    V.tensor_scalar(acc[:, k, :], acc[:, k, :], ncol[:, g + k:g + k + 1],
                                    ncol[:, g + KT + k:g + KT + k + 1], ALU.mult, ALU.add).then_inc(h_done, 1)

            norm_vector(0)
            for k in range(KT):
                dve.wait_ge(hT_hi_done, KT + k + 1)
                V.tensor_tensor(hT_lo[:, k, 0:SEQ], acc[:, k, :], hT_hi[:, k, 0:SEQ].bitcast(F32),
                                ALU.subtract).then_inc(hT_lo_done, 1)
                dve.wait_ge(hT_lo_done, KT + k + 1)
                V.tensor_scalar(acc[:, k, :], acc[:, k, :], ALPHA, None, ALU.mult).then_inc(scaled, 1)
            dve.wait_ge(sk_hi_done, 1)
            V.tensor_tensor(sk_lo[:, :, :], sk_raw[:, :, :], sk_hi[:, :, :].bitcast(F32), ALU.subtract).then_inc(sk_done, 1)
            for q in range(N_PQ):
                split_lo(dve, FIRST_PQ + q + AHEAD)
                dve.wait_ge(pq_hi_done, q + 1)
                if q >= 2:
                    dve.wait_ge(sc_mm, q - 1)
                V.tensor_tensor(pq_lo[:, q % 2, :], psS[:, q % 2, 0:SEQ], pq_hi[:, q % 2, :].bitcast(F32),
                                ALU.subtract).then_inc(pq_lo_done, 1)

            def top_half(part, r, unit, loads):
                cols = bass.ds(unit * TOPK, TOPK)
                if part == 0:
                    dve.wait_ge(now_in[r], 16 * loads)
                    V.memset(spare[:, :], 0.0)
                    for p in range(2):
                        own.mark(V.max(topv[:, p, 0:8], now[:, r, p, :]))
                    own.settle_apart(V.memset, spare[:, :])
                    for p in range(2):
                        own.mark(V.max_index(topi[:, p, 0:8], topv[:, p, 0:8], now[:, r, p, :]))
                        own.mark(V.match_replace(rest[:, p * NKEYS:(p + 1) * NKEYS], topv[:, p, 0:8], now[:, r, p, :], LOWEST))
                    own.settle_apart(V.memset, spare[:, :])
                    for p in range(2):
                        own.mark(V.max(topv[:, p, 8:16], rest[:, p * NKEYS:(p + 1) * NKEYS]))
                    own.settle_apart(V.memset, spare[:, :])
                    for p in range(2):
                        own.mark(V.max_index(topi[:, p, 8:16], topv[:, p, 8:16], rest[:, p * NKEYS:(p + 1) * NKEYS]))
                    own.link(V.tensor_tensor(cand[:, :].rearrange("p (a b) -> p a b", a=TOPK),
                                             topv[:, 0, :].unsqueeze(2).to_broadcast([P, TOPK, TOPK]),
                                             topv[:, 1, :].unsqueeze(1).to_broadcast([P, TOPK, TOPK]), ALU.add))
                    own.mark(V.tensor_copy(topf[:, :, :], topi[:, :, :]))
                    own.mark(V.max(topv[:, 0, 0:8], cand[:, :]))
                if part == 1:
                    own.settle_apart(V.memset, spare[:, :])
                    own.mark(V.max_index(flat[:, 0:8], topv[:, 0, 0:8], cand[:, :]))
                    own.mark(V.match_replace(rest[:, :], topv[:, 0, 0:8], cand[:, :], LOWEST))
                    own.settle_apart(V.memset, spare[:, :])
                    own.mark(V.max(topv[:, 0, 8:16], rest[:, :]))
                    own.settle_apart(V.memset, spare[:, :])
                    own.mark(V.max_index(flat[:, 8:16], topv[:, 0, 8:16], rest[:, :]))
                    own.link(V.tensor_copy(best[:, cols], topv[:, 0, :]))
                    own.mark(V.tensor_single_scalar(pos[:, 0, :], flat[:, :], 4, ALU.logical_shift_right))
                    own.link(V.tensor_single_scalar(pos[:, 1, :], flat[:, :], TOPK - 1, ALU.bitwise_and))
                    own.link(V.tensor_copy(posf[:, :, :], pos[:, :, :]))
                    view = eq[:, :, :].rearrange("p s (k j) -> p s k j", k=TOPK)
                    for p in range(2):
                        own.mark(V.tensor_tensor(view[:, p], posf[:, p, :].unsqueeze(2).to_broadcast([P, TOPK, TOPK]),
                                                 iota16.unsqueeze(1).to_broadcast([P, TOPK, TOPK]), ALU.is_equal))
                    own.settle()
                    for p in range(2):
                        own.mark(V.tensor_tensor(view[:, p], view[:, p],
                                                 topf[:, p, :].unsqueeze(1).to_broadcast([P, TOPK, TOPK]), ALU.mult))
                    own.settle()
                    own.mark(V.tensor_reduce(ia[:, cols], view[:, 0], AX.X, ALU.add))
                    own.settle()
                    V.tensor_reduce(ib[:, cols], view[:, 1], AX.X, ALU.add).then_inc(top_done, 1)

            def hot(q, toks, r):
                wait_at(dve, G_mm, -1, 1, q)

                def spread(v):
                    return v[:, toks].unsqueeze(1).to_broadcast([P, NKEYS, CHUNK])

                own.mark(V.tensor_tensor(hotA[:, r], spread(iaT), iota_h[:, :, :], ALU.is_equal))
                own.link(V.tensor_tensor(hotB[:, :, :], spread(ibT), iota_h[:, :, :], ALU.is_equal))
                own.mark(V.tensor_tensor(hotG_hi[:, r], hotB[:, :, :], spread(gT_hi), ALU.mult))
                V.tensor_tensor(hotG_lo[:, r], hotB[:, :, :], spread(gT_lo), ALU.mult).then_inc(hot_done, 1)
                dve.wait_ge(hot_done, q + 1)

            def top_group(i, t):
                for j in range(GROUP):
                    split_lo(dve, FIRST_U + j + AHEAD, i, GROUP)
                    k = i - t * BGROUP
                    top_half(j % 2, j // 2, k * 2 + j // 2, k + (t * HEADS // 2 + 1))

            def hot_group(i, t):
                k = i - (t * BGROUP + BGROUP // 2)
                for j in range(GROUP):
                    if not (isinstance(i, int) and GROUP * i + j + AHEAD >= NKEYS):
                        split_lo(dve, FIRST_U + j + AHEAD, i, GROUP)
                    hot(k * GROUP + (t * (P // CHUNK) + j), bass.ds(k * (GROUP * CHUNK) + j * CHUNK, CHUNK), j % 2)

            for c in range(CHUNK):
                own.mark(V.tensor_copy(iota_h[:, :, c], cst[:, C_IOTA:C_IOTA + P]))
            own.settle()
            for t in range(NBLK):
                start, mid, end = BGROUP * t, BGROUP * t + BGROUP // 2, BGROUP * (t + 1)
                if t == 0:
                    top_group(0, 0)
                    start = 1
                with dve.Fori(start, mid) as i:
                    own.loop(i - start, TOP_MARKS)
                    top_group(i, t)
                    own.end(mid - start)

                dve.wait_ge(top_done, HEADS * (t + 1))
                b3 = best[:, :].rearrange("p (u k) -> p u k", k=TOPK)
                own.link(V.tensor_reduce(gsum[:, 2, :], b3, AX.X, ALU.max))
                V.tensor_tensor(b3, b3, gsum[:, 2, :].unsqueeze(2).to_broadcast([P, HEADS, TOPK]),
                                ALU.subtract).then_inc(less_done, 1)
                dve.wait_ge(g_exp_done, t + 1)
                own.link(V.tensor_reduce(gsum[:, 0, :], b3, AX.X, ALU.add))
                own.link(V.reciprocal(gsum[:, 1, :], gsum[:, 0, :]))
                V.tensor_tensor(b3, b3, gsum[:, 1, :].unsqueeze(2).to_broadcast([P, HEADS, TOPK]),
                                ALU.mult).then_inc(g_done, 1)
                dve.wait_ge(idx_turned, t + 1)
                own.mark(V.tensor_copy(iaT[:, :], banks[4][:, 0:P]))
                own.mark(V.tensor_copy(ibT[:, :], banks[4][:, P:2 * P]))
                dve.wait_ge(gT_hi_done, t + 1)
                own.link(V.scalar_tensor_tensor(gT_lo[:, :], banks[5][:, 0:P], GATE_SCALE, gT_hi[:, :],
                                                ALU.mult, ALU.subtract))
                if t == NBLK - 1:
                    end -= 1
                if t == 0:
                    hot_group(mid, 0)
                    mid += 1
                with dve.Fori(mid, end) as i:
                    own.loop(i - mid, HOT_MARKS)
                    hot_group(i, t)
                    own.end(end - mid)
            hot_group(NGROUP - 1, NBLK - 1)

            def weigh(j, g, par, part):
                slot = par * GROUP + j
                src = hi[:, slot, :] if slot < RING else hi_x[:, slot - RING, :]
                dst = lo[:, slot, :] if slot < RING else lo_x[:, slot - RING, :]
                if part == 0:
                    dve.wait_ge(gel_in_s[j], 16 + g * 16)
                    dve.wait_ge(gate_in_s[j], 16 + g * 16)
                    wait_at(dve, ahi_done, j - RING + 1, RING, g)
                    wait_at(dve, alo_done, j - RING + 1, RING, g)
                    V.tensor_tensor(act_t[:, j, :], gel_in[:, j, :], gate_in[:, j, :], ALU.mult).then_inc(act_done, 1)
                    dve.wait_ge(vhi_done, g * GROUP + (j + 1))
                    V.tensor_tensor(dst, raw[:, (FIRST_V + j) % RING, :], src.bitcast(F32), ALU.subtract).then_inc(vlo_done, 1)
                else:
                    dve.wait_ge(ahi_done, g * GROUP + (j + 1))
                    V.tensor_tensor(hT_lo[:, slot, 0:SEQ], act_t[:, j, :], hT_hi[:, slot, 0:SEQ].bitcast(F32),
                                    ALU.subtract).then_inc(alo_done, 1)

            def group(g, par, last=False):
                for m in range(KT):
                    if not last:
                        weigh(m // 2, g + 1, 1 - par, m % 2)
                    dve.wait_ge(v_mm, g * KT + (m + 1))
                    V.tensor_tensor(acc[:, m, :], acc[:, m, :], banks[4 + m % 4], ALU.add).then_inc(y_added, 1)

            for j in range(GROUP):
                weigh(j, 0, 0, 0)
                weigh(j, 0, 0, 1)
            with dve.Fori(0, NGROUP // 2 - 1) as i:
                for par in range(2):
                    group(i * 2 + par, par)
            group(NGROUP - 2, 0)
            group(NGROUP - 1, 1, last=True)
            dve.wait_ge(y_added, NGROUP * KT)
            norm_vector(1)

        @block.tensor
        def _(pe):
            mm, turn = nc.tensor.matmul, nc.tensor.transpose

            def slab(n, slot, out_ap, x_h, x_l, ks, i=0, per=0):
                for a, (k, kx) in enumerate(ks):
                    wh, wl = slab_parts(slot, k)
                    last = split_product(out_ap, wh, wl, x_h(kx), x_l(kx), a == 0, a == len(ks) - 1)
                return last

            def tokens(k):
                return hT_hi[:, k, 0:SEQ]

            def tokens_lo(k):
                return hT_lo[:, k, 0:SEQ]

            all_k = [(k, k) for k in range(KT)]
            pe.wait_ge(cst_in, 48)
            pe.wait_ge(norm_done, NBLK + 2)
            for k in range(KT):
                if k >= 2:
                    pe.wait_ge(xT_done, k - 1)
                for t in range(NBLK):
                    turn(psS[:, k % 2, t * P:(t + 1) * P], xin[:, t, k * P:(k + 1) * P], ident)
                turn(psS[:, k % 2, SEQ:COLS], xin[0:META, NBLK, k * P:(k + 1) * P],
                     ident[0:META, 0:META]).then_inc(turned, 1)
            pe.wait_ge(bias_in, 64)
            mm(psO[0:HEADS, 0, 0:3 * P], relb[:, :], buck[:, :], start=True, stop=True).then_inc(w_mm, 1)
            pe.wait_ge(hT_lo_done, KT)
            for n in range(N_PROJ):
                pe.wait_ge(lo_done, n + 1)
                if n >= 2:
                    pe.wait_ge(evacuated, n - 1)
                last = slab(n, n % RING, psS[:, n % 2, 0:SEQ], tokens, tokens_lo, all_k)
                if not (1 <= n <= 4 or 7 <= n <= 10):
                    last = slab(n, n % RING, psS[:, n % 2, SEQ:COLS], lambda k: hT_hi[:, k, SEQ:COLS],
                                lambda k: hT_lo[:, k, SEQ:COLS], all_k)
                last.then_inc(slab_used, 1)
                if n == 6:
                    pe.wait_ge(c_done, 1)
                    for b in range(NBLK):
                        last = turn(psO[:, 1, b * HEADS:(b + 1) * HEADS], logf[:, 5, b * P:(b + 1) * P],
                                    ident[0:HEADS, 0:HEADS])
                    last.then_inc(c_turned, 1)
            pe.wait_ge(evacuated, N_PROJ)
            for b in range(NBLK + 1):
                if 2 <= b < NBLK:
                    pe.wait_ge(v_ready, b - 1)
                for f in range(5):
                    if b < NBLK:
                        last = turn(psS[:, b % 2, f * P:(f + 1) * P], vT[:, f, b * P:(b + 1) * P], ident)
                    else:
                        last = turn(psT[0:META, f * P:(f + 1) * P], vT[:, f, SEQ:COLS], ident)
                last.then_inc(v_turned, 1)
            pe.wait_ge(v_ready, NBLK + 1)

            def key_cols(block_no):
                return slice(SEQ, COLS) if block_no is None else slice(block_no * P, (block_no + 1) * P)

            for s in range(-1, UNITS + 2):
                if s + 1 < UNITS:
                    u = s + 1
                    window, n, h, tile, half = unit_of(u)
                    rows = slice(HD * half, HD * half + HD)
                    if u >= 2:
                        pe.wait_ge(exp_done, exp_count(u - 2))
                    q = (qaT if window else qbT)[rows, tile, n * P:(n + 1) * P]
                    for c, width, b in pieces_of(u):
                        k = kaT[rows, key_cols(b)] if window else kbT[rows, tile, key_cols(b)]
                        last = mm(psS[:, u % 2, c:c + width], q, k, start=True, stop=True)
                    last.then_inc(s_mm, 1)
                if 1 <= s <= UNITS:
                    u = s - 1
                    pe.wait_ge(p_done, u + 1)
                    if u >= 1:
                        pe.wait_ge(pT_done, u)
                        pe.wait_ge(pM_done, max(1, meta_count(u - 1)))
                    at = 0
                    for c, width, b in pieces_of(u):
                        src = pexp[:, u % 2, c:c + width]
                        if b is None:
                            last = turn(psT[0:META, SEQ:SEQ + P], src, ident)
                        else:
                            last = turn(psT[:, at:at + P], src, ident)
                            at += P
                    last.then_inc(p_turned, 1)
                if s >= 2:
                    u = s - 2
                    window, n, h, tile, half = unit_of(u)
                    w = u // HEADS
                    pe.wait_ge(pT_done, u + 1)
                    pe.wait_ge(pM_done, max(1, meta_count(u)))
                    if w >= 2 and h == 0:
                        pe.wait_ge(o_hi_done, w - 1)
                        pe.wait_ge(o_lo_done, w - 1)
                    f = half * HD if window else P + h * HD
                    dst = psO[HD * half:HD * half + HD, w % 2, tile * P:(tile + 1) * P]
                    pieces = pieces_of(u)
                    at = 0
                    for a, (_, _, b) in enumerate(pieces):
                        ends = dict(start=a == 0, stop=a == len(pieces) - 1)
                        if b is None:
                            last = mm(dst, vM[:, f:f + HD], pM[:, u % 2, :], **ends)
                        else:
                            last = mm(dst, vN[:, b, f:f + HD], pT[:, u % 2, at:at + P], **ends)
                            at += P
                    last.then_inc(pv_mm, 1)

            pe.wait_ge(o_lo_done, 2 * NBLK)
            for m in range(KT):
                for j in range(3):
                    n = FIRST_MERGE + 3 * m + j
                    pe.wait_ge(lo_done, n + 1)
                    if j < 2:
                        if m >= 2:
                            pe.wait_ge(gate_done, 2 * (m - 2) + j + 1)
                        last = slab(n, n % RING, psS[:, m % 2, j * SEQ:(j + 1) * SEQ], tokens, tokens_lo, all_k)
                    else:
                        if m >= 2:
                            pe.wait_ge(mix_done, m - 1)
                        for e in range(2):
                            last = slab(n, n % RING, banks[4 + 2 * (m % 2) + e], lambda k: oT_hi[:, e, k, :],
                                        lambda k: oT_lo[:, e, k, :], [(4 * e + k, k) for k in range(4)])
                    last.then_inc(slab_used, 1)
            pe.wait_ge(gate_done, 2 * KT)
            for m in range(N_OUT):
                n = FIRST_OUT + m
                pe.wait_ge(lo_done, n + 1)
                pe.wait_ge(m_lo_done, KT)
                if m >= 2:
                    pe.wait_ge(r_done, m - 1)
                slab(n, n % RING, psS[:, m % 2, 0:SEQ], lambda k: m_hi[:, k, :], lambda k: m_lo[:, k, :],
                     all_k).then_inc(slab_used, 1)

            def norm_tensor(r):
                for k in range(KT):
                    last = mm(banks[4], mean_of, acc[:, k, :], start=k == 0, stop=k == KT - 1)
                last.then_inc(mean_mm, 1)
                for k in range(KT):
                    pe.wait_ge(sq_done, KT * r + k + 1)
                    mm(banks[5], mean_of, sq[:, k % 2, :], start=k == 0, stop=k == KT - 1).then_inc(var_mm, 1)

            pe.wait_ge(r_done, N_OUT)
            norm_tensor(0)
            pe.wait_ge(hT_lo_done, 2 * KT)
            pe.wait_ge(sk_done, 1)
            for q in range(N_PQ + 1):
                if q < N_PQ:
                    n = FIRST_PQ + q
                    pe.wait_ge(lo_done, n + 1)
                    if q >= 2:
                        pe.wait_ge(pq_lo_done, q - 1)
                    slab(n, n % RING, psS[:, q % 2, 0:SEQ], tokens, tokens_lo, all_k).then_inc(slab_used, 1)
                if q >= 1:
                    c = q - 1
                    pe.wait_ge(pq_lo_done, c + 1)
                    if c >= 4:
                        pe.wait_ge(sc_done, c - 3)
                    for t in range(NBLK):
                        toks = slice(t * P, (t + 1) * P)
                        last = split_product(banks[4 + c % 4][:, toks], pq_hi[:, c % 2, toks], pq_lo[:, c % 2, toks],
                                             sk_hi[:, c, :], sk_lo[:, c, :], True, True)
                    last.then_inc(sc_mm, 1)

            def expert_slab(n, i):
                pe.wait_ge(lo_done, FIRST_U + n + 1 + i * GROUP)
                wait_at(pe, gelu_done, n - GROUP + 1, GROUP, i)
                slab(FIRST_U + n, (FIRST_U + n) % RING, banks[n % GROUP], tokens, tokens_lo, all_k).then_inc(slab_used, 1)

            def gate_matrices(q, r):
                pe.wait_ge(hot_done, q + 1)
                wait_at(pe, G_act, -1, 1, q)
                for c in range(CHUNK):
                    dst = banks[4 + 2 * r + c // 4][:, (c % 4) * P:(c % 4 + 1) * P]
                    mm(dst, hotA[:, r, :, c], hotG_hi[:, r, :, c], start=True, stop=False)
                    last = mm(dst, hotA[:, r, :, c], hotG_lo[:, r, :, c], start=False, stop=True)
                last.then_inc(G_mm, 1)

            def expert_group(i, t=None):
                for j in range(GROUP):
                    if not (isinstance(i, int) and GROUP * i + j + 1 >= NKEYS):
                        expert_slab(j + 1, i)
                    if t is not None:
                        k = i - (t * BGROUP + BGROUP // 2)
                        gate_matrices(k * GROUP + (t * (P // CHUNK) + j), j % 2)

            pe.wait_ge(pq_lo_done, N_PQ)
            pe.wait_ge(sc_done, N_PQ)
            expert_slab(0, 0)
            for t in range(NBLK):
                start, mid, end = BGROUP * t, BGROUP * t + BGROUP // 2, BGROUP * (t + 1)
                if t == 0:
                    expert_group(0)
                    start = 1
                with pe.Fori(start, mid) as i:
                    expert_group(i)
                pe.wait_ge(g_done, t + 1)
                if t > 0:
                    pe.wait_ge(G_act, t * (P // CHUNK))
                turn(banks[4][:, 0:P], ia[:, :], ident)
                turn(banks[4][:, P:2 * P], ib[:, :], ident)
                last = turn(banks[5][:, 0:P], best[:, :], ident)
                last.then_inc(idx_turned, 1)
                if t == 0:
                    expert_group(mid, 0)
                    mid += 1
                if t == NBLK - 1:
                    end -= 1
                with pe.Fori(mid, end) as i:
                    expert_group(i, t)
            expert_group(NGROUP - 1, NBLK - 1)

            def group(g, par):
                pe.wait_ge(vlo_done, (g + 1) * GROUP)
                pe.wait_ge(alo_done, (g + 1) * GROUP)
                for m in range(KT):
                    wait_at(pe, y_added, m - 3, KT, g)
                    for j in range(GROUP):
                        slot = par * GROUP + j
                        wh, wl = (hi, lo) if slot < RING else (hi_x, lo_x)
                        cols = slice(m * P, (m + 1) * P)
                        last = split_product(banks[4 + m % 4], wh[:, slot % RING, cols], wl[:, slot % RING, cols],
                                             hT_hi[:, slot, 0:SEQ], hT_lo[:, slot, 0:SEQ], j == 0, j == GROUP - 1)
                    last.then_inc(v_mm, 1)

            pe.wait_ge(G_act, BATCHES)
            for g in range(2):
                group(g, g)
            with pe.Fori(1, NGROUP // 2) as i:
                for par in range(2):
                    group(i * 2 + par, par)
            pe.wait_ge(y_added, NGROUP * KT)
            norm_tensor(1)
            pe.wait_ge(h_done, 2 * KT)
            for t in range(NBLK):
                if t >= 2:
                    pe.wait_ge(tok_done, t - 1)
                for k in range(KT):
                    last = turn(psS[:, t % 2, k * P:(k + 1) * P], acc[:, k, t * P:(t + 1) * P], ident)
                last.then_inc(out_turned, 1)


def constants():
    c = np.zeros((P, C_COLS), np.float32)
    c[:, C_ID:C_ID + P] = np.eye(P)
    c[:, C_MASK:C_MASK + P] = np.where(np.arange(P)[None, :] > np.arange(P)[:, None], NEG, 0.0)
    c[:, C_MEAN:C_MEAN + P] = 1.0 / D
    c[:, C_IOTA:C_IOTA + P] = np.arange(P)
    c[:, C_IOTA16:C_IOTA16 + TOPK] = np.arange(TOPK)
    c[:, C_EPS] = EPS
    c[:, C_ONE] = 1.0
    dist = 2 * P - 1 - np.arange(3 * P)
    inside = (dist >= 0) & (dist < P)
    d = np.clip(dist, 1, P - 1).astype(np.float32)
    exact = BUCKETS // 2
    large = exact + (np.log(d / exact) / np.log(P / exact) * (BUCKETS - exact)).astype(np.int32)
    bucket = np.where(dist < exact, np.clip(dist, 0, P), np.minimum(large, BUCKETS - 1))
    hot = ((np.arange(BUCKETS)[:, None] == bucket[None, :]) & inside[None, :]).astype(np.float32)
    outside = np.repeat(np.where(inside, 0.0, NEG)[None, :], HEADS, axis=0).astype(np.float32)
    return c, hot, outside


def tiles(w):
    k, f = w.shape
    return w.reshape(k // P, P, f // P, P).transpose(2, 1, 0, 3)


def kernel(x, meta_tokens, emb_ln_g, emb_ln_b, rel_bias, w_in, b_in, attn_sinks, w_pa, w_pb, w_o,
           ln1_g, ln1_b, peer_wq, peer_subkeys, peer_u, peer_v, ln2_g, ln2_b):
    import concourse.bacc as bacc
    from concourse.bass_utils import run_bass_kernel_spmd

    a = {k: np.asarray(v) for k, v in dict(
        x=x, meta=meta_tokens, eg=emb_ln_g, eb=emb_ln_b, rel=rel_bias, w_in=w_in, b_in=b_in, sinks=attn_sinks, w_pa=w_pa,
        w_pb=w_pb, w_o=w_o, g1=ln1_g, b1=ln1_b, wq=peer_wq, sk=peer_subkeys, u=peer_u, v=peer_v, g2=ln2_g,
        b2=ln2_b).items()}
    order = [h + 4 * s for h in range(4) for s in range(2)]
    qa, ka, va, qb, kb, vb = 0, 512, 640, 768, 1280, 1792
    fb = vb + 512
    ga = fb + HEADS
    gb = ga + D
    win = a["w_in"][0]
    pick = np.concatenate([np.arange(fb, fb + P)] + [np.arange(qa + h * HD, qa + (h + 1) * HD) for h in order] +
                          [np.arange(ka, ka + 2 * P), np.arange(qb, fb)])
    w_proj = tiles(win[:, pick])
    both = np.stack([tiles(win[:, ga:ga + D]), tiles(win[:, gb:gb + D]),
                     np.concatenate([tiles(a["w_pa"][0].reshape(HEADS, HD, D)[order].reshape(512, D)),
                                     tiles(a["w_pb"][0])], axis=2)], axis=1)
    bias = a["b_in"][0]
    b_cols = np.concatenate([bias[pick], bias[ga:ga + 2 * D]]).reshape(-1, P).T
    norm_cols = np.stack([a[n].reshape(KT, P) for n in ("eg", "eb", "g1", "b1", "g2", "b2")]).reshape(-1, P).T
    cst, hot, outside = constants()
    ins = {
        "x": a["x"][0], "meta": a["meta"], "consts": cst, "buckets": hot, "outside": outside, "norm_cols": norm_cols,
        "b_cols": b_cols, "rel_bias": a["rel"], "sinks": a["sinks"][0],
        "w_proj": w_proj.reshape(N_PROJ, P, D), "w_merge": both.reshape(N_MERGE, P, D),
        "w_out": tiles(a["w_o"][0]).reshape(N_OUT, P, D), "w_pq": tiles(a["wq"][0]).reshape(N_PQ, P, D),
        "subkeys": a["sk"][0].reshape(2 * HEADS, NKEYS, P).transpose(2, 0, 1),
        "u_exp": a["u"][0].reshape(NKEYS, NKEYS, KT, P).transpose(1, 3, 2, 0).reshape(NKEYS, P, D),
        "v_exp": a["v"][0].reshape(NKEYS, NKEYS, D).transpose(1, 0, 2),
    }
    nc = bacc.Bacc("TRN2", target_bir_lowering=False, num_devices=1)
    arrays, args = {}, []
    for name, v in ins.items():
        v = np.ascontiguousarray(v)
        arrays[f"in_{name}"] = v
        args.append(nc.dram_tensor(f"in_{name}", v.shape, mybir.dt.from_np(v.dtype), kind="ExternalInput").ap())
    out = nc.dram_tensor("out_0", (SEQ, D), F32, kind="ExternalOutput").ap()
    build(nc, *args, out)
    r = run_bass_kernel_spmd(nc, [arrays], core_ids=[0])
    return r.results[0]["out_0"].reshape(1, SEQ, D)
```

```python
from contextlib import ExitStack

import numpy as np

import concourse.bass as bass
from concourse import mybir

P = 128
D = 1024
SEQ = 512
META = 16
COLS = SEQ + META
HALF = COLS // 2
KT = D // P
NBLK = SEQ // P
HEADS = 8
HD = 64
NKEYS = 128
TOPK = 16
BUCKETS = 32
EPS = 1e-5
ALPHA = 2.0 ** 0.25
NEG = -1e30
LOWEST = -3.0e38
GATE_SCALE = 2.0 ** 15

RING = 4
N_PROJ = 19
N_MERGE = 24
N_OUT = 8
N_PQ = 16
FIRST_MERGE = N_PROJ
N_GATE = 2 * (KT - 1)
UNIT_TILES = 2
FIRST_MIX = FIRST_MERGE + N_GATE
FIRST_OUT = FIRST_MERGE + N_MERGE
FIRST_PQ = FIRST_OUT + N_OUT
FIRST_U = FIRST_PQ + N_PQ
FIRST_V = FIRST_U + NKEYS
UNITS = 2 * NBLK * HEADS
GROUP = 4
NGROUP = NKEYS // GROUP
BGROUP = NGROUP // NBLK
CHUNK = P // (BGROUP // 2 * GROUP)
RANGES = BGROUP // 2 * 2
BRANGE = NKEYS // RANGES
TOP_MARKS = 46
HOT_MARKS = 12
BATCHES = SEQ // CHUNK

F32 = mybir.dt.float32
F32R = mybir.dt.float32r
F16 = mybir.dt.float16
U32 = mybir.dt.uint32
ALU = mybir.AluOpType
ACT = mybir.ActivationFunctionType
AX = mybir.AxisListType

C_ID, C_MASK, C_IOTA, C_IOTA16, C_EPS, C_ONE = 0, 128, 256, 384, 400, 401
C_COLS = 402


class Chain:

    def __init__(self, eng, sem):
        self.eng, self.sem, self.n, self.past = eng, sem, 0, 0

    def mark(self, ins):
        ins.then_inc(self.sem, 1)
        self.n += 1

    def settle(self):
        self.eng.wait_ge(self.sem, self.n + self.past)

    def settle_apart(self, memset, spare):
        self.settle()
        memset(spare, 0.0)

    def link(self, ins):
        self.mark(ins)
        self.settle()

    def loop(self, i, each):
        self.start, self.each, self.past = self.n, each, i * each

    def end(self, times):
        assert self.n - self.start == self.each, (self.n - self.start, self.each)
        self.n = self.start + self.each * times
        self.past = 0


def unit_of(u):
    window = u < UNITS // 2
    n, h = (u % (UNITS // 2)) // HEADS, u % HEADS
    tile, half = (h % 4, h // 4) if window else (h // 2, h % 2)
    return window, n, h, tile, half


def pieces_of(u):
    window, n, _, _, _ = unit_of(u)
    if window:
        return [(0, META, None), (META, P, 0)] if n == 0 else [(0, P, n - 1), (P, P, n)]
    return [(0, META, None)] + [(META + P * b, P, b) for b in range(n + 1)]


def width_of(u):
    c, k, _ = pieces_of(u)[-1]
    return c + k


PAIRED = UNITS // 2
STEPS = [(u, u + 1) for u in range(0, PAIRED, 2)] + [(u,) for u in range(PAIRED, UNITS)]
N_STEPS = len(STEPS)


def placed(s):
    return [(u, i * width_of(u)) for i, u in enumerate(STEPS[s])]


def pieces_at(s):
    return [(u, first + c, keys, b) for u, first in placed(s) for c, keys, b in pieces_of(u)]


def has_meta(s):
    return sum(b is None for _, _, _, b in pieces_at(s))


def tiles_before(s):
    return min(KT * N_GATE, UNIT_TILES * sum(len(x) for x in STEPS[:s]))


def slab_ended(s):
    done, before = tiles_before(s + 1) // KT, tiles_before(s) // KT
    return done - 1 if 0 <= s < N_STEPS and done > before else None


def block_ended(s):
    return STEPS[s][-1] // HEADS if 0 <= s < N_STEPS and STEPS[s][-1] % HEADS == HEADS - 1 else None


def build(nc, x, meta, consts, buckets, outside, norm_cols, b_cols, rel_bias, sinks, w_proj, w_merge, w_out,
          w_pq, subkeys, u_exp, v_exp, norm_rows, out):
    ctx = ExitStack()
    with ctx:
        def sem(name):
            return ctx.enter_context(nc.semaphore(name))

        def place(stack, **specs):
            return [stack.enter_context(nc.sbuf_tensor(n, s, t)) for n, (s, t) in specs.items()]

        cst, ncol, bcol = place(ctx, cst=([P, C_COLS], F32), ncol=([P, 4 * KT], F32), bcol=([P, N_PROJ + 16], F32))
        raw, hi, lo = place(ctx, raw=([P, RING, D], F32), hi=([P, RING, D], F32R), lo=([P, RING, D], F32R))
        hT_hi, hT_lo = place(ctx, hT_hi=([P, KT, COLS], F32R), hT_lo=([P, KT, COLS], F32R))
        ident = cst[:, C_ID:C_ID + P]
        mask = cst[:, C_MASK:C_MASK + P]
        mean_of, = place(ctx, mean_of=([P, P], F32R))
        iota16 = cst[:, C_IOTA16:C_IOTA16 + TOPK]
        eps = cst[:, C_EPS:C_EPS + 1]
        one = cst[:, C_ONE:C_ONE + 1]
        spare, = place(ctx, spare=([P, 1], F32))
        with ExitStack() as s:
            biasA, qaT = place(s, biasA=([P, HEADS, 2 * P], F32), qaT=([P, 4, SEQ], F32))
        with ExitStack() as s:
            late_gates, = place(s, late_gates=([P, N_GATE // 2, SEQ], F32))
        acc, = place(ctx, acc=([P, KT, SEQ], F32))
        with ExitStack() as s:
            xin, xT = place(s, xin=([P, 5, D], F32), xT=([P, 2, COLS], F32))
            stats, mv, rs = place(s, stats=([P, 5, 12], F32), mv=([P, 5, 2], F32), rs=([P, 4, 5], F32))
        with ExitStack() as s:
            vT, logf = place(s, vT=([P, 5, COLS], F32), logf=([HEADS, 6, COLS], F32))
        with ExitStack() as s:
            oT_hi, oT_lo = place(s, oT_hi=([P, 2, 4, SEQ], F32R), oT_lo=([P, 2, 4, SEQ], F32R))
            with ExitStack() as t:
                kaT, qbT, kbT = place(t, kaT=([P, COLS], F32), qbT=([P, 4, SEQ], F32), kbT=([P, 4, COLS], F32))
                vN, vM = place(t, vN=([P, NBLK, 640], F32), vM=([META, 640], F32))
                ckB, cq = place(t, ckB=([P, HEADS, COLS], F32), cq=([P, NBLK, HEADS], F32))
                pexp, pT, pM = place(t, pexp=([P, 2, COLS], F32), pT=([P, 2, SEQ], F32), pM=([META, 2, 2, P], F32))
                nmax, rsum, sexp, snk = place(t, nmax=([P, UNITS], F32), rsum=([P, 2, UNITS], F32),
                                              sexp=([P, UNITS], F32), snk=([P, 2, HEADS], F32))
                with ExitStack() as v:
                    relb, buck, wrow = place(v, relb=([BUCKETS, HEADS], F32), buck=([BUCKETS, 3 * P], F32),
                                             wrow=([HEADS, 2, 3 * P], F32))
                early_gates, = place(t, early_gates=([P, N_GATE // 2, SEQ], F32))
            gate, mix = place(s, gate=([P, 2, 2, SEQ], F32), mix=([P, 2, 2, SEQ], F32))
            m_hi, m_lo = place(s, m_hi=([P, KT, SEQ], F32R), m_lo=([P, KT, SEQ], F32R))
            r_hi, r_lo = place(s, r_hi=([P, 2, SEQ], F32R), r_lo=([P, 2, SEQ], F32R))
        with ExitStack() as s:
            sq_hi, sq_lo, sq, rinv, nw = place(s, sq_hi=([P, 2, SEQ], F32R), sq_lo=([P, 2, SEQ], F32R),
                                               sq=([P, 2, SEQ], F32), rinv=([P, SEQ], F32), nw=([P, 2, SEQ], F32))
        with ExitStack() as s:
            now, keys, best = place(s, now=([P, 2, 2, NKEYS], F32), keys=([P, 2, P], F32), best=([P, P], F32))
            rest, cand, topv, topi, topf = place(
                s, rest=([P, 2 * NKEYS], F32), cand=([P, TOPK * TOPK], F32),
                topv=([P, 2, TOPK], F32), topi=([P, 2, TOPK], U32), topf=([P, 2, TOPK], F32))
            flat, pos, posf, eq = place(s, flat=([P, TOPK], U32), pos=([P, 2, TOPK], U32),
                                        posf=([P, 2, TOPK], F32), eq=([P, 2, TOPK, TOPK], F32))
            gsum, iaT, ibT, gT_hi, gT_lo, iota_h = place(
                s, gsum=([P, 3, HEADS], F32), iaT=([P, P], F16), ibT=([P, P], F16), gT_hi=([P, P], F16),
                gT_lo=([P, P], F16), iota_h=([P, NKEYS, CHUNK], F16))
            hotA, hotB, hotG_hi, hotG_lo = place(
                s, hotA=([P, 2, NKEYS, CHUNK], F16), hotB=([P, NKEYS, CHUNK], F16),
                hotG_hi=([P, 2, NKEYS, CHUNK], F16), hotG_lo=([P, 2, NKEYS, CHUNK], F16))
            gelu, = place(s, gelu=([P, RING, SEQ], F32))
            with ExitStack() as t:
                sk_raw, sk_hi, sk_lo = place(t, sk_raw=([P, 2 * HEADS, NKEYS], F32),
                                             sk_hi=([P, 2 * HEADS, NKEYS], F32R), sk_lo=([P, 2 * HEADS, NKEYS], F32R))
                pq_hi, pq_lo, sc = place(t, pq_hi=([P, 2, SEQ], F32R), pq_lo=([P, 2, SEQ], F32R), sc=([P, 2, SEQ], F32))
            with ExitStack() as t:
                gates, gate_first = place(t, gates=([P, NKEYS, P], F32), gate_first=([P, RING, (NBLK - 1) * P], F32))
            tok, gain_shift = place(s, tok=([P, NBLK, D], F32), gain_shift=([P, 2, D], F32))
            stats2, mv2, rs2 = place(s, stats2=([P, NBLK, 12], F32), mv2=([P, NBLK, 2], F32), rs2=([P, 5, NBLK], F32))
            half_pad, = place(s, half_pad=([P, (NKEYS // 2) * P - (NBLK + 2) * D - NBLK * (12 + 2 + 5)], F32))
            hi_x, lo_x = place(s, hi_x=([P, RING, D], F32R), lo_x=([P, RING, D], F32R))
        with ExitStack() as s:
            gel_in, gate_in, act_t = place(s, gel_in=([P, RING, SEQ], F32), gate_in=([P, RING, SEQ], F32),
                                           act_t=([P, RING, SEQ], F32))

        psS = ctx.enter_context(nc.psum_tensor("psS", [P, 2, 2 * SEQ], F32))
        psT = ctx.enter_context(nc.psum_tensor("psT", [P, 2 * SEQ], F32))
        psO = ctx.enter_context(nc.psum_tensor("psO", [P, 2, SEQ], F32))
        banks = [psS[:, 0, 0:SEQ], psS[:, 0, SEQ:], psS[:, 1, 0:SEQ], psS[:, 1, SEQ:],
                 psT[:, 0:SEQ], psT[:, SEQ:], psO[:, 0, :], psO[:, 1, :]]

        wide = [psS[:, 0, :], psS[:, 1, :], psT[:, :], psO[:, :, :].rearrange("p o q -> p (o q)")]

        w_dram = nc.dram_tensor("w_dram", [P, HEADS, 3 * P], F32).ap()
        c_dram = nc.dram_tensor("c_dram", [HEADS, COLS], F32).ap()
        sc_dram = nc.dram_tensor("sc_dram", [NBLK, P, 2 * HEADS * NKEYS], F32).ap()
        gelu_dram = nc.dram_tensor("gelu_dram", [NKEYS, P, SEQ], F32).ap()
        gates_dram = nc.dram_tensor("gates_dram", [NKEYS, P, SEQ], F32).ap()

        cst_in, bias_in, x_in, keys_in = sem("cst_in"), sem("bias_in"), [sem(f"x_in{t}") for t in range(5)], sem("keys_in")
        landed = [sem(f"landed{r}") for r in range(RING)]
        hi_done, lo_done, slab_used = sem("hi_done"), sem("lo_done"), sem("slab_used")
        std_done, norm_done, turned, xT_done, hT_hi_done, hT_lo_done = (
            sem("std_done"), sem("norm_done"), sem("turned"), sem("xT_done"), sem("hT_hi_done"), sem("hT_lo_done"))
        evacuated = sem("evacuated")
        z_done, soft_done, c_done, c_out, ck_in, c_turned = (
            sem("z_done"), sem("soft_done"), sem("c_done"), sem("c_out"), sem("ck_in"), sem("c_turned"))
        w_mm, w_done, w_stored, biasA_in = sem("w_mm"), sem("w_done"), sem("w_stored"), sem("biasA_in")
        v_turned, v_ready = sem("v_turned"), sem("v_ready")
        s_mm, nmax_done, exp_done, p_done, p_turned, pT_done, pM_done = (
            sem("s_mm"), sem("nmax_done"), sem("exp_done"), sem("p_done"), sem("p_turned"), sem("pT_done"), sem("pM_done"))
        pv_mm, o_hi_done, o_lo_done = sem("pv_mm"), sem("o_hi_done"), sem("o_lo_done")
        gate_in_done = sem("gate_in_done")
        gate_done, mix_done, m_hi_done, m_lo_done = sem("gate_done"), sem("mix_done"), sem("m_hi_done"), sem("m_lo_done")
        r_done, mean_mm, xc_done, sq_done, var_mm, sd_done, h_done, scaled = (
            sem("r_done"), sem("mean_mm"), sem("xc_done"), sem("sq_done"), sem("var_mm"), sem("sd_done"), sem("h_done"), sem("scaled"))
        gained = sem("gained")
        r_hi_done, r_lo_done, sq_hi_done, sq_lo_done = sem("r_hi_done"), sem("r_lo_done"), sem("sq_hi_done"), sem("sq_lo_done")
        mean_set = sem("mean_set")
        sk_hi_done, sk_done, pq_hi_done, pq_lo_done, sc_mm, sc_done = (
            sem("sk_hi_done"), sem("sk_done"), sem("pq_hi_done"), sem("pq_lo_done"), sem("sc_mm"), sem("sc_done"))
        gelu_done, top_done = sem("gelu_done"), sem("top_done")
        sc_out, now_in = [sem(f"sc_out{r}") for r in range(2)], [sem(f"now_in{r}") for r in range(2)]
        gelu_out = [sem(f"gelu_out{r}") for r in range(RING)]
        less_done, g_exp_done, g_done, idx_turned, gT_hi_done, idx_done = (
            sem("less_done"), sem("g_exp_done"), sem("g_done"), sem("idx_turned"), sem("gT_hi_done"), sem("idx_done"))
        last_out = [sem(f"last_out{r}") for r in range(2)]
        hot_done, G_mm, G_act, gates_out = sem("hot_done"), sem("G_mm"), sem("G_act"), sem("gates_out")
        gel_in_s, gate_in_s = [sem(f"gel_in{r}") for r in range(RING)], [sem(f"gate_in{r}") for r in range(RING)]
        vhi_done, vlo_done, act_done, ahi_done, alo_done = (
            sem("vhi_done"), sem("vlo_done"), sem("act_done"), sem("ahi_done"), sem("alo_done"))
        v_mm, y_added = sem("v_mm"), sem("y_added")
        out_turned, tok_done, out_sent = sem("out_turned"), sem("tok_done"), sem("out_sent")
        rows_in, std2_done, rs2_done, unit_done = sem("rows_in"), sem("std2_done"), sem("rs2_done"), sem("unit_done")
        act_step, dve_step = sem("act_step"), sem("dve_step")

        block = ctx.enter_context(nc.Block())

        def slab_source(n):
            if n < FIRST_MERGE:
                return w_proj[n]
            if n < FIRST_OUT:
                return w_merge[n - FIRST_MERGE]
            if n < FIRST_PQ:
                return w_out[n - FIRST_OUT]
            if n < FIRST_U:
                return w_pq[n - FIRST_PQ]
            return u_exp[n - FIRST_U]

        def landed_wait(eng, n, i=0, per=0):
            eng.wait_ge(landed[n % RING], 16 * (n // RING + 1) + i * (16 * per // RING))

        def load(sp, n, source, i=0, per=0):
            if n >= RING:
                sp.wait_ge(lo_done, n - RING + 1 + i * per)
            sp.dma_start(raw[:, n % RING, :], source).then_inc(landed[n % RING], 16)

        def split_hi(act, n, i=0, per=0, done=hi_done):
            landed_wait(act, n, i, per)
            if n >= RING:
                act.wait_ge(slab_used, n - RING + 1 + i * per)
            nc.scalar.activation(hi[:, n % RING, :], raw[:, n % RING, :], ACT.Copy).then_inc(done, 1)

        def split_lo(dve, n, i=0, per=0):
            dve.wait_ge(hi_done, n + 1 + i * per)
            nc.vector.tensor_tensor(lo[:, n % RING, :], raw[:, n % RING, :], hi[:, n % RING, :].bitcast(F32),
                                    ALU.subtract).then_inc(lo_done, 1)

        def output_parts(slot):
            if slot < RING:
                return hi[:, (FIRST_V + slot) % RING, :], lo[:, (FIRST_V + slot) % RING, :]
            return hi_x[:, slot - RING, :], lo_x[:, slot - RING, :]

        def split_product(out_ap, w_h, w_l, x_h, x_l, start, stop):
            nc.tensor.matmul(out_ap, w_h, x_l, start=start, stop=False)
            nc.tensor.matmul(out_ap, w_l, x_h, start=False, stop=False)
            return nc.tensor.matmul(out_ap, w_h, x_h, start=False, stop=stop)

        def slab_parts(slot, k):
            return hi[:, slot, k * P:(k + 1) * P], lo[:, slot, k * P:(k + 1) * P]

        def store_gates(eng, t, first, sem_out):
            bs = bass.ds(first, BRANGE)
            eng.dma_start(gates_dram[bs, :, t * P:(t + 1) * P].rearrange("b a c -> a b c"),
                          gates[:, bs, :]).then_inc(sem_out, 16)

        def gate_input(v):
            half = N_GATE // 2
            return early_gates[:, v, :] if v < half else late_gates[:, v - half, :]

        AHEAD = 3

        def wait_at(eng, semaphore, first, per, i):
            if not isinstance(i, int) or first + per * i > 0:
                eng.wait_ge(semaphore, first + per * i)

        def exp_count(s):
            return sum(2 if unit_of(u)[0] else 1 for step in STEPS[:s + 1] for u in step)

        def meta_count(s):
            return sum(has_meta(t) > 0 for t in range(s + 1))

        @block.sync
        def _(sp):
            for t in range(NBLK):
                sp.dma_start(xin[:, t, :], x[t * P:(t + 1) * P, :]).then_inc(x_in[t], 16)
            sp.dma_start(xin[0:META, NBLK, :], meta).then_inc(x_in[NBLK], 16)
            sp.dma_start(cst[:, :], consts).then_inc(cst_in, 16)
            sp.dma_start(ncol[:, :], norm_cols).then_inc(cst_in, 16)
            sp.dma_start(bcol[:, :], b_cols).then_inc(cst_in, 16)
            for n in range(RING):
                load(sp, n, slab_source(n))
            sp.dma_start(relb[:, :], rel_bias).then_inc(bias_in, 16)
            sp.dma_start(buck[:, :], buckets).then_inc(bias_in, 16)
            sp.dma_start(wrow[:, 1, :], outside).then_inc(bias_in, 16)
            sp.dma_start(snk[:, 0, :], sinks.partition_broadcast(P)).then_inc(bias_in, 16)
            for n in range(RING, FIRST_U + RING):
                load(sp, n, slab_source(n))
            with sp.Fori(1, NGROUP) as i:
                for j in range(GROUP):
                    n = FIRST_U + j
                    load(sp, n, u_exp[i * GROUP + j], i, GROUP)
                    sp.wait_ge(gelu_done, i * GROUP + (j - GROUP + 1))
                    sp.dma_start(gelu_dram[i * GROUP + (j - GROUP)], gelu[:, j, :]).then_inc(gelu_out[j], 16)
            for j in range(GROUP):
                load(sp, FIRST_V + j, v_exp[j])
            sp.wait_ge(idx_turned, NBLK)
            sp.wait_ge(gates_out, 16 * RANGES * (NBLK - 1))
            early = (NBLK - 1) * P
            for j in range(GROUP):
                sp.dma_start(gel_in[:, j, :], gelu_dram[j]).then_inc(gel_in_s[j], 16)
                sp.dma_start(gate_first[:, j, :], gates_dram[j][:, 0:early]).then_inc(gate_in_s[j], 16)
            for j in range(GROUP):
                sp.wait_ge(gelu_done, NKEYS - GROUP + j + 1)
                sp.dma_start(gelu_dram[NKEYS - GROUP + j], gelu[:, j, :]).then_inc(gelu_out[j], 16)
            sp.wait_ge(G_act, BATCHES)

            def load_tiles(b, j, i, cols=SEQ):
                sp.wait_ge(act_done, j - RING + 1 + RING * i)
                sp.dma_start(gel_in[:, j, :], gelu_dram[b]).then_inc(gel_in_s[j], 16)
                sp.dma_start(gate_in[:, j, 0:cols], gates_dram[b][:, 0:cols]).then_inc(gate_in_s[j], 16)

            def load_group(i, cols=SEQ):
                for j in range(GROUP):
                    sp.wait_ge(vlo_done, i * GROUP + (j - RING + 1))
                    sp.dma_start(raw[:, (FIRST_V + j) % RING, :],
                                 v_exp[i * GROUP + j]).then_inc(landed[(FIRST_V + j) % RING], 16)
                    load_tiles(i * GROUP + j, j, i, cols)

            load_group(1, early)
            for r in range(2):
                sp.wait_ge(last_out[r], 16 * RANGES // 2)
            for j in range(RING):
                sp.wait_ge(gelu_out[j], 16 * NGROUP)
            with sp.Fori(2, NGROUP) as i:
                load_group(i)
            for t in range(NBLK):
                sp.wait_ge(tok_done, t + 1)
                sp.dma_start(out[t * P:(t + 1) * P, :], tok[:, t, :]).then_inc(out_sent, 16)
            sp.wait_ge(out_sent, 16 * NBLK)

        @block.gpsimd
        def _(pool):
            pool.wait_ge(w_done, 1)
            pool.dma_start(w_dram.rearrange("q h m -> h q m"),
                           wrow[:, 0, :].unsqueeze(1).to_broadcast([HEADS, P, 3 * P])).then_inc(w_stored, 16)
            pool.wait_ge(w_stored, 16)
            skewed = bass.AP(w_dram.tensor, P - 1, [[3 * P * HEADS - 1, P], [3 * P, HEADS], [1, 2 * P]])
            pool.dma_start(biasA[:, :, :], skewed).then_inc(biasA_in, 16)
            pool.wait_ge(c_done, 1)
            pool.dma_start(c_dram[:, 0:META], logf[:, 5, SEQ:COLS]).then_inc(c_out, 16)
            pool.dma_start(c_dram[:, META:COLS], logf[:, 5, 0:SEQ]).then_inc(c_out, 16)
            pool.wait_ge(c_out, 32)
            pool.wait_ge(xT_done, KT)
            pool.dma_start(ckB[:, :, :].rearrange("p h c -> p (h c)"),
                           c_dram.rearrange("h c -> (h c)").partition_broadcast(P)).then_inc(ck_in, 16)
            pool.wait_ge(r_done, N_OUT)
            pool.dma_start(sk_raw[:, :, :], subkeys).then_inc(keys_in, 16)
            for k in range(KT):
                pool.wait_ge(hT_lo_done, KT + k + 1)
                nc.gpsimd.tensor_scalar(acc[:, k, :], acc[:, k, :], ALPHA, None, ALU.mult).then_inc(scaled, 1)
            for q in range(N_PQ):
                pool.wait_ge(sc_done, q + 1)
                pool.dma_start(sc_dram[:, :, q * NKEYS:(q + 1) * NKEYS].rearrange("t p k -> p t k"),
                               sc[:, q % 2, :].rearrange("p (t k) -> p t k", t=NBLK)).then_inc(sc_out[q % 2], 16)
            for r in range(2):
                pool.wait_ge(sc_out[r], 16 * N_PQ // 2)

            def load_now(t, h, r):
                pool.dma_start(now[:, r, :, :].rearrange("p s k -> p (s k)"),
                               sc_dram[t][:, bass.ds(h * 2 * NKEYS, 2 * NKEYS)]).then_inc(now_in[r], 16)

            for t in range(NBLK):
                for r in range(2):
                    if t > 0:
                        pool.wait_ge(top_done, HEADS * t + r - 1)
                    load_now(t, r, r)
                with pool.Fori(1, HEADS // 2) as i:
                    for r in range(2):
                        pool.wait_ge(top_done, i * 2 + (HEADS * t + r - 1))
                        load_now(t, i * 2 + r, r)
            pool.wait_ge(last_out[0], 16 * RANGES // 2)
            pool.wait_ge(act_done, 2 * RING)
            pool.dma_start(gain_shift[:, :, :].rearrange("p r d -> p (r d)"),
                           norm_rows.rearrange("r d -> (r d)").partition_broadcast(P)).then_inc(rows_in, 16)

        @block.scalar
        def _(act):
            own = Chain(act, act_step)
            act.wait_ge(norm_done, 1)
            nc.scalar.activation(rs[:, 0, :], mv[:, :, 1], ACT.Sqrt, bias=eps).then_inc(std_done, 1)
            for n in range(AHEAD):
                split_hi(act, n)
            for k in range(KT):
                act.wait_ge(turned, k + 1)
                if k >= 2:
                    act.wait_ge(hT_lo_done, k - 1)
                nc.scalar.activation(xT[:, k % 2, :], psS[:, k % 2, 0:COLS], ACT.Identity, scale=ncol[:, k:k + 1],
                                     bias=ncol[:, KT + k:KT + k + 1]).then_inc(xT_done, 1)
                act.wait_ge(xT_done, k + 1)
                nc.scalar.activation(hT_hi[:, k, :], xT[:, k % 2, :], ACT.Copy).then_inc(hT_hi_done, 1)
            for n in range(N_PROJ):
                split_hi(act, n + AHEAD)
                if n == 1:
                    act.wait_ge(z_done, 1)
                    own.link(nc.scalar.activation(logf[:, 1, :], logf[:, 0, :], ACT.Abs))
                    own.link(nc.scalar.activation(logf[:, 2, :], logf[:, 1, :], ACT.Exp, scale=-1.0))
                    nc.scalar.activation(logf[:, 3, :], logf[:, 2, :], ACT.Ln, bias=one[0:HEADS, :]).then_inc(soft_done, 1)
            for b in range(NBLK + 1):
                act.wait_ge(v_turned, b + 1)
                if b < NBLK:
                    nc.scalar.activation(vN[:, b, :], psS[:, b % 2, 0:640], ACT.Copy).then_inc(v_ready, 1)
                else:
                    nc.scalar.activation(vM[:, :], psT[0:META, 0:640], ACT.Copy).then_inc(v_ready, 1)

            for s in range(N_STEPS + 4):
                if s < N_STEPS:
                    act.wait_ge(nmax_done, s + 1)
                    if s >= 2:
                        act.wait_ge(p_turned, s - 1)
                    for u, first in placed(s):
                        window, n, h, tile, half = unit_of(u)
                        if window:
                            nc.scalar.activation(sexp[:, u:u + 1], snk[:, 0, h:h + 1], ACT.Exp,
                                                 bias=nmax[:, u:u + 1]).then_inc(exp_done, 1)
                        cols = slice(first, first + width_of(u))
                        nc.scalar.activation(pexp[:, s % 2, cols], psS[:, s % 2, cols], ACT.Exp,
                                             bias=nmax[:, u:u + 1], accum_out=rsum[:, 0, u:u + 1]).then_inc(exp_done, 1)
                v = slab_ended(s - 1)
                if v is not None:
                    act.wait_ge(slab_used, FIRST_MERGE + v + 1)
                    tile = N_PROJ + 8 * (v % 2) + v // 2
                    nc.scalar.activation(gate_input(v), psS[:, v % 2, SEQ:], ACT.Identity,
                                         bias=bcol[:, tile:tile + 1]).then_inc(gate_in_done, 1)
                if 1 <= s <= N_STEPS:
                    act.wait_ge(p_turned, s)
                    if s >= 3:
                        act.wait_ge(pv_mm, s - 2)
                    cols = P * sum(b is not None for _, _, _, b in pieces_at(s - 1))
                    nc.scalar.activation(pT[:, (s - 1) % 2, 0:cols], psT[:, 0:cols], ACT.Copy).then_inc(pT_done, 1)
                    if has_meta(s - 1):
                        cols = P * has_meta(s - 1)
                        nc.scalar.activation(pM[:, (s - 1) % 2, :, :].rearrange("p g q -> p (g q)")[:, 0:cols],
                                             psT[0:META, SEQ:SEQ + cols], ACT.Copy).then_inc(pM_done, 1)
                v = slab_ended(s)
                if v is not None:
                    split_hi(act, FIRST_MERGE + v + AHEAD)
                w = block_ended(s - 3)
                if w is not None:
                    act.wait_ge(pv_mm, s - 2)
                    nc.scalar.activation(oT_hi[:, w // NBLK, :, (w % NBLK) * P:(w % NBLK + 1) * P],
                                         psO[:, w % 2, :].rearrange("p (t q) -> p t q", t=4),
                                         ACT.Copy).then_inc(o_hi_done, 1)

            for m in range(KT):
                if m >= 2:
                    act.wait_ge(mix_done, m - 1)
                if m < KT - 1:
                    split_hi(act, FIRST_MIX + m + AHEAD)
                    for j in range(2):
                        nc.scalar.activation(gate[:, m % 2, j, :], gate_input(2 * m + j), ACT.Sigmoid).then_inc(gate_done, 1)
                else:
                    for j in range(3):
                        n = FIRST_MIX + m + j
                        split_hi(act, n + AHEAD)
                        if j < 2:
                            act.wait_ge(slab_used, n + 1)
                            nc.scalar.activation(gate[:, m % 2, j, :], psS[:, m % 2, j * SEQ:(j + 1) * SEQ], ACT.Sigmoid,
                                                 bias=bcol[:, N_PROJ + 8 * j + m:N_PROJ + 8 * j + m + 1]).then_inc(gate_done, 1)
                act.wait_ge(mix_done, m + 1)
                nc.scalar.activation(m_hi[:, m, :], mix[:, m % 2, 0, :], ACT.Copy).then_inc(m_hi_done, 1)
            for m in range(N_OUT):
                split_hi(act, FIRST_OUT + m + AHEAD)
                act.wait_ge(r_done, m + 1)
                if m >= 2:
                    act.wait_ge(mean_mm, m - 1)
                nc.scalar.activation(r_hi[:, m % 2, :], acc[:, m, :], ACT.Copy).then_inc(r_hi_done, 1)

            for k in range(KT):
                act.wait_ge(xc_done, k + 1)
                if k >= 2:
                    act.wait_ge(sq_lo_done, k - 1)
                    act.wait_ge(var_mm, k - 1)
                nc.scalar.activation(sq[:, k % 2, :], acc[:, k, :], ACT.Square).then_inc(sq_done, 1)
                act.wait_ge(sq_done, k + 1)
                nc.scalar.activation(sq_hi[:, k % 2, :], sq[:, k % 2, :], ACT.Copy).then_inc(sq_hi_done, 1)
            act.wait_ge(var_mm, KT)
            nc.scalar.activation(nw[:, 0, :], banks[5], ACT.Sqrt, bias=eps).then_inc(sd_done, 1)
            for k in range(KT):
                act.wait_ge(gained, k + 1)
                nc.scalar.activation(acc[:, k, :], acc[:, k, :], ACT.Identity,
                                     bias=ncol[:, 3 * KT + k:3 * KT + k + 1]).then_inc(h_done, 1)
                act.wait_ge(h_done, k + 1)
                nc.scalar.activation(hT_hi[:, k, 0:SEQ], acc[:, k, :], ACT.Copy).then_inc(hT_hi_done, 1)
            act.wait_ge(keys_in, 16)
            nc.scalar.activation(sk_hi[:, :, :], sk_raw[:, :, :], ACT.Copy).then_inc(sk_hi_done, 1)
            for q in range(N_PQ + 1):
                if q < N_PQ:
                    n = FIRST_PQ + q
                    split_hi(act, n + AHEAD)
                    act.wait_ge(slab_used, n + 1)
                    if q >= 2:
                        act.wait_ge(sc_mm, q - 1)
                    nc.scalar.activation(pq_hi[:, q % 2, :], psS[:, q % 2, 0:SEQ], ACT.Copy).then_inc(pq_hi_done, 1)
                if q >= 1:
                    act.wait_ge(sc_mm, q)
                    if q >= 3:
                        act.wait_ge(sc_out[(q - 1) % 2], 16 * ((q - 1) // 2))
                    nc.scalar.activation(sc[:, (q - 1) % 2, :], banks[4 + (q - 1) % 4], ACT.Copy).then_inc(sc_done, 1)

            def split_first_hi(v):
                split_hi(act, FIRST_V + v, done=vhi_done)

            def expert_step(j, i, block=None, before_gelu=None, stored=None):
                n = FIRST_U + j + 1
                if isinstance(i, int) and GROUP * i + j + 1 + AHEAD >= NKEYS:
                    split_first_hi(GROUP * i + j + 1 + AHEAD - NKEYS)
                else:
                    split_hi(act, n + AHEAD, i, GROUP)
                if before_gelu:
                    before_gelu()
                if not (isinstance(i, int) and GROUP * i + j + 1 >= NKEYS):
                    act.wait_ge(slab_used, n + 1 + i * GROUP)
                    wait_at(act, gelu_out[(j + 1) % RING], 16 * ((j + 1) // RING), 16, i)
                    nc.scalar.activation(gelu[:, (j + 1) % RING, :], banks[(j + 1) % RING], ACT.Gelu).then_inc(gelu_done, 1)
                if stored is not None and j % 2 == 0:
                    store_gates(act, stored, (i - (stored + 1) * BGROUP) * (2 * BRANGE) + j // 2 * BRANGE, gates_out)
                if block is not None:
                    first = block * BGROUP + BGROUP // 2
                    act.wait_ge(G_mm, (i - first) * GROUP + (block * (P // CHUNK) + j + 1))
                    src = (psT[:, :], psO[:, :, :].rearrange("p o q -> p (o q)"))[j % 2]
                    nc.scalar.activation(gates[:, :, bass.ds((i - first) * (GROUP * CHUNK) + j * CHUNK, CHUNK)],
                                         src.rearrange("p (c b) -> p b c", c=CHUNK), ACT.Copy,
                                         scale=1.0 / GATE_SCALE).then_inc(G_act, 1)

            def gate_exp(t):
                act.wait_ge(less_done, t + 1)
                nc.scalar.activation(best[:, :], best[:, :], ACT.Exp).then_inc(g_exp_done, 1)

            split_hi(act, FIRST_U + AHEAD)
            act.wait_ge(slab_used, FIRST_U + 1)
            nc.scalar.activation(gelu[:, 0, :], banks[0], ACT.Gelu).then_inc(gelu_done, 1)
            for t in range(NBLK):
                start, mid, end = BGROUP * t, BGROUP * t + BGROUP // 2, BGROUP * (t + 1)
                if t == 0:
                    for j in range(GROUP):
                        expert_step(j, 0)
                stored = t - 1 if t > 0 else None
                with act.Fori(max(start, 1), mid - 1) as i:
                    for j in range(GROUP):
                        expert_step(j, i, stored=stored)
                for j in range(GROUP):
                    expert_step(j, mid - 1, before_gelu=(lambda: gate_exp(t)) if j == GROUP - 1 else None, stored=stored)
                act.wait_ge(idx_turned, t + 1)
                nc.scalar.activation(gT_hi[:, :], banks[5][:, 0:P], ACT.Copy, scale=GATE_SCALE).then_inc(gT_hi_done, 1)
                for r in range(2):
                    act.wait_ge(sc_out[r], 16 * N_PQ // 2)
                if t > 0:
                    act.wait_ge(gates_out, 16 * RANGES * t)
                with act.Fori(mid, end if t < NBLK - 1 else end - 1) as i:
                    for j in range(GROUP):
                        expert_step(j, i, t)
                if t == NBLK - 1:
                    for j in range(GROUP):
                        expert_step(j, end - 1, t)
                act.wait_ge(G_act, (t + 1) * (P // CHUNK))
            def weigh(j, g, par):
                slot = par * GROUP + j
                if not (isinstance(g, int) and g == 0):
                    act.wait_ge(landed[(FIRST_V + j) % RING], 16 * ((FIRST_V + j) // RING + 1) + g * 16)
                    wait_at(act, v_mm, -KT, KT, g)
                    nc.scalar.activation(output_parts(slot)[0], raw[:, (FIRST_V + j) % RING, :], ACT.Copy).then_inc(vhi_done, 1)
                act.wait_ge(act_done, g * GROUP + (j + 1))
                nc.scalar.activation(hT_hi[:, slot, 0:SEQ], act_t[:, j, :], ACT.Copy).then_inc(ahi_done, 1)

            act.wait_ge(slab_used, FIRST_V)
            for j in range(GROUP):
                weigh(j, 0, 0)
            for r in reversed(range(RANGES)):
                store_gates(act, NBLK - 1, r * BRANGE, last_out[r // (RANGES // 2)])
            act.wait_ge(last_out[1], 16 * RANGES // 2)
            for j in range(GROUP):
                weigh(j, 1, 1)
            with act.Fori(1, NGROUP // 2) as i:
                for par in range(2):
                    for j in range(GROUP):
                        weigh(j, i * 2 + par, par)
            act.wait_ge(rs2_done, 1)
            nc.scalar.activation(rs2[:, 0, :], mv2[:, :, 1], ACT.Sqrt, bias=eps).then_inc(std2_done, 1)
            act.wait_ge(rs2_done, 2)
            for t in range(NBLK):
                nc.scalar.activation(tok[:, t, :], wide[t], ACT.Identity, bias=rs2[:, 4, t:t + 1],
                                     scale=rs2[:, 3, t:t + 1]).then_inc(unit_done, 1)

        @block.vector
        def _(dve):
            own = Chain(dve, dve_step)
            V = nc.vector

            def newton(y, var, t1):
                own.link(V.tensor_tensor(t1, y, y, ALU.mult))
                own.link(V.scalar_tensor_tensor(t1, var, EPS, t1, ALU.add, ALU.mult))
                own.link(V.tensor_scalar(t1, t1, -0.5, 1.5, ALU.mult, ALU.add))
                own.link(V.tensor_tensor(y, y, t1, ALU.mult))

            own.link(V.memset(mv[:, :, :], 1.0))
            for t in range(NBLK + 1):
                rows = P if t < NBLK else META
                dve.wait_ge(x_in[t], 16)
                for c in range(2):
                    own.mark(V.bn_stats(stats[0:rows, t, 6 * c:6 * c + 6], xin[0:rows, t, c * 512:(c + 1) * 512]))
                own.settle()
                own.mark(V.bn_aggr(mv[0:rows, t, :], stats[0:rows, t, :]))
            own.settle()
            own.link(V.tensor_copy(rs[:, 1, :], mv[:, :, 1]))
            dve.wait_ge(cst_in, 48)
            V.tensor_copy(rs[:, 2, :], mv[:, :, 0]).then_inc(norm_done, 1)
            dve.wait_ge(std_done, 1)
            own.link(V.reciprocal(rs[:, 3, :], rs[:, 0, :]))
            newton(rs[:, 3, :], rs[:, 1, :], rs[:, 2, :])
            for t in range(NBLK + 1):
                rows = P if t < NBLK else META
                V.tensor_scalar(xin[0:rows, t, :], xin[0:rows, t, :], mv[0:rows, t, 0:1], rs[0:rows, 3, t:t + 1],
                                ALU.subtract, ALU.mult).then_inc(norm_done, 1)
            for k in range(KT):
                dve.wait_ge(xT_done, k + 1)
                dve.wait_ge(hT_hi_done, k + 1)
                V.tensor_tensor(hT_lo[:, k, :], xT[:, k % 2, :], hT_hi[:, k, :].bitcast(F32),
                                ALU.subtract).then_inc(hT_lo_done, 1)
                if k < AHEAD:
                    split_lo(dve, k)
            V.tensor_scalar(mean_of[:, :], ident, 0.0, 1.0 / D, ALU.mult, ALU.add).then_inc(mean_set, 1)
            dve.wait_ge(bias_in, 64)
            dve.wait_ge(w_mm, 1)
            V.tensor_tensor(wrow[:, 0, :], psO[0:HEADS, 0, 0:3 * P], wrow[:, 1, :], ALU.add).then_inc(w_done, 1)
            own.link(V.tensor_scalar(snk[:, 1, :], snk[:, 0, :], -1.0, None, ALU.mult))

            for n in range(N_PROJ):
                split_lo(dve, n + AHEAD)
                dve.wait_ge(slab_used, n + 1)
                bias = bcol[:, n:n + 1]

                def halves(v):
                    return v.rearrange("p (b c) -> p b c", b=2)

                ps = halves(psS[:, n % 2, :])[:, :, 0:HALF]
                if n == 0:
                    V.tensor_scalar(halves(logf[:, 0, :]), ps[0:HEADS], bias[0:HEADS, :], None, ALU.add).then_inc(z_done, 1)
                    dve.wait_ge(z_done, 1)
                    V.tensor_scalar(logf[:, 4, :], logf[:, 0, :], 0.0, None, ALU.min).then_inc(evacuated, 1)
                    continue
                if 1 <= n <= 4 or 7 <= n <= 10:
                    dst = (qaT[:, n - 1, :] if n <= 4 else qbT[:, n - 7, :])
                    V.tensor_scalar(dst, psS[:, n % 2, 0:SEQ], bias, HD ** -0.5, ALU.add, ALU.mult).then_inc(evacuated, 1)
                else:
                    dst = kaT[:, :] if n == 5 else vT[:, 0, :] if n == 6 else (
                        kbT[:, n - 11, :] if n <= 14 else vT[:, n - 14, :])
                    if n == 5 or 11 <= n <= 14:
                        V.tensor_scalar(dst[:, 0:META], ps[:, 1, HALF - META:], bias, None, ALU.add)
                        V.tensor_scalar(dst[:, META:META + HALF], ps[:, 0, :], bias, None, ALU.add)
                        V.tensor_scalar(dst[:, META + HALF:], ps[:, 1, 0:HALF - META], bias, None,
                                        ALU.add).then_inc(evacuated, 1)
                    else:
                        V.tensor_scalar(halves(dst), ps, bias, None, ALU.add).then_inc(evacuated, 1)
                if n == 3:
                    dve.wait_ge(soft_done, 1)
                    own.mark(V.memset(logf[:, 1, :], 1.0))
                    own.link(V.tensor_tensor(logf[:, 4, :], logf[:, 4, :], logf[:, 3, :], ALU.subtract))
                    own.link(V.tensor_tensor_scan(logf[:, 5, SEQ:COLS], logf[:, 1, SEQ:COLS], logf[:, 4, SEQ:COLS],
                                                  0.0, ALU.mult, ALU.add))
                    V.tensor_tensor_scan(logf[:, 5, 0:SEQ], logf[:, 1, 0:SEQ], logf[:, 4, 0:SEQ],
                                         logf[:, 5, COLS - 1:COLS], ALU.mult, ALU.add).then_inc(c_done, 1)
                if n == 8:
                    dve.wait_ge(c_turned, 1)
                    own.link(V.tensor_copy(cq[:, :, :].rearrange("p n h -> p (n h)"), psO[:, 1, 0:NBLK * HEADS]))

            dve.wait_ge(biasA_in, 16)
            dve.wait_ge(ck_in, 16)
            for s in range(N_STEPS + 4):
                last_step = 1 <= s <= N_STEPS
                if last_step:
                    u0, u1 = STEPS[s - 1][0], STEPS[s - 1][-1] + 1

                def sum_done():
                    if last_step:
                        dve.wait_ge(exp_done, exp_count(s - 1))
                        if unit_of(u0)[0]:
                            r0 = rsum[:, 0, u0:u1]
                            own.mark(V.tensor_tensor(r0, r0, sexp[:, u0:u1], ALU.add))

                def invert_sum():
                    if last_step:
                        own.mark(V.reciprocal(rsum[:, 1, u0:u1], rsum[:, 0, u0:u1]))

                if s < N_STEPS:
                    u, count = STEPS[s][0], len(STEPS[s])
                    window, n, h, tile, half = unit_of(u)
                    L = width_of(u)
                    S = psS[:, s % 2, 0:count * L].rearrange("p (g k) -> p g k", g=count)
                    dve.wait_ge(s_mm, s + 1)
                    if window:
                        own.mark(V.tensor_tensor(S, S, biasA[:, h:h + count, 2 * P - L:2 * P], ALU.add))
                        sum_done()
                        own.settle()
                        own.mark(V.tensor_reduce(nmax[:, u:u + count], S, AX.X, ALU.max, negate=True))
                        invert_sum()
                        own.settle()
                        V.tensor_tensor(nmax[:, u:u + count], nmax[:, u:u + count], snk[:, 1, h:h + count],
                                        ALU.min).then_inc(nmax_done, 1)
                    else:
                        for g in range(count):
                            own.mark(V.scalar_tensor_tensor(S[:, g], S[:, g], cq[:, n, h + g:h + g + 1],
                                                            ckB[:, h + g, 0:L], ALU.add, ALU.subtract))
                        sum_done()
                        own.settle()
                        own.mark(V.tensor_tensor(S[:, :, L - P:L], S[:, :, L - P:L],
                                                 mask.unsqueeze(1).to_broadcast([P, count, P]), ALU.add))
                        invert_sum()
                        own.settle()
                        V.tensor_reduce(nmax[:, u:u + count], S, AX.X, ALU.max, negate=True).then_inc(nmax_done, 1)
                else:
                    sum_done()
                    own.settle()
                    invert_sum()
                    own.settle()
                if last_step:
                    for v, first in placed(s - 1):
                        probs = pexp[:, (s - 1) % 2, first:first + width_of(v)]
                        ins = V.tensor_scalar(probs, probs, rsum[:, 1, v:v + 1], None, ALU.mult)
                    ins.then_inc(p_done, 1)
                v = slab_ended(s)
                if v is not None:
                    split_lo(dve, FIRST_MERGE + v + AHEAD)
                w = block_ended(s - 3)
                if w is not None:
                    dve.wait_ge(o_hi_done, w + 1)
                    cols = slice((w % NBLK) * P, (w % NBLK + 1) * P)
                    V.tensor_tensor(oT_lo[:, w // NBLK, :, cols], psO[:, w % 2, :].rearrange("p (t q) -> p t q", t=4),
                                    oT_hi[:, w // NBLK, :, cols].bitcast(F32), ALU.subtract).then_inc(o_lo_done, 1)

            for m in range(KT):
                last = FIRST_MIX + m if m < KT - 1 else FIRST_OUT - 1
                for n in range(FIRST_MIX + m, last + 1):
                    split_lo(dve, n + AHEAD)
                dve.wait_ge(slab_used, last + 1)
                dve.wait_ge(gate_done, 2 * m + 2)
                if m >= 2:
                    dve.wait_ge(m_hi_done, m - 1)
                for j in range(2):
                    own.mark(V.tensor_tensor(mix[:, m % 2, j, :], banks[4 + 2 * (m % 2) + j], gate[:, m % 2, j, :], ALU.mult))
                own.settle()
                V.tensor_tensor(mix[:, m % 2, 0, :], mix[:, m % 2, 0, :], mix[:, m % 2, 1, :], ALU.add).then_inc(mix_done, 1)
                dve.wait_ge(m_hi_done, m + 1)
                V.tensor_tensor(m_lo[:, m, :], mix[:, m % 2, 0, :], m_hi[:, m, :].bitcast(F32),
                                ALU.subtract).then_inc(m_lo_done, 1)
            for m in range(KT):
                split_lo(dve, FIRST_OUT + m + AHEAD)
                own.link(V.tensor_tensor(acc[:, m, :], hT_hi[:, m, 0:SEQ].bitcast(F32), hT_lo[:, m, 0:SEQ].bitcast(F32),
                                         ALU.add))
                dve.wait_ge(slab_used, FIRST_OUT + m + 1)
                V.scalar_tensor_tensor(acc[:, m, :], acc[:, m, :], ALPHA, psS[:, m % 2, 0:SEQ],
                                       ALU.mult, ALU.add).then_inc(r_done, 1)
                dve.wait_ge(r_hi_done, m + 1)
                if m >= 2:
                    dve.wait_ge(mean_mm, m - 1)
                V.tensor_tensor(r_lo[:, m % 2, :], acc[:, m, :], r_hi[:, m % 2, :].bitcast(F32),
                                ALU.subtract).then_inc(r_lo_done, 1)

            dve.wait_ge(mean_mm, KT)
            for k in range(KT + 2):
                if k < KT:
                    V.tensor_tensor(acc[:, k, :], acc[:, k, :], banks[4], ALU.subtract).then_inc(xc_done, 1)
                if k >= 2:
                    dve.wait_ge(sq_hi_done, k - 1)
                    if k >= 4:
                        dve.wait_ge(var_mm, k - 3)
                    V.tensor_tensor(sq_lo[:, k % 2, :], sq[:, k % 2, :], sq_hi[:, k % 2, :].bitcast(F32),
                                    ALU.subtract).then_inc(sq_lo_done, 1)
            dve.wait_ge(sd_done, 1)
            own.link(V.reciprocal(rinv[:, :], nw[:, 0, :]))
            newton(rinv[:, :], banks[5], nw[:, 1, :])
            for k in range(KT + 1):
                if k < KT:
                    V.scalar_tensor_tensor(acc[:, k, :], acc[:, k, :], ncol[:, 2 * KT + k:2 * KT + k + 1], rinv[:, :],
                                           ALU.mult, ALU.mult).then_inc(gained, 1)
                if k >= 1:
                    dve.wait_ge(hT_hi_done, KT + k)
                    V.tensor_tensor(hT_lo[:, k - 1, 0:SEQ], acc[:, k - 1, :], hT_hi[:, k - 1, 0:SEQ].bitcast(F32),
                                    ALU.subtract).then_inc(hT_lo_done, 1)
            dve.wait_ge(sk_hi_done, 1)
            V.tensor_tensor(sk_lo[:, :, :], sk_raw[:, :, :], sk_hi[:, :, :].bitcast(F32), ALU.subtract).then_inc(sk_done, 1)
            for q in range(N_PQ):
                split_lo(dve, FIRST_PQ + q + AHEAD)
                dve.wait_ge(pq_hi_done, q + 1)
                if q >= 2:
                    dve.wait_ge(sc_mm, q - 1)
                V.tensor_tensor(pq_lo[:, q % 2, :], psS[:, q % 2, 0:SEQ], pq_hi[:, q % 2, :].bitcast(F32),
                                ALU.subtract).then_inc(pq_lo_done, 1)

            def top_half(part, r, unit, loads):
                cols = bass.ds(unit * TOPK, TOPK)
                if part == 0:
                    dve.wait_ge(now_in[r], 16 * loads)
                    V.memset(spare[:, :], 0.0)
                    for p in range(2):
                        own.mark(V.max(topv[:, p, 0:8], now[:, r, p, :]))
                    own.settle_apart(V.memset, spare[:, :])
                    for p in range(2):
                        own.mark(V.max_index(topi[:, p, 0:8], topv[:, p, 0:8], now[:, r, p, :]))
                        own.mark(V.match_replace(rest[:, p * NKEYS:(p + 1) * NKEYS], topv[:, p, 0:8], now[:, r, p, :], LOWEST))
                    own.settle_apart(V.memset, spare[:, :])
                    for p in range(2):
                        own.mark(V.max(topv[:, p, 8:16], rest[:, p * NKEYS:(p + 1) * NKEYS]))
                    own.settle_apart(V.memset, spare[:, :])
                    for p in range(2):
                        own.mark(V.max_index(topi[:, p, 8:16], topv[:, p, 8:16], rest[:, p * NKEYS:(p + 1) * NKEYS]))
                    own.link(V.tensor_tensor(cand[:, :].rearrange("p (a b) -> p a b", a=TOPK),
                                             topv[:, 0, :].unsqueeze(2).to_broadcast([P, TOPK, TOPK]),
                                             topv[:, 1, :].unsqueeze(1).to_broadcast([P, TOPK, TOPK]), ALU.add))
                    own.mark(V.tensor_copy(topf[:, :, :], topi[:, :, :]))
                    own.mark(V.max(topv[:, 0, 0:8], cand[:, :]))
                if part == 1:
                    own.settle_apart(V.memset, spare[:, :])
                    own.mark(V.max_index(flat[:, 0:8], topv[:, 0, 0:8], cand[:, :]))
                    own.mark(V.match_replace(rest[:, :], topv[:, 0, 0:8], cand[:, :], LOWEST))
                    own.settle_apart(V.memset, spare[:, :])
                    own.mark(V.max(topv[:, 0, 8:16], rest[:, :]))
                    own.settle_apart(V.memset, spare[:, :])
                    own.mark(V.max_index(flat[:, 8:16], topv[:, 0, 8:16], rest[:, :]))
                    own.link(V.tensor_copy(best[:, cols], topv[:, 0, :]))
                    own.mark(V.tensor_single_scalar(pos[:, 0, :], flat[:, :], 4, ALU.logical_shift_right))
                    own.link(V.tensor_single_scalar(pos[:, 1, :], flat[:, :], TOPK - 1, ALU.bitwise_and))
                    own.link(V.tensor_copy(posf[:, :, :], pos[:, :, :]))
                    whole = [P, 2, TOPK, TOPK]
                    own.link(V.tensor_tensor(eq[:, :, :, :], posf[:, :, :].unsqueeze(3).to_broadcast(whole),
                                             iota16.unsqueeze(1).unsqueeze(1).to_broadcast(whole), ALU.is_equal))
                    own.link(V.tensor_tensor(eq[:, :, :, :], eq[:, :, :, :], topf[:, :, :].unsqueeze(2).to_broadcast(whole),
                                             ALU.mult))
                    V.tensor_reduce(keys[:, :, cols], eq[:, :, :, :], AX.X, ALU.add).then_inc(top_done, 1)

            def hot(q, toks, r):
                wait_at(dve, G_mm, -1, 1, q)

                def spread(v):
                    return v[:, toks].unsqueeze(1).to_broadcast([P, NKEYS, CHUNK])

                own.mark(V.tensor_tensor(hotA[:, r], spread(iaT), iota_h[:, :, :], ALU.is_equal))
                own.link(V.tensor_tensor(hotB[:, :, :], spread(ibT), iota_h[:, :, :], ALU.is_equal))
                own.mark(V.tensor_tensor(hotG_hi[:, r], hotB[:, :, :], spread(gT_hi), ALU.mult))
                V.tensor_tensor(hotG_lo[:, r], hotB[:, :, :], spread(gT_lo), ALU.mult).then_inc(hot_done, 1)
                dve.wait_ge(hot_done, q + 1)

            def split_first_lo(v):
                wh, wl = output_parts(v)
                dve.wait_ge(vhi_done, v + 1)
                V.tensor_tensor(wl, raw[:, (FIRST_V + v) % RING, :], wh.bitcast(F32), ALU.subtract).then_inc(vlo_done, 1)

            def top_group(i, t):
                for j in range(GROUP):
                    split_lo(dve, FIRST_U + j + AHEAD, i, GROUP)
                    k = i - t * BGROUP
                    top_half(j % 2, j // 2, k * 2 + j // 2, k + (t * HEADS // 2 + 1))

            def hot_group(i, t):
                k = i - (t * BGROUP + BGROUP // 2)
                for j in range(GROUP):
                    if isinstance(i, int) and GROUP * i + j + AHEAD >= NKEYS:
                        split_first_lo(GROUP * i + j + AHEAD - NKEYS)
                    else:
                        split_lo(dve, FIRST_U + j + AHEAD, i, GROUP)
                    hot(k * GROUP + (t * (P // CHUNK) + j), bass.ds(k * (GROUP * CHUNK) + j * CHUNK, CHUNK), j % 2)

            for c in range(CHUNK):
                own.mark(V.tensor_copy(iota_h[:, :, c], cst[:, C_IOTA:C_IOTA + P]))
            own.settle()
            for t in range(NBLK):
                start, mid, end = BGROUP * t, BGROUP * t + BGROUP // 2, BGROUP * (t + 1)
                if t == 0:
                    top_group(0, 0)
                    start = 1
                with dve.Fori(start, mid) as i:
                    own.loop(i - start, TOP_MARKS)
                    top_group(i, t)
                    own.end(mid - start)

                dve.wait_ge(top_done, HEADS * (t + 1))
                b3 = best[:, :].rearrange("p (u k) -> p u k", k=TOPK)
                own.link(V.tensor_reduce(gsum[:, 2, :], b3, AX.X, ALU.max))
                V.tensor_tensor(b3, b3, gsum[:, 2, :].unsqueeze(2).to_broadcast([P, HEADS, TOPK]),
                                ALU.subtract).then_inc(less_done, 1)
                dve.wait_ge(g_exp_done, t + 1)
                own.link(V.tensor_reduce(gsum[:, 0, :], b3, AX.X, ALU.add))
                own.link(V.reciprocal(gsum[:, 1, :], gsum[:, 0, :]))
                V.tensor_tensor(b3, b3, gsum[:, 1, :].unsqueeze(2).to_broadcast([P, HEADS, TOPK]),
                                ALU.mult).then_inc(g_done, 1)
                dve.wait_ge(idx_turned, t + 1)
                own.mark(V.tensor_copy(iaT[:, :], banks[4][:, 0:P]))
                own.mark(V.tensor_copy(ibT[:, :], banks[4][:, P:2 * P]))
                dve.wait_ge(gT_hi_done, t + 1)
                own.link(V.scalar_tensor_tensor(gT_lo[:, :], banks[5][:, 0:P], GATE_SCALE, gT_hi[:, :],
                                                ALU.mult, ALU.subtract))
                if t == NBLK - 1:
                    end -= 1
                if t == 0:
                    hot_group(mid, 0)
                    mid += 1
                with dve.Fori(mid, end) as i:
                    own.loop(i - mid, HOT_MARKS)
                    hot_group(i, t)
                    own.end(end - mid)
            hot_group(NGROUP - 1, NBLK - 1)

            def weigh(j, g, par, part):
                slot = par * GROUP + j
                wh, wl = output_parts(slot)
                if part == 0:
                    dve.wait_ge(gel_in_s[j], 16 + g * 16)
                    dve.wait_ge(gate_in_s[j], 16 + g * 16)
                    wait_at(dve, ahi_done, j - RING + 1, RING, g)
                    wait_at(dve, alo_done, j - RING + 1, RING, g)
                    cut = SEQ
                    if isinstance(g, int) and g < 2:
                        cut = (NBLK - 1) * P
                        own.mark(V.tensor_tensor(act_t[:, j, cut:], gel_in[:, j, cut:], gates[:, g * GROUP + j, :], ALU.mult))
                        own.settle()
                    tile = gate_first if isinstance(g, int) and g == 0 else gate_in
                    V.tensor_tensor(act_t[:, j, 0:cut], gel_in[:, j, 0:cut], tile[:, j, 0:cut], ALU.mult).then_inc(act_done, 1)
                    if not (isinstance(g, int) and g == 0 and j < AHEAD):
                        dve.wait_ge(vhi_done, g * GROUP + (j + 1))
                        V.tensor_tensor(wl, raw[:, (FIRST_V + j) % RING, :], wh.bitcast(F32), ALU.subtract).then_inc(vlo_done, 1)
                else:
                    dve.wait_ge(ahi_done, g * GROUP + (j + 1))
                    V.tensor_tensor(hT_lo[:, slot, 0:SEQ], act_t[:, j, :], hT_hi[:, slot, 0:SEQ].bitcast(F32),
                                    ALU.subtract).then_inc(alo_done, 1)

            def group(g, par, last=False):
                for m in range(KT):
                    first = isinstance(g, int) and g == 0
                    parts = [m] if not first else [] if m < KT // 2 else [2 * m - KT, 2 * m - KT + 1]
                    for part in parts if not last else []:
                        weigh(part // 2, g + 1, 1 - par, part % 2)
                    dve.wait_ge(v_mm, g * KT + (m + 1))
                    V.tensor_tensor(acc[:, m, :], acc[:, m, :], banks[4 + m % 4], ALU.add).then_inc(y_added, 1)

            dve.wait_ge(G_act, BATCHES)
            dve.wait_ge(scaled, KT)
            for j in range(GROUP):
                weigh(j, 0, 0, 0)
            for j in range(GROUP):
                weigh(j, 0, 0, 1)
            for g in range(2):
                group(g, g)
            with dve.Fori(1, NGROUP // 2 - 1) as i:
                for par in range(2):
                    group(i * 2 + par, par)
            group(NGROUP - 2, 0)
            group(NGROUP - 1, 1, last=True)
            for t in range(NBLK):
                dve.wait_ge(out_turned, t + 1)
                for c in range(2):
                    own.mark(V.bn_stats(stats2[:, t, 6 * c:6 * c + 6], wide[t][:, c * 512:(c + 1) * 512]))
                own.settle()
                own.mark(V.bn_aggr(mv2[:, t, :], stats2[:, t, :]))
            own.settle()
            V.tensor_copy(rs2[:, 1, :], mv2[:, :, 1]).then_inc(rs2_done, 1)
            dve.wait_ge(rs2_done, 1)
            dve.wait_ge(std2_done, 1)
            own.link(V.reciprocal(rs2[:, 3, :], rs2[:, 0, :]))
            newton(rs2[:, 3, :], rs2[:, 1, :], rs2[:, 2, :])
            V.scalar_tensor_tensor(rs2[:, 4, :], mv2[:, :, 0], -1.0, rs2[:, 3, :], ALU.mult, ALU.mult).then_inc(rs2_done, 1)
            dve.wait_ge(rows_in, 16)
            for t in range(NBLK):
                dve.wait_ge(unit_done, t + 1)
                own.link(V.tensor_tensor(tok[:, t, :], tok[:, t, :], gain_shift[:, 0, :], ALU.mult))
                V.tensor_tensor(tok[:, t, :], tok[:, t, :], gain_shift[:, 1, :], ALU.add).then_inc(tok_done, 1)

        @block.tensor
        def _(pe):
            mm, turn = nc.tensor.matmul, nc.tensor.transpose

            def slab(n, slot, out_ap, x_h, x_l, ks, ends=(True, True)):
                for a, (k, kx) in enumerate(ks):
                    wh, wl = slab_parts(slot, k)
                    last = split_product(out_ap, wh, wl, x_h(kx), x_l(kx), ends[0] and a == 0,
                                         ends[1] and a == len(ks) - 1)
                return last

            def tokens(k):
                return hT_hi[:, k, 0:SEQ]

            def tokens_lo(k):
                return hT_lo[:, k, 0:SEQ]

            all_k = [(k, k) for k in range(KT)]
            pe.wait_ge(cst_in, 48)
            pe.wait_ge(norm_done, NBLK + 2)
            for k in range(KT):
                if k >= 2:
                    pe.wait_ge(xT_done, k - 1)
                for t in range(NBLK):
                    turn(psS[:, k % 2, t * P:(t + 1) * P], xin[:, t, k * P:(k + 1) * P], ident)
                turn(psS[:, k % 2, SEQ:COLS], xin[0:META, NBLK, k * P:(k + 1) * P],
                     ident[0:META, 0:META]).then_inc(turned, 1)
            pe.wait_ge(bias_in, 64)
            mm(psO[0:HEADS, 0, 0:3 * P], relb[:, :], buck[:, :], start=True, stop=True).then_inc(w_mm, 1)
            pe.wait_ge(xT_done, KT)
            for n in range(N_PROJ):
                pe.wait_ge(lo_done, n + 1)
                if n >= 2:
                    pe.wait_ge(evacuated, n - 1)
                if 1 <= n <= 4 or 7 <= n <= 10:
                    last = slab(n, n % RING, psS[:, n % 2, 0:SEQ], tokens, tokens_lo, all_k)
                else:
                    for b in range(2):
                        half = slice(b * HALF, (b + 1) * HALF)
                        if n == 0 and b == 0:
                            for k in range(KT):
                                pe.wait_ge(hT_lo_done, k + 1)
                                slab(n, 0, psS[:, 0, 0:HALF], lambda k: hT_hi[:, k, half], lambda k: hT_lo[:, k, half],
                                     [(k, k)], ends=(k == 0, k == KT - 1))
                            continue
                        last = slab(n, n % RING, psS[:, n % 2, b * SEQ:b * SEQ + HALF], lambda k: hT_hi[:, k, half],
                                    lambda k: hT_lo[:, k, half], all_k)
                last.then_inc(slab_used, 1)
                if n == 6:
                    pe.wait_ge(c_done, 1)
                    for b in range(NBLK):
                        last = turn(psO[:, 1, b * HEADS:(b + 1) * HEADS], logf[:, 5, b * P:(b + 1) * P],
                                    ident[0:HEADS, 0:HEADS])
                    last.then_inc(c_turned, 1)
            pe.wait_ge(evacuated, N_PROJ)
            for b in range(NBLK + 1):
                if 2 <= b < NBLK:
                    pe.wait_ge(v_ready, b - 1)
                for f in range(5):
                    if b < NBLK:
                        last = turn(psS[:, b % 2, f * P:(f + 1) * P], vT[:, f, b * P:(b + 1) * P], ident)
                    else:
                        last = turn(psT[0:META, f * P:(f + 1) * P], vT[:, f, SEQ:COLS], ident)
                last.then_inc(v_turned, 1)
            pe.wait_ge(v_ready, NBLK + 1)

            def key_runs(u):
                runs = []
                for c, width, b in pieces_of(u):
                    k = 0 if b is None else META + b * P
                    if runs and runs[-1][2] == k:
                        runs[-1] = (*runs[-1][:2], k + width)
                    else:
                        runs.append((c, k, k + width))
                c, k0, k1 = runs[-1]
                if c + k1 - k0 > SEQ:
                    runs[-1:] = [(c, k0, k0 + SEQ - c), (SEQ, k0 + SEQ - c, k1)]
                return runs

            for s in range(-1, N_STEPS + 2):
                r = s + 1
                if r < N_STEPS:
                    if r >= 2:
                        pe.wait_ge(exp_done, exp_count(r - 2))
                    for u, first in placed(r):
                        window, n, h, tile, half = unit_of(u)
                        rows = slice(HD * half, HD * half + HD)
                        if width_of(u) > SEQ:
                            pe.wait_ge(gate_in_done, N_GATE - 1 + r % 2)
                        q = (qaT if window else qbT)[rows, tile, n * P:(n + 1) * P]
                        for c, k0, k1 in key_runs(u):
                            k = kaT[rows, k0:k1] if window else kbT[rows, tile, k0:k1]
                            last = mm(psS[:, r % 2, first + c:first + c + k1 - k0], q, k, start=True, stop=True)
                    last.then_inc(s_mm, 1)
                for done in range(tiles_before(max(s, 0)), tiles_before(s + 1)):
                    v, k = done // KT, done % KT
                    if k == 0:
                        pe.wait_ge(lo_done, FIRST_MERGE + v + 1)
                        if v >= 2:
                            pe.wait_ge(gate_in_done, v - 1)
                    last = slab(FIRST_MERGE + v, (FIRST_MERGE + v) % RING, psS[:, v % 2, SEQ:], tokens, tokens_lo,
                                [(k, k)], ends=(k == 0, k == KT - 1))
                    if k == KT - 1:
                        last.then_inc(slab_used, 1)
                if 1 <= s <= N_STEPS:
                    pe.wait_ge(p_done, s)
                    if s >= 2:
                        pe.wait_ge(pT_done, s - 1)
                        pe.wait_ge(pM_done, max(1, meta_count(s - 2)))
                    at = at_meta = 0
                    for _, c, width, b in pieces_at(s - 1):
                        src = pexp[:, (s - 1) % 2, c:c + width]
                        if b is None:
                            last = turn(psT[0:META, SEQ + at_meta:SEQ + at_meta + P], src, ident)
                            at_meta += P
                        else:
                            last = turn(psT[:, at:at + P], src, ident)
                            at += P
                    last.then_inc(p_turned, 1)
                if s >= 2:
                    pe.wait_ge(pT_done, s - 1)
                    pe.wait_ge(pM_done, max(1, meta_count(s - 2)))
                    at = at_meta = 0
                    for u in STEPS[s - 2]:
                        window, n, h, tile, half = unit_of(u)
                        w = u // HEADS
                        if w >= 2 and h == 0:
                            pe.wait_ge(o_hi_done, w - 1)
                            pe.wait_ge(o_lo_done, w - 1)
                        f = half * HD if window else P + h * HD
                        dst = psO[HD * half:HD * half + HD, w % 2, tile * P:(tile + 1) * P]
                        pieces = pieces_of(u)
                        for a, (_, _, b) in enumerate(pieces):
                            ends = dict(start=a == 0, stop=a == len(pieces) - 1)
                            if b is None:
                                last = mm(dst, vM[:, f:f + HD], pM[:, s % 2, at_meta, :], **ends)
                                at_meta += 1
                            else:
                                last = mm(dst, vN[:, b, f:f + HD], pT[:, s % 2, at:at + P], **ends)
                                at += P
                    last.then_inc(pv_mm, 1)

            pe.wait_ge(o_lo_done, 2 * NBLK)
            for m in range(KT):
                for j in (range(3) if m == KT - 1 else (2,)):
                    n = FIRST_MIX + m + (j if m == KT - 1 else 0)
                    pe.wait_ge(lo_done, n + 1)
                    if j < 2:
                        last = slab(n, n % RING, psS[:, m % 2, j * SEQ:(j + 1) * SEQ], tokens, tokens_lo, all_k)
                    else:
                        if m >= 2:
                            pe.wait_ge(mix_done, m - 1)
                        for e in range(2):
                            last = slab(n, n % RING, banks[4 + 2 * (m % 2) + e], lambda k: oT_hi[:, e, k, :],
                                        lambda k: oT_lo[:, e, k, :], [(4 * e + k, k) for k in range(4)])
                    last.then_inc(slab_used, 1)


            pe.wait_ge(mean_set, 1)

            def feature_mean(k):
                pe.wait_ge(r_lo_done, k + 1)
                mm(banks[4], mean_of[:, :], r_lo[:, k % 2, :], start=k == 0, stop=False)
                mm(banks[4], mean_of[:, :], r_hi[:, k % 2, :], start=False, stop=k == KT - 1).then_inc(mean_mm, 1)

            pe.wait_ge(gate_done, 2 * KT)
            for m in range(N_OUT):
                n = FIRST_OUT + m
                pe.wait_ge(lo_done, n + 1)
                pe.wait_ge(m_lo_done, KT)
                if m >= 2:
                    pe.wait_ge(r_done, m - 1)
                slab(n, n % RING, psS[:, m % 2, 0:SEQ], lambda k: m_hi[:, k, :], lambda k: m_lo[:, k, :],
                     all_k).then_inc(slab_used, 1)
                if m >= 1:
                    feature_mean(m - 1)

            feature_mean(KT - 1)
            for k in range(KT):
                pe.wait_ge(sq_lo_done, k + 1)
                mm(banks[5], mean_of[:, :], sq_lo[:, k % 2, :], start=k == 0, stop=False)
                mm(banks[5], mean_of[:, :], sq_hi[:, k % 2, :], start=False, stop=k == KT - 1).then_inc(var_mm, 1)
            for q in range(N_PQ + 1):
                if q < N_PQ:
                    n = FIRST_PQ + q
                    pe.wait_ge(lo_done, n + 1)
                    if q >= 2:
                        pe.wait_ge(pq_lo_done, q - 1)
                    if q == 0:
                        for k in range(KT):
                            pe.wait_ge(hT_lo_done, KT + k + 1)
                            last = slab(n, n % RING, psS[:, 0, 0:SEQ], tokens, tokens_lo, [(k, k)], ends=(k == 0, k == KT - 1))
                        last.then_inc(slab_used, 1)
                    else:
                        slab(n, n % RING, psS[:, q % 2, 0:SEQ], tokens, tokens_lo, all_k).then_inc(slab_used, 1)
                if q >= 1:
                    c = q - 1
                    pe.wait_ge(sk_done, 1)
                    pe.wait_ge(pq_lo_done, c + 1)
                    if c >= 4:
                        pe.wait_ge(sc_done, c - 3)
                    for t in range(NBLK):
                        toks = slice(t * P, (t + 1) * P)
                        last = split_product(banks[4 + c % 4][:, toks], pq_hi[:, c % 2, toks], pq_lo[:, c % 2, toks],
                                             sk_hi[:, c, :], sk_lo[:, c, :], True, True)
                    last.then_inc(sc_mm, 1)

            def expert_slab(n, i):
                pe.wait_ge(lo_done, FIRST_U + n + 1 + i * GROUP)
                wait_at(pe, gelu_done, n - GROUP + 1, GROUP, i)
                slab(FIRST_U + n, (FIRST_U + n) % RING, banks[n % GROUP], tokens, tokens_lo, all_k).then_inc(slab_used, 1)

            def gate_matrices(q, r):
                pe.wait_ge(hot_done, q + 1)
                wait_at(pe, G_act, -1, 1, q)
                for c in range(CHUNK):
                    dst = banks[4 + 2 * r + c // 4][:, (c % 4) * P:(c % 4 + 1) * P]
                    mm(dst, hotA[:, r, :, c], hotG_hi[:, r, :, c], start=True, stop=False)
                    last = mm(dst, hotA[:, r, :, c], hotG_lo[:, r, :, c], start=False, stop=True)
                last.then_inc(G_mm, 1)

            def expert_group(i, t=None):
                for j in range(GROUP):
                    if not (isinstance(i, int) and GROUP * i + j + 1 >= NKEYS):
                        expert_slab(j + 1, i)
                    if t is not None:
                        k = i - (t * BGROUP + BGROUP // 2)
                        gate_matrices(k * GROUP + (t * (P // CHUNK) + j), j % 2)

            pe.wait_ge(pq_lo_done, N_PQ)
            pe.wait_ge(sc_done, N_PQ)
            expert_slab(0, 0)
            for t in range(NBLK):
                start, mid, end = BGROUP * t, BGROUP * t + BGROUP // 2, BGROUP * (t + 1)
                if t == 0:
                    expert_group(0)
                    start = 1
                with pe.Fori(start, mid) as i:
                    expert_group(i)
                pe.wait_ge(g_done, t + 1)
                if t > 0:
                    pe.wait_ge(G_act, t * (P // CHUNK))
                turn(banks[4][:, 0:P], keys[:, 0, :], ident)
                turn(banks[4][:, P:2 * P], keys[:, 1, :], ident)
                last = turn(banks[5][:, 0:P], best[:, :], ident)
                last.then_inc(idx_turned, 1)
                if t == 0:
                    expert_group(mid, 0)
                    mid += 1
                if t == NBLK - 1:
                    end -= 1
                with pe.Fori(mid, end) as i:
                    expert_group(i, t)
            expert_group(NGROUP - 1, NBLK - 1)

            def group(g, par):
                pe.wait_ge(vlo_done, (g + 1) * GROUP)
                pe.wait_ge(alo_done, (g + 1) * GROUP)
                for m in range(KT):
                    wait_at(pe, y_added, m - 3, KT, g)
                    for j in range(GROUP):
                        slot = par * GROUP + j
                        wh, wl = output_parts(slot)
                        cols = slice(m * P, (m + 1) * P)
                        last = split_product(banks[4 + m % 4], wh[:, cols], wl[:, cols],
                                             hT_hi[:, slot, 0:SEQ], hT_lo[:, slot, 0:SEQ], j == 0, j == GROUP - 1)
                    last.then_inc(v_mm, 1)

            pe.wait_ge(G_act, BATCHES)
            for g in range(2):
                group(g, g)
            with pe.Fori(1, NGROUP // 2) as i:
                for par in range(2):
                    group(i * 2 + par, par)
            pe.wait_ge(y_added, NGROUP * KT)
            for t in range(NBLK):
                for k in range(KT):
                    last = turn(wide[t][:, k * P:(k + 1) * P], acc[:, k, t * P:(t + 1) * P], ident)
                last.then_inc(out_turned, 1)


def constants():
    c = np.zeros((P, C_COLS), np.float32)
    c[:, C_ID:C_ID + P] = np.eye(P)
    c[:, C_MASK:C_MASK + P] = np.where(np.arange(P)[None, :] > np.arange(P)[:, None], NEG, 0.0)
    c[:, C_IOTA:C_IOTA + P] = np.arange(P)
    c[:, C_IOTA16:C_IOTA16 + TOPK] = np.arange(TOPK)
    c[:, C_EPS] = EPS
    c[:, C_ONE] = 1.0
    dist = 2 * P - 1 - np.arange(3 * P)
    inside = (dist >= 0) & (dist < P)
    d = np.clip(dist, 1, P - 1).astype(np.float32)
    exact = BUCKETS // 2
    large = exact + (np.log(d / exact) / np.log(P / exact) * (BUCKETS - exact)).astype(np.int32)
    bucket = np.where(dist < exact, np.clip(dist, 0, P), np.minimum(large, BUCKETS - 1))
    hot = ((np.arange(BUCKETS)[:, None] == bucket[None, :]) & inside[None, :]).astype(np.float32)
    outside = np.repeat(np.where(inside, 0.0, NEG)[None, :], HEADS, axis=0).astype(np.float32)
    return c, hot, outside


def tiles(w):
    k, f = w.shape
    return w.reshape(k // P, P, f // P, P).transpose(2, 1, 0, 3)


def kernel(x, meta_tokens, emb_ln_g, emb_ln_b, rel_bias, w_in, b_in, attn_sinks, w_pa, w_pb, w_o,
           ln1_g, ln1_b, peer_wq, peer_subkeys, peer_u, peer_v, ln2_g, ln2_b):
    import concourse.bacc as bacc
    from concourse.bass_utils import run_bass_kernel_spmd

    a = {k: np.asarray(v) for k, v in dict(
        x=x, meta=meta_tokens, eg=emb_ln_g, eb=emb_ln_b, rel=rel_bias, w_in=w_in, b_in=b_in, sinks=attn_sinks, w_pa=w_pa,
        w_pb=w_pb, w_o=w_o, g1=ln1_g, b1=ln1_b, wq=peer_wq, sk=peer_subkeys, u=peer_u, v=peer_v, g2=ln2_g,
        b2=ln2_b).items()}
    order = [h + 4 * s for h in range(4) for s in range(2)]
    qa, ka, va, qb, kb, vb = 0, 512, 640, 768, 1280, 1792
    fb = vb + 512
    ga = fb + HEADS
    gb = ga + D
    win = a["w_in"][0]
    pick = np.concatenate([np.arange(fb, fb + P)] + [np.arange(qa + h * HD, qa + (h + 1) * HD) for h in order] +
                          [np.arange(ka, ka + 2 * P), np.arange(qb, fb)])
    w_proj = tiles(win[:, pick])
    both = np.stack([tiles(win[:, ga:ga + D]), tiles(win[:, gb:gb + D]),
                     np.concatenate([tiles(a["w_pa"][0].reshape(HEADS, HD, D)[order].reshape(512, D)),
                                     tiles(a["w_pb"][0])], axis=2)], axis=1)
    w_merge = np.concatenate([both[:-1, :2].reshape(N_GATE, P, D), both[:-1, 2].reshape(KT - 1, P, D),
                              both[-1].reshape(3, P, D)])
    bias = a["b_in"][0]
    b_cols = np.concatenate([bias[pick], bias[ga:ga + 2 * D]]).reshape(-1, P).T
    norm_cols = np.stack([a[n].reshape(KT, P) for n in ("eg", "eb", "g1", "b1")]).reshape(-1, P).T
    cst, hot, outside = constants()
    ins = {
        "x": a["x"][0], "meta": a["meta"], "consts": cst, "buckets": hot, "outside": outside, "norm_cols": norm_cols,
        "b_cols": b_cols, "rel_bias": a["rel"], "sinks": a["sinks"][0],
        "w_proj": w_proj.reshape(N_PROJ, P, D), "w_merge": w_merge,
        "w_out": tiles(a["w_o"][0]).reshape(N_OUT, P, D), "w_pq": tiles(a["wq"][0]).reshape(N_PQ, P, D),
        "subkeys": a["sk"][0].reshape(2 * HEADS, NKEYS, P).transpose(2, 0, 1),
        "u_exp": a["u"][0].reshape(NKEYS, NKEYS, KT, P).transpose(1, 3, 2, 0).reshape(NKEYS, P, D),
        "v_exp": a["v"][0].reshape(NKEYS, NKEYS, D).transpose(1, 0, 2),
        "norm_rows": np.stack([a["g2"][0], a["b2"][0]]),
    }
    nc = bacc.Bacc("TRN2", target_bir_lowering=False, num_devices=1)
    arrays, args = {}, []
    for name, v in ins.items():
        v = np.ascontiguousarray(v)
        arrays[f"in_{name}"] = v
        args.append(nc.dram_tensor(f"in_{name}", v.shape, mybir.dt.from_np(v.dtype), kind="ExternalInput").ap())
    out = nc.dram_tensor("out_0", (SEQ, D), F32, kind="ExternalOutput").ap()
    build(nc, *args, out)
    r = run_bass_kernel_spmd(nc, [arrays], core_ids=[0])
    return r.results[0]["out_0"].reshape(1, SEQ, D)
```
